# Optimizing a Trainium2 kernel written in Bass

```python
import jax, jax.numpy as jnp
from jax import lax
import numpy as np

D_MODEL = 2048
BATCH = 1
SEQ = 512
DEPTH = 1
DEC_BATCH = 8
DEC_SEQ = 8
PAST_LEN = 2048
PAGE_SIZE = 128

H_A = 6
HD_A = 128
D_A = H_A * HD_A
DILATED_PATTERNS = ((128, 1), (512, 4), (2048, 16))
WIN_MAX = 2048
POOL_WINDOWS = (2, 4, 8, 16)
N_POOL = 4
D_B = 512
POOL_GROUP = D_B // N_POOL
POOL_BUF = 15
H_C = 4
DK_C = 96
DV_C = 192
D_C = H_C * DV_C
GATE_RANK = 16
GATE_NORMALIZER = 16.0
GLA_CHUNK = 32
PROJ_SPLITS = (D_A, D_A, D_A, D_B, H_C * DK_C, H_C * DK_C, D_C, D_C, GATE_RANK)
D_IN = 3 * D_A + D_B + 2 * H_C * DK_C + 2 * D_C + GATE_RANK
D_MIX = D_A + D_B + D_C
D_FF = -(-8 * D_MODEL // (3 * 256)) * 256
EPS = 1e-6
NEG_INF = -1e30

kernel_name = 'hybrid_dilated_pool_gla_step'

def rmsnorm(x, g):
    xf = x.astype(jnp.float32)
    y = xf * lax.rsqrt(jnp.mean(xf * xf, axis=-1, keepdims=True) + EPS)
    return (y * g.astype(jnp.float32)).astype(x.dtype)

def dilated_band(q, k, v, window, dil):
    B, S, H, Dh = q.shape
    blk = window // dil
    span = dil * blk
    S_pad = -(-S // span) * span
    L = S_pad // dil
    nb = L // blk

    def to_blocks(t):
        t = jnp.pad(t.astype(jnp.float32), ((0, 0), (0, S_pad - S), (0, 0), (0, 0)))
        t = jnp.moveaxis(t.reshape(B, L, dil, H, Dh), 2, 1)
        return t.reshape(B, dil, nb, blk, H, Dh)

    def with_prev(t):
        prev = jnp.pad(t[:, :, :-1], ((0, 0), (0, 0), (1, 0), (0, 0), (0, 0), (0, 0)))
        return jnp.concatenate([prev, t], axis=3)

    qb, kb, vb = to_blocks(q), to_blocks(k), to_blocks(v)
    kk, vv = with_prev(kb), with_prev(vb)
    s = jnp.einsum('brnqhd,brnkhd->brnhqk', qb, kk) * (Dh ** -0.5)
    qi = jnp.arange(blk)[:, None]
    ki = jnp.arange(2 * blk)[None, :]
    dist = qi + blk - ki
    band = (dist >= 0) & (dist <= blk)
    exists = (jnp.arange(nb)[:, None, None] > 0) | (ki[None] >= blk)
    mask = band[None] & exists
    s = jnp.where(mask[None, None, :, None], s, NEG_INF)
    m = jnp.max(s, axis=-1, keepdims=True)
    p = jnp.exp(s - m)
    den = jnp.sum(p, axis=-1, keepdims=True)
    o = jnp.einsum('brnhqk,brnkhd->brnqhd', p, vv) / jnp.transpose(den, (0, 1, 2, 4, 3, 5))
    lse = jnp.transpose((m + jnp.log(den))[..., 0], (0, 1, 2, 4, 3))

    def from_blocks(t):
        t = t.reshape((B, dil, L) + t.shape[4:])
        t = jnp.moveaxis(t, 1, 2).reshape((B, S_pad) + t.shape[3:])
        return t[:, :S]

    return from_blocks(o), from_blocks(lse)

def dilated_gather(q, k_ext, v_ext, window, dil, P):
    T = q.shape[1]
    Dh = q.shape[-1]
    n = window // dil
    idx = P + jnp.arange(T)[:, None] - dil * jnp.arange(n + 1)[None, :]
    valid = idx >= 0
    idxc = jnp.maximum(idx, 0)
    kg = k_ext[:, idxc].astype(jnp.float32)
    vg = v_ext[:, idxc].astype(jnp.float32)
    s = jnp.einsum('bthd,btjhd->bthj', q.astype(jnp.float32), kg) * (Dh ** -0.5)
    s = jnp.where(valid[None, :, None, :], s, NEG_INF)
    m = jnp.max(s, axis=-1, keepdims=True)
    p = jnp.exp(s - m)
    den = jnp.sum(p, axis=-1, keepdims=True)
    o = jnp.einsum('bthj,btjhd->bthd', p, vg) / den
    return o, (m + jnp.log(den))[..., 0]

def pool_mix(u_ext, pos0, w_pool, scale):
    B, Lx, C = u_ext.shape
    T = Lx - POOL_BUF
    uf = u_ext.astype(jnp.float32)
    csum = jnp.concatenate([jnp.zeros((B, 1, C), jnp.float32), jnp.cumsum(uf, axis=1)], axis=1)
    end = csum[:, POOL_BUF + 1:]
    pos = pos0 + jnp.arange(T)
    means = []
    for gi, w in enumerate(POOL_WINDOWS):
        lo, hi = gi * POOL_GROUP, (gi + 1) * POOL_GROUP
        start = csum[:, POOL_BUF + 1 - w: POOL_BUF + 1 - w + T, lo:hi]
        cnt = jnp.minimum(w, pos + 1).astype(jnp.float32)[None, :, None]
        means.append((end[..., lo:hi] - start) / cnt)
    pooled = (jnp.concatenate(means, axis=-1) - uf[:, POOL_BUF:]).reshape(B, T, N_POOL, POOL_GROUP)
    out = jnp.einsum('btgc,gcd->btgd', pooled, w_pool.astype(jnp.float32)).reshape(B, T, D_B)
    return (out * scale.astype(jnp.float32)).astype(u_ext.dtype)

def gla_chunked(q, k, v, g, S0):
    B, T, H, DK = q.shape
    DV = v.shape[-1]
    c = min(GLA_CHUNK, T)
    Tp = -(-T // c) * c
    n = Tp // c

    def prep(t):
        t = jnp.pad(t.astype(jnp.float32), ((0, 0), (0, Tp - T), (0, 0), (0, 0)))
        return jnp.transpose(t.reshape(B, n, c, H, t.shape[-1]), (1, 0, 3, 2, 4))

    tril = jnp.tril(jnp.ones((c, c), dtype=bool))

    def step(S, inp):
        qc, kc, vc, gc = inp
        b = jnp.cumsum(gc, axis=2)
        qe = qc * jnp.exp(b)
        ke = kc * jnp.exp(-b)
        A = jnp.where(tril, jnp.einsum('bhid,bhjd->bhij', qe, ke), 0.0)
        o = jnp.einsum('bhij,bhjv->bhiv', A, vc) + jnp.einsum('bhid,bhdv->bhiv', qe, S)
        bl = b[:, :, -1:, :]
        S = jnp.exp(bl)[:, :, 0, :, None] * S + jnp.einsum('bhjd,bhjv->bhdv', kc * jnp.exp(bl - b), vc)
        return S, o

    S, o = lax.scan(step, S0.astype(jnp.float32), (prep(q), prep(k), prep(v), prep(g)))
    o = jnp.transpose(o, (1, 0, 3, 2, 4)).reshape(B, Tp, H, DV)[:, :T]
    return o, S

def layer(x, kv_buf, pool_buf, gla_s0, pos0, norm1_g, w_in, w_gate2, b_gate, w_pool, pool_scale,
          gla_norm_g, w_o, norm2_g, w_ffn_gate, w_ffn_up, w_ffn_down):
    B, T, _ = x.shape
    h = rmsnorm(x, norm1_g)
    proj = jnp.einsum('btd,de->bte', h, w_in)
    points = [int(p) for p in np.cumsum(PROJ_SPLITS)[:-1]]
    qa, ka, va, ub, qc, kc, vc, rc, ga = jnp.split(proj, points, axis=-1)
    qa = qa.reshape(B, T, H_A, HD_A)
    ka = ka.reshape(B, T, H_A, HD_A)
    va = va.reshape(B, T, H_A, HD_A)
    if kv_buf is None:
        outs = [dilated_band(qa, ka, va, w, d) for (w, d) in DILATED_PATTERNS]
    else:
        k_buf, v_buf = kv_buf
        P = k_buf.shape[1]
        k_ext = jnp.concatenate([k_buf.astype(ka.dtype), ka], axis=1)
        v_ext = jnp.concatenate([v_buf.astype(va.dtype), va], axis=1)
        outs = [dilated_gather(qa, k_ext, v_ext, w, d, P) for (w, d) in DILATED_PATTERNS]
    o_stack = jnp.stack([o for o, _ in outs])
    lse_stack = jnp.stack([l for _, l in outs])
    wts = jax.nn.softmax(lse_stack, axis=0)
    out_a = jnp.sum(wts[..., None] * o_stack, axis=0).reshape(B, T, D_A).astype(x.dtype)
    if pool_buf is None:
        pool_buf = jnp.zeros((B, POOL_BUF, D_B), ub.dtype)
    u_ext = jnp.concatenate([pool_buf.astype(ub.dtype), ub], axis=1)
    out_b = pool_mix(u_ext, pos0, w_pool, pool_scale).astype(x.dtype)
    new_pool = u_ext[:, -POOL_BUF:]
    qc = qc.reshape(B, T, H_C, DK_C) * (DK_C ** -0.5)
    kc = kc.reshape(B, T, H_C, DK_C)
    vc = vc.reshape(B, T, H_C, DV_C)
    g = jax.nn.log_sigmoid(jnp.einsum('btr,re->bte', ga, w_gate2).astype(jnp.float32)
                           + b_gate.astype(jnp.float32)) / GATE_NORMALIZER
    g = g.reshape(B, T, H_C, DK_C)
    oc, S_new = gla_chunked(qc, kc, vc, g, gla_s0)
    oc = oc * lax.rsqrt(jnp.mean(oc * oc, axis=-1, keepdims=True) + EPS) * gla_norm_g.astype(jnp.float32)
    out_c = (oc.reshape(B, T, D_C) * jax.nn.silu(rc.astype(jnp.float32))).astype(x.dtype)
    mix = jnp.concatenate([out_a, out_b, out_c], axis=-1)
    x = x + jnp.einsum('btm,md->btd', mix, w_o)
    h2 = rmsnorm(x, norm2_g)
    f = jax.nn.silu(jnp.einsum('btd,df->btf', h2, w_ffn_gate)) * jnp.einsum('btd,df->btf', h2, w_ffn_up)
    x = x + jnp.einsum('btf,fd->btd', f, w_ffn_down)
    return x, ka, va, new_pool, S_new.astype(x.dtype)

def setup_inputs(seed: int = 0) -> dict:
    key = jax.random.key(seed)
    ks = jax.random.split(key, 20)
    f32 = jnp.float32

    def nrm(k, shape, scale):
        return jax.random.normal(k, shape, f32) * scale

    w_buf = min(WIN_MAX, PAST_LEN)
    return {
        'x_prompt': nrm(ks[0], (BATCH, SEQ, D_MODEL), 1.0),
        'x_sample': nrm(ks[1], (DEC_BATCH, DEC_SEQ, D_MODEL), 1.0),
        'cache_win_k': nrm(ks[2], (DEPTH, DEC_BATCH, w_buf, H_A, HD_A), 1.0),
        'cache_win_v': nrm(ks[3], (DEPTH, DEC_BATCH, w_buf, H_A, HD_A), 1.0),
        'state_pool': nrm(ks[4], (DEPTH, DEC_BATCH, POOL_BUF, D_B), 1.0),
        'state_gla': nrm(ks[5], (DEPTH, DEC_BATCH, H_C, DK_C, DV_C), 0.3),
        'norm1_g': 1.0 + nrm(ks[6], (DEPTH, D_MODEL), 0.02),
        'w_in': nrm(ks[7], (DEPTH, D_MODEL, D_IN), D_MODEL ** -0.5),
        'w_gate2': nrm(ks[8], (DEPTH, GATE_RANK, H_C * DK_C), GATE_RANK ** -0.5),
        'b_gate': nrm(ks[9], (DEPTH, H_C * DK_C), 0.1),
        'w_pool': nrm(ks[10], (DEPTH, N_POOL, POOL_GROUP, POOL_GROUP), POOL_GROUP ** -0.5),
        'pool_scale': 1.0 + nrm(ks[11], (DEPTH, D_B), 0.02),
        'gla_norm_g': 1.0 + nrm(ks[12], (DEPTH, DV_C), 0.02),
        'w_o': nrm(ks[13], (DEPTH, D_MIX, D_MODEL), D_MIX ** -0.5),
        'norm2_g': 1.0 + nrm(ks[14], (DEPTH, D_MODEL), 0.02),
        'w_ffn_gate': nrm(ks[15], (DEPTH, D_MODEL, D_FF), D_MODEL ** -0.5),
        'w_ffn_up': nrm(ks[16], (DEPTH, D_MODEL, D_FF), D_MODEL ** -0.5),
        'w_ffn_down': nrm(ks[17], (DEPTH, D_FF, D_MODEL), D_FF ** -0.5),
        'final_norm_g': 1.0 + nrm(ks[18], (D_MODEL,), 0.02),
    }

def reference(x_prompt, x_sample, cache_win_k, cache_win_v, state_pool, state_gla, norm1_g, w_in,
              w_gate2, b_gate, w_pool, pool_scale, gla_norm_g, w_o, norm2_g, w_ffn_gate, w_ffn_up,
              w_ffn_down, final_norm_g):
    xp, xs = x_prompt, x_sample
    Bp = xp.shape[0]
    keep = min(WIN_MAX, xp.shape[1])
    p_k, p_v, p_pool, p_gla = [], [], [], []
    s_k, s_v, s_pool, s_gla = [], [], [], []
    for l in range(DEPTH):
        wl = (norm1_g[l], w_in[l], w_gate2[l], b_gate[l], w_pool[l], pool_scale[l], gla_norm_g[l],
              w_o[l], norm2_g[l], w_ffn_gate[l], w_ffn_up[l], w_ffn_down[l])
        s0 = jnp.zeros((Bp, H_C, DK_C, DV_C), jnp.float32)
        xp, ka, va, pool_new, S = layer(xp, None, None, s0, 0, *wl)
        p_k.append(ka[:, -keep:])
        p_v.append(va[:, -keep:])
        p_pool.append(pool_new)
        p_gla.append(S)
        xs, ka, va, pool_new, S = layer(xs, (cache_win_k[l], cache_win_v[l]), state_pool[l], state_gla[l],
                                        PAST_LEN, *wl)
        s_k.append(ka)
        s_v.append(va)
        s_pool.append(pool_new)
        s_gla.append(S)
    y_prompt = rmsnorm(xp, final_norm_g)
    y_sample = rmsnorm(xs, final_norm_g)
    return (y_prompt, y_sample, jnp.stack(p_k), jnp.stack(p_v), jnp.stack(p_pool), jnp.stack(p_gla),
            jnp.stack(s_k), jnp.stack(s_v), jnp.stack(s_pool), jnp.stack(s_gla))


_drawn_inputs = setup_inputs


def setup_inputs(seed=0):
    import zlib

    import numpy as np

    out = dict(_drawn_inputs(seed))
    spreads = {}
    factors = {'pool_scale': 61.394,
     'gla_norm_g': 76.03,
     'norm2_g': 11.45,
     'final_norm_g': 22.859,
     'cache_win_k': 3.603,
     'cache_win_v': 2.847}
    for name, (base, spread) in spreads.items():
        noise = np.random.default_rng([zlib.crc32(name.encode()), seed]).standard_normal(out[name].shape)
        drawn = base * np.exp(spread * noise) if base else spread * noise
        out[name] = __import__('jax').numpy.asarray(drawn.astype(out[name].dtype))
    for name, factor in factors.items():
        out[name] = (out[name] * factor).astype(out[name].dtype)
    return out
```

```python
import concourse.bass as bass
from concourse import mybir
from contextlib import ExitStack

F32 = mybir.dt.float32
F32R = mybir.dt.float32r
I32 = mybir.dt.int32
ALU = mybir.AluOpType
ACT = mybir.ActivationFunctionType
AX = mybir.AxisListType

P = 128
D = 2048
KT = D // P
TP, TB, TT = 512, 8, 8
TS = TB * TT
T = TP + TS
HALF = T // 2
NTT = -(-T // P)
TILES = [(n * P, min(P, T - n * P)) for n in range(-(-T // P))]
HA, HD = 6, 128
DA = HA * HD
HC, DK, DV = 4, 96, 192
CK, CV = HC * DK, HC * DV
DB, NPOOL, PBUF = 512, 4, 15
RANK = 16
PAST = 2048
FF = 5632
NJ = FF // 256
EPS = 1e-6
GATE_NORM = 16.0
OQ, OK, OV, OU = 0, DA, 2 * DA, 3 * DA
OQC = OU + DB
OKC = OQC + CK
OVC = OKC + CK
ORC = OVC + CV
OGA = ORC + CV
G_IN, G_O = OGA // 256, D // 256
MIX_B, MIX_C = DA // P, (DA + DB) // P
NEG = -1e30
LN2 = 0.6931471805599453
LN3 = 1.0986122886681098
UNIQ, DIL, LAST = 6, 3, 1
NBLK = UNIQ + DIL + LAST
SCALE_A = HD ** -0.5
SCALE_C = DK ** -0.5
CHUNK_P, CHUNK_S = 32, TT


def count_log(dist, window_ok=True):
    n = int(0 <= dist <= 128) + int(dist >= 0 and dist % 4 == 0 and dist <= 512) \
        + int(dist >= 0 and dist % 16 == 0 and dist <= 2048)
    return [NEG, 0.0, LN2, LN3][n]


TABLE = {}
_at = 0
for _name, _w in (("ident", P), ("mask_a", TP), ("log_dve", UNIQ + 2 * DIL), ("log_last", TT), ("log_new", TS),
                  ("neg_own", TT), ("neg_oth", TT), ("is_own", TT), ("is_oth", TT),
                  ("upto_p", P), ("after_p", P), ("chunk_p", P // CHUNK_P),
                  ("upto_s", TS), ("after_s", TS), ("chunk_s", TB), ("inv_count", NPOOL * 16)):
    TABLE[_name] = (_at, _w)
    _at += _w
TABLE_W = _at


def table_columns():
    import numpy as np
    t = np.zeros((P, TABLE_W), np.float32)

    def col(name):
        a, w = TABLE[name]
        return t[:, a:a + w]

    col("ident")[:] = np.eye(P)
    for p in range(P):
        for c in range(TP):
            col("mask_a")[p, c] = count_log(p + TP - P - c) / SCALE_A
        own, oth = p % TT, (p + 4) % TT
        for j in range(DIL):
            r = 1536 + P * j + p
            col("log_dve")[p, UNIQ + j] = count_log(PAST + own - r)
            col("log_dve")[p, UNIQ + DIL + j] = count_log(PAST + oth - r)
        for q in range(TT):
            col("log_last")[p, q] = count_log(PAST + q - (PAST - P + p))
            col("neg_own")[p, q] = 0.0 if q == own else NEG
            col("neg_oth")[p, q] = 0.0 if q == oth else NEG
            col("is_own")[p, q] = q == own
            col("is_oth")[p, q] = q == oth
    for r in range(TS):
        for c in range(TS):
            same = r // TT == c // TT
            col("log_new")[r, c] = count_log(c - r) if same else NEG
            col("upto_s")[r, c] = (same and r <= c) / GATE_NORM
            col("after_s")[r, c] = (same and r > c) / GATE_NORM
        col("chunk_s")[r, r // TT] = 1 / GATE_NORM
    for r in range(P):
        for c in range(P):
            same = r // CHUNK_P == c // CHUNK_P
            col("upto_p")[r, c] = (same and r <= c) / GATE_NORM
            col("after_p")[r, c] = (same and r > c) / GATE_NORM
        col("chunk_p")[r, r // CHUNK_P] = 1 / GATE_NORM
    for g in range(NPOOL):
        for c in range(16):
            col("inv_count")[:, 16 * g + c] = 1.0 / min(2 << g, c + 1)
    return t


class Steps:

    def __init__(self, eng, sem, base=0):
        self.eng, self.sem, self.base, self.n = eng, sem, base, 0

    def done(self, ins):
        ins.then_inc(self.sem, 1)
        self.n += 1
        return self.n

    def wait(self, n):
        self.eng.wait_ge(self.sem, self.base + n)

    def last(self):
        self.wait(self.n)


def build(nc, x_prompt, x_sample, cache_k, cache_v, state_pool, state_gla, norm1_g, w_in, w_gate2, b_gate,
          w_pool, pool_scale, gla_norm_g, w_o, norm2_g, w_gate, w_up, w_down, final_g, table,
          y_p, y_s, o_pk, o_pv, o_pp, o_pg, o_sk, o_sv, o_sp, o_sg):
    proj_d = nc.dram_tensor("proj_scratch", (OGA, T), F32).ap()
    xT_d = nc.dram_tensor("xT_scratch", (P, KT * T), F32).ap()
    q_d = nc.dram_tensor("q_scratch", (2, TS, DA), F32).ap()
    oa_d = nc.dram_tensor("decode_out_scratch", (TS, DA), F32).ap()
    den_d = nc.dram_tensor("decode_den_scratch", (HA, TS), F32).ap()
    proj_m = proj_d.rearrange("(m p) t -> p m t", p=P)

    x_d = [x_prompt[0, a:a + n, :] if a < TP else x_sample.rearrange("b t d -> (b t) d") for a, n in TILES]
    y_d = [y_p[0, a:a + n, :] if a < TP else y_s.rearrange("b t d -> (b t) d") for a, n in TILES]
    ck = cache_k[0].rearrange("b r h d -> b r (h d)")
    cv = cache_v[0].rearrange("b r h d -> b r (h d)")
    pk, pv = (a[0, 0].rearrange("r h d -> r (h d)") for a in (o_pk, o_pv))
    sk, sv = (a[0].rearrange("b t h d -> (b t) (h d)") for a in (o_sk, o_sv))
    kv_out = [[pk[a:a + n, :], pv[a:a + n, :]] if a < TP else [sk, sv] for a, n in TILES]

    ctx = ExitStack()
    with ctx:
        def sb(name, shape, dt=F32):
            return ctx.enter_context(nc.sbuf_tensor(name, shape, dt))[tuple(slice(None) for _ in shape)]

        def sem(name):
            return ctx.enter_context(nc.semaphore(name))

        act_r = sb("act_r", [P, 2, KT, T], F32R)
        w_hi = sb("w_hi", [P, 4, 1024], F32R)
        w_lo = sb("w_lo", [P, 4, 1024], F32R)
        w_raw = sb("w_raw", [P, 4, 1024])
        ffn_r = sb("ffn_r", [P, 2, 2, 2, T], F32R)
        tab = sb("tab", [P, TABLE_W])
        ones = sb("ones", [P, P])
        vecs = sb("vecs", [P, 64])
        misc = sb("misc", [P, 8])
        GW = 15200
        g_sb = sb("general", [P, GW])
        psum = ctx.enter_context(nc.psum_tensor("psum", [P, 8, 512], F32))
        pool_at = [0]

        def area(*shape, at=None):
            n = 1
            for s in shape:
                n *= s
            a = pool_at[0] if at is None else at
            pool_at[0] = a + n
            assert a + n <= GW, (a, n)
            v = g_sb[:, a:a + n]
            if len(shape) == 2:
                v = v.rearrange("p (a b) -> p a b", a=shape[0])
            if len(shape) == 3:
                v = v.rearrange("p (a b c) -> p a b c", a=shape[0], b=shape[1])
            return v

        def C(name, rows=P):
            a, w = TABLE[name]
            return tab[0:rows, a:a + w]

        ident = C("ident")
        eps_c = misc[:, 0:1]
        hi, lo = act_r[:, 0], act_r[:, 1]
        G1, G2, GF, GS, GN = (vecs[:, a:b] for a, b in ((0, 16), (16, 32), (32, 48), (48, 52), (52, 58)))

        xT = area(KT, T, at=0)
        tmp2 = area(2, T)
        rstd = area(T)
        xs = area(2, D)
        sil = area(2, T, at=KT * T + 3 * T)
        ftmp = area(2, T)
        stage_in = area(2, 2 * T, at=0)

        s_const = sem("consts_in")
        s_ready = sem("consts_ready")
        x_in = [sem(f"x_in{i}") for i in range(2)]
        xt_tr = sem("xt_transposed")
        xt_act = sem("xt_copied_act")
        xt_dve = sem("xt_copied_dve")
        xt_out = sem("xt_spilled")
        xt_in = sem("xt_back")
        sq_done = sem("squares_done")
        acc_done = sem("squares_added")
        ss_done = sem("square_sums_done")
        rms_done = sem("rms_done")
        rstd_done = sem("rstd_done")
        h_done = sem("h_done")
        hhi_done = sem("h_high_done")
        hlo_done = sem("h_low_done")
        raw_in = [sem(f"raw_in{i}") for i in range(4)]
        whi_done = sem("w_high_done")
        wlo_done = sem("w_low_done")
        w_used = sem("w_chunk_used")
        in_ev = sem("in_group_copied")
        in_out = [sem(f"in_group_stored{i}") for i in range(2)]
        o_added = sem("o_group_added")
        sil_done = sem("silu_done")
        f_done = sem("gated_done")
        fhi_done = sem("gated_high_done")
        flo_done = sem("gated_low_done")
        dn_done = sem("down_pair_done")
        dn_added = sem("down_pair_added")
        y_tr = sem("y_transposed")
        y_ev = [sem("y_copied_act"), sem("y_copied_dve")]
        y_out = [sem(f"y_stored{i}") for i in range(2)]
        yn_done = sem("y_normalised")

        block = ctx.enter_context(nc.Block())

        win_v = w_in[0, :, 0:OGA].rearrange("(q k p) e -> q p k e", k=4, p=P)
        wo_v = w_o[0].rearrange("(q k p) e -> q p k e", k=4, p=P)
        wg_v = w_gate[0].rearrange("(q k p) e -> q p k e", k=4, p=P)
        wu_v = w_up[0].rearrange("(q k p) e -> q p k e", k=4, p=P)
        wd_v = w_down[0].rearrange("(j k p) e -> j p k e", k=2, p=P)

        def load_group(sp, g, src):
            for q in range(4):
                if not (isinstance(g, int) and g == 0):
                    sp.wait_ge(wlo_done, 4 * (g - 1) + q + 1)
                k, e = (4, 256) if src(q).shape[1] == 4 else (2, 512)
                sp.dma_start(w_raw[:, q].rearrange("p (k e) -> p k e", k=k), src(q)).then_inc(raw_in[q], 16)

        def cols(v, g):
            return lambda q: v[q, :, :, bass.ds(g * 256, 256)]

        def down_src(j):
            return lambda q: wd_v[bass.ds(j, 1), :, :, 512 * q:512 * q + 512].rearrange("o p k e -> (o p) k e")

        def split_high(act, g, q):
            act.wait_ge(raw_in[q], 16 * (g + 1))
            if not (isinstance(g, int) and g == 0):
                act.wait_ge(w_used, 4 * (g - 1) + q + 1)
            act.activation(w_hi[:, q], w_raw[:, q], ACT.Copy).then_inc(whi_done, 1)

        def split_low(dve, g, q):
            dve.wait_ge(whi_done, 4 * g + q + 1)
            dve.tensor_tensor(w_lo[:, q], w_raw[:, q], w_hi[:, q].bitcast(F32), ALU.subtract).then_inc(wlo_done, 1)

        def product(pe, out2, wslot, c0, rhs_hi, rhs_lo, first, last):
            for w, r, n in ((w_hi, rhs_hi, 0), (w_hi, rhs_lo, 1), (w_lo, rhs_hi, 2)):
                for half in range(2):
                    mm = pe.matmul(psum[:, out2 + half, 0:HALF], w[:, wslot, c0:c0 + P],
                                   r[:, half * HALF:(half + 1) * HALF],
                                   start=first and n == 0, stop=last and n == 2)
            return mm

        def full_group(pe, g, bank, norm=None):
            for q in range(4):
                pe.wait_ge(wlo_done, 4 * g + q + 1)
                for k in range(4):
                    kk = 4 * q + k
                    if norm is not None:
                        pe.wait_ge(hlo_done, KT * norm + kk + 1)
                    for m in range(2):
                        mm = product(pe, bank + 2 * m, q, 256 * k + P * m, hi[:, kk], lo[:, kk], kk == 0, kk == KT - 1)
                mm.then_inc(w_used, 1)
            return mm

        def two(bank):
            return psum[:, bank:bank + 4, 0:HALF]

        def sp_start(sp):
            sp.dma_start(tab[:, :], table).then_inc(s_const, 16)
            for tt, (a, n) in enumerate(TILES):
                if tt >= 2:
                    sp.wait_ge(xt_tr, 4 * (tt - 1))
                sp.dma_start(xs[0:n, tt % 2, :], x_d[tt]).then_inc(x_in[tt % 2], 16)
                if tt == 0:
                    rows = vrow[0:16, :], vrow[16:32, :], vrow[32:48, :], vrow[48:52, :]
                    for dst, src in zip(rows, (norm1_g[0], norm2_g[0], final_g, pool_scale[0])):
                        sp.dma_start(dst, src.rearrange("(k p) -> k p", p=P)).then_inc(s_vec, 16)
                    gn = gla_norm_g[0:1, :]
                    for half in range(2):
                        r = 52 + 3 * half
                        for dst, src in ((vrow[r:r + 1, :], gn[:, 0:P]), (vrow[r + 1:r + 2, 0:DV - P], gn[:, P:DV]),
                                         (vrow[r + 1:r + 2, DV - P:P], gn[:, 0:2 * P - DV]),
                                         (vrow[r + 2:r + 3, :], gn[:, 2 * P - DV:DV])):
                            sp.dma_start(dst, src).then_inc(s_vec, 16)
                    load_group(sp, 0, cols(win_v, 0))
                    sp.dma_start(ga_raw, w_in[0, :, OGA:OGA + RANK].rearrange("(k p) e -> p k e", p=P)).then_inc(s_ga, 16)
            sp.wait_ge(xt_act, 10)
            sp.wait_ge(xt_dve, 10)
            sp.dma_start(xT_d, xT.rearrange("p k t -> p (k t)")).then_inc(xt_out, 16)

        s_vec = sem("gain_rows_in")
        s_vt = sem("gain_rows_transposed")
        s_vc = sem("gain_columns_done")
        s_ga = sem("gate_columns_in")
        s_gs = sem("gate_columns_split")
        s_gm = sem("gate_product_done")
        s_gT = sem("gate_inputs_done")
        vrow = sb("vrow", [64, P])
        ga_raw = sb("ga_raw", [P, KT, RANK])
        ga_hi = ffn_r[:, 0, 0, 0, 0:KT * RANK].rearrange("p (k e) -> p k e", k=KT)
        ga_lo = ffn_r[:, 0, 1, 0, 0:KT * RANK].rearrange("p (k e) -> p k e", k=KT)
        gaT = sb("gaT", [32, T])

        def transposes_in(pe):
            pe.wait_ge(s_const, 16)
            for tt, (a, n) in enumerate(TILES):
                pe.wait_ge(x_in[tt % 2], 16 * (tt // 2 + 1))
                for g in range(4):
                    u = 4 * tt + g
                    if u >= 8:
                        pe.wait_ge(xt_act if u % 2 == 0 else xt_dve, (u - 8) // 2 + 1)
                    for k in range(4):
                        mm = pe.transpose(psum[:, u % 8, P * k:P * k + n], xs[0:n, tt % 2, P * (4 * g + k):P * (4 * g + k + 1)],
                                          ident[0:n, 0:n])
                    mm.then_inc(xt_tr, 1)
            pe.wait_ge(s_vec, 16 * 12)
            pe.wait_ge(xt_act, 7)
            pe.transpose(psum[:, 4, 0:58], vrow[0:58, :], ident[0:58, 0:58]).then_inc(s_vt, 1)

        def copies_in(eng, own, parity):
            for u in range(parity, 4 * NTT, 2):
                tt, g = divmod(u, 4)
                a, n = TILES[tt]
                eng.wait_ge(xt_tr, u + 1)
                dst = xT[:, 4 * g:4 * g + 4, a:a + n]
                src = psum[:, u % 8, :].rearrange("p (k t) -> p k t", k=4)[:, :, 0:n]
                ins = eng.activation(dst, src, ACT.Copy) if own is xt_act else eng.tensor_copy(dst, src)
                ins.then_inc(own, 1)

        def norm_act(act, nrm, hi_out=True):
            for k in range(KT):
                n = KT * nrm + k
                if k >= 2:
                    act.wait_ge(acc_done, n - 1)
                elif nrm and k < 2:
                    act.wait_ge(hlo_done, KT * nrm)
                act.activation(tmp2[:, k % 2], xT[:, k], ACT.Square).then_inc(sq_done, 1)
            act.wait_ge(ss_done, nrm + 1)
            act.activation(rstd.rearrange("p (a t) -> p a t", a=2), psum[:, 0:2, 0:HALF], ACT.Sqrt, bias=eps_c, scale=1.0 / D).then_inc(rms_done, 1)
            if hi_out:
                for k in range(KT):
                    n = KT * nrm + k
                    act.wait_ge(h_done, n + 1)
                    act.activation(hi[:, k], tmp2[:, k % 2], ACT.Copy).then_inc(hhi_done, 1)

        def norm_dve(dve, nrm, gain, hi_out=True):
            for k in range(KT):
                n = KT * nrm + k
                dve.wait_ge(sq_done, n + 1)
                if k:
                    dve.wait_ge(acc_done, n)
                    ins = dve.tensor_tensor(rstd, rstd, tmp2[:, k % 2], ALU.add)
                else:
                    ins = dve.tensor_copy(rstd, tmp2[:, 0])
                ins.then_inc(acc_done, 1)
            dve.wait_ge(rms_done, nrm + 1)
            dve.reciprocal(rstd, rstd).then_inc(rstd_done, 1)
            dve.wait_ge(rstd_done, nrm + 1)
            if hi_out:
                for k in range(KT):
                    n = KT * nrm + k
                    if k >= 2:
                        dve.wait_ge(hlo_done, n - 1)
                    dve.scalar_tensor_tensor(out=tmp2[:, k % 2], in0=xT[:, k], scalar=gain[:, k:k + 1], in1=rstd,
                                             op0=ALU.mult, op1=ALU.mult).then_inc(h_done, 1)

        def norm_pool(pool, nrm):
            for k in range(KT):
                n = KT * nrm + k
                pool.wait_ge(hhi_done, n + 1)
                pool.tensor_tensor(lo[:, k], tmp2[:, k % 2], hi[:, k].bitcast(F32), ALU.subtract).then_inc(hlo_done, 1)

        def norm_pe(pe, nrm):
            pe.wait_ge(acc_done, KT * (nrm + 1))
            for half in range(2):
                mm = pe.matmul(psum[:, half, 0:HALF], ones[:, :], rstd[:, half * HALF:(half + 1) * HALF], start=True, stop=True)
            mm.then_inc(ss_done, 1)

        def in_store(pool, g, s, i):
            pool.wait_ge(in_ev, 2 + g + 1)
            pool.dma_start(proj_m[:, bass.ds(2 * g, 2), :], stage_in[:, s].rearrange("p (m t) -> p m t", m=2)).then_inc(in_out[s], 16)

        def in_copy(dve, g, s, i):
            dve.wait_ge(w_used, 4 * g + 4)
            if not isinstance(i, int):
                dve.wait_ge(in_out[s], 16 * i)
            dve.tensor_copy(stage_in[:, s].rearrange("p (a t) -> p a t", a=4), two(4 * s)).then_inc(in_ev, 1)

        def in_pe(pe):
            pe.wait_ge(rms_done, 1)
            for g in range(2):
                full_group(pe, g, 4 * g, norm=0)
            with pe.Fori(1, G_IN // 2) as i:
                for s in range(2):
                    pe.wait_ge(in_ev, 2 * i + s + 1)
                    full_group(pe, 2 * i + s, 4 * s)
            pe.wait_ge(s_gs, 2)
            pe.wait_ge(in_ev, G_IN + 1)
            for k in range(KT):
                for w, r, n in ((ga_hi, hi, 0), (ga_hi, lo, 1), (ga_lo, hi, 2)):
                    for half in range(2):
                        mm = pe.matmul(psum[0:RANK, half, 0:HALF], w[:, k, :], r[:, k, half * HALF:(half + 1) * HALF],
                                       start=k == 0 and n == 0, stop=k == KT - 1 and n == 2)
            mm.then_inc(s_gm, 1)

        def in_act(act):
            for q in range(4):
                split_high(act, 0, q)
            act.wait_ge(s_ga, 16)
            act.activation(ga_hi, ga_raw, ACT.Copy).then_inc(s_gs, 1)

        def in_act_loop(act):
            with act.Fori(0, G_IN) as g:
                for q in range(4):
                    split_high(act, g + 1, q)
            act.wait_ge(s_gm, 1)
            act.wait_ge(s_ready, 3)
            act.activation(gaT[0:RANK, :].rearrange("p (a t) -> p a t", a=2), psum[0:RANK, 0:2, 0:HALF], ACT.Copy).then_inc(s_gT, 1)

        def in_dve(dve):
            for q in range(4):
                split_low(dve, 0, q)
            dve.wait_ge(s_gs, 1)
            dve.tensor_tensor(ga_lo, ga_raw, ga_hi.bitcast(F32), ALU.subtract).then_inc(s_gs, 1)

        def in_dve_loop(dve):
            def pair(i):
                for s in range(2):
                    g = 2 * i + s
                    for q in range(4):
                        split_low(dve, g + 1, q)
                    in_copy(dve, g, s, i)

            pair(0)
            with dve.Fori(1, G_IN // 2) as i:
                pair(i)

        def in_pool(pool):
            with pool.Fori(0, G_IN // 2) as i:
                for s in range(2):
                    in_store(pool, 2 * i + s, s, i)

        def o_pe(pe):
            pe.wait_ge(s_mix, 1)
            with pe.Fori(0, G_O // 2) as i:
                for s in range(2):
                    pe.wait_ge(o_added, 2 * i + s + 1)
                    full_group(pe, G_IN + 2 * i + s, 4 * s)

        def o_dve(dve):
            dve.wait_ge(xt_in, 16)
            with dve.Fori(0, G_O // 2) as i:
                for s in range(2):
                    g = 2 * i + s
                    for q in range(4):
                        split_low(dve, G_IN + g + 1, q)
                    dve.wait_ge(w_used, 4 * (G_IN + g) + 4)
                    x2 = xT[:, bass.ds(2 * g, 2), :].rearrange("p m (a t) -> p (m a) t", a=2)
                    dve.tensor_tensor(x2, two(4 * s), x2, ALU.add).then_inc(o_added, 1)

        def o_act(act):
            with act.Fori(0, G_O) as g:
                for q in range(4):
                    split_high(act, G_IN + g + 1, q)

        def g_gate(j):
            return G_IN + G_O + (3 * j - 1 if not (isinstance(j, int) and j == 0) else 0)

        def g_up(j):
            return g_gate(j) + 1

        def g_down(j):
            return G_IN + G_O + 3 * (j + 1) + (1 if not (isinstance(j, int) and j == NJ - 1) else -1)

        def sp_ffn(sp):
            load_group(sp, g_gate(0), cols(wg_v, 0))
            load_group(sp, g_up(0), cols(wu_v, 0))
            with sp.Fori(1, NJ) as j:
                load_group(sp, g_gate(j), cols(wg_v, j))
                load_group(sp, g_up(j), cols(wu_v, j))
                load_group(sp, g_down(j - 1), down_src(j - 1))
            load_group(sp, g_down(NJ - 1), down_src(NJ - 1))

        def down_group(pe, j, s, last=False):
            g = g_down(j)
            fh, fl = ffn_r[:, s, 0], ffn_r[:, s, 1]
            pe.wait_ge(flo_done, 2 * j + 2)
            for q in range(4):
                pe.wait_ge(wlo_done, 4 * g + q + 1)
                for pair in range(2):
                    n = 2 * q + pair
                    if n >= 2 or last:
                        pe.wait_ge(dn_added, 8 * j + n - 1)
                    for k in range(2):
                        for m in range(2):
                            mm = product(pe, 4 * pair + 2 * m, q, 512 * k + 256 * pair + P * m, fh[:, k], fl[:, k], k == 0, k == 1)
                    mm.then_inc(dn_done if pair == 0 else w_used, 1)

        def gate_up(pe, j, norm=None):
            pe.wait_ge(dn_added, 8 * (j - 1) - 1) if not (isinstance(j, int) and j <= 1) else None
            full_group(pe, g_gate(j), 0, norm)
            pe.wait_ge(dn_added, 8 * (j - 1)) if not (isinstance(j, int) and j <= 1) else None
            full_group(pe, g_up(j), 4)

        def before_down(pe, j):
            pe.wait_ge(sil_done, 2 * j + 2)
            pe.wait_ge(f_done, 2 * j + 2)

        def ffn_pe(pe):
            gate_up(pe, 0, norm=1)
            gate_up(pe, 1)
            before_down(pe, 1)
            down_group(pe, 0, 0)
            with pe.Fori(0, NJ // 2 - 1) as i:
                for s in range(2):
                    gate_up(pe, 2 * i + 2 + s)
                    before_down(pe, 2 * i + 2 + s)
                    down_group(pe, 2 * i + 1 + s, 1 - s)
            down_group(pe, NJ - 1, 1, last=True)

        def act_silu(act, j):
            act.wait_ge(w_used, 4 * g_gate(j) + 4)
            for t in range(2):
                if not (isinstance(j, int) and j == 0):
                    act.wait_ge(f_done, 2 * (j - 1) + t + 1)
                act.activation(sil[:, t].rearrange("p (a t) -> p a t", a=2), psum[:, 2 * t:2 * t + 2, 0:HALF], ACT.Silu).then_inc(sil_done, 1)

        def act_fhigh(act, j, s):
            for t in range(2):
                act.wait_ge(f_done, 2 * j + t + 1)
                if not (isinstance(j, int) and j < 2):
                    act.wait_ge(w_used, 4 * g_down(j - 2) + 4)
                act.activation(ffn_r[:, s, 0, t], ftmp[:, t], ACT.Copy).then_inc(fhi_done, 1)

        def dve_gated(dve, j):
            dve.wait_ge(w_used, 4 * g_up(j) + 4)
            for t in range(2):
                dve.wait_ge(sil_done, 2 * j + t + 1)
                if not (isinstance(j, int) and j == 0):
                    dve.wait_ge(flo_done, 2 * (j - 1) + t + 1)
                dve.tensor_tensor(ftmp[:, t].rearrange("p (a t) -> p a t", a=2), psum[:, 4 + 2 * t:6 + 2 * t, 0:HALF],
                                  sil[:, t].rearrange("p (a t) -> p a t", a=2), ALU.mult).then_inc(f_done, 1)

        def dve_flow(dve, j, s):
            for t in range(2):
                dve.wait_ge(fhi_done, 2 * j + t + 1)
                dve.tensor_tensor(ffn_r[:, s, 1, t], ftmp[:, t], ffn_r[:, s, 0, t].bitcast(F32), ALU.subtract).then_inc(flo_done, 1)

        def dve_add_down(dve, j, n):
            if n % 2 == 0:
                dve.wait_ge(dn_done, 4 * j + n // 2 + 1)
            else:
                dve.wait_ge(w_used, 4 * g_down(j) + n // 2 + 1)
            if not (isinstance(j, int) and j == 0):
                dve.wait_ge(dn_added, 8 * (j - 1) + n + 1)
            x2 = xT[:, 2 * n:2 * n + 2, :].rearrange("p m (a t) -> p (m a) t", a=2)
            dve.tensor_tensor(x2, two(4 * (n % 2)), x2, ALU.add).then_inc(dn_added, 1)

        def ffn_act(act):
            def split(g, qs):
                for q in qs:
                    split_high(act, g, q)

            def step(j, s, nxt):
                split(g_up(j), range(3))
                act_silu(act, j)
                split(g_up(j), [3])
                split(g_down(j - 1), range(4))
                act_fhigh(act, j, s)
                split(nxt, range(4))

            split(g_up(0), range(3))
            act_silu(act, 0)
            split(g_up(0), [3])
            split(g_gate(1), range(4))
            act_fhigh(act, 0, 0)
            step(1, 1, g_gate(2))
            with act.Fori(0, NJ // 2 - 2) as i:
                for s in range(2):
                    step(2 * i + 2 + s, s, g_gate(2 * i + 3 + s))
            step(NJ - 2, 0, g_gate(NJ - 1))
            step(NJ - 1, 1, g_down(NJ - 1))

        def ffn_dve(dve):
            def split(g, qs):
                for q in qs:
                    split_low(dve, g, q)

            def step(j, s, nxt):
                split(g_up(j), range(4))
                split(g_down(j - 1), range(3))
                dve_gated(dve, j)
                split(g_down(j - 1), [3])
                dve_flow(dve, j, s)
                for q in range(4):
                    dve_add_down(dve, j - 1, 2 * q)
                    dve_add_down(dve, j - 1, 2 * q + 1)
                    split(nxt, [q])

            split(g_up(0), range(4))
            split(g_gate(1), range(3))
            dve_gated(dve, 0)
            split(g_gate(1), [3])
            dve_flow(dve, 0, 0)
            step(1, 1, g_gate(2))
            with dve.Fori(0, NJ // 2 - 2) as i:
                for s in range(2):
                    step(2 * i + 2 + s, s, g_gate(2 * i + 3 + s))
            step(NJ - 2, 0, g_gate(NJ - 1))
            step(NJ - 1, 1, g_down(NJ - 1))
            for n in range(8):
                dve_add_down(dve, NJ - 1, n)

        ysb = area(2, D, at=KT * T + 3 * T)

        def final_dve(dve):
            norm_dve(dve, 2, GF, hi_out=False)
            for k in range(KT):
                dve.scalar_tensor_tensor(out=xT[:, k], in0=xT[:, k], scalar=GF[:, k:k + 1], in1=rstd,
                                         op0=ALU.mult, op1=ALU.mult).then_inc(yn_done, 1)
            final_copies(dve, 1)

        def final_act(act):
            norm_act(act, 2, hi_out=False)
            final_copies(act, 0)

        def final_copies(eng, parity):
            for u in range(parity, 4 * NTT, 2):
                tt, g = divmod(u, 4)
                a, n = TILES[tt]
                eng.wait_ge(y_tr, u + 1)
                if tt >= 2:
                    eng.wait_ge(y_out[tt % 2], 16 * (tt // 2))
                dst, src = ysb[0:n, tt % 2, 512 * g:512 * g + 512], psum[0:n, u % 8, :]
                ins = eng.activation(dst, src, ACT.Copy) if parity == 0 else eng.tensor_copy(dst, src)
                ins.then_inc(y_ev[parity], 1)

        def final_pe(pe):
            norm_pe(pe, 2)
            for tt, (a, n) in enumerate(TILES):
                for g in range(4):
                    u = 4 * tt + g
                    pe.wait_ge(yn_done, 4 * g + 4)
                    if u >= 8:
                        pe.wait_ge(y_ev[u % 2], (u - 8) // 2 + 1)
                    for k in range(4):
                        mm = pe.transpose(psum[0:n, u % 8, P * k:P * k + P], xT[:, 4 * g + k, a:a + n], ident)
                    mm.then_inc(y_tr, 1)

        def final_sp(sp):
            for tt, (a, n) in enumerate(TILES):
                for par in range(2):
                    sp.wait_ge(y_ev[par], 2 * tt + 2)
                sp.dma_start(y_d[tt], ysb[0:n, tt % 2, :]).then_inc(y_out[tt % 2], 16)
            sp.wait_ge(y_out[0], 48)
            sp.wait_ge(y_out[1], 32)

        kvf = area(2, 2 * HA * P, at=0)
        kvt = area(2, 2 * DA)
        kv_in = [sem(f"kv_in{i}") for i in range(2)]
        kv_tr = sem("kv_transposed")
        kv_act = sem("kv_copied_act")
        kv_dve = sem("kv_copied_dve")
        kv_st = [sem(f"kv_stored{i}") for i in range(2)]

        def kv_sp(sp):
            for s in range(2):
                sp.wait_ge(in_out[s], 16 * (G_IN // 2))
            def store(tt):
                a, n = TILES[tt]
                sp.wait_ge(kv_act, 2 * tt + 2)
                sp.wait_ge(kv_dve, tt + 1)
                for i in range(2):
                    sp.dma_start(kv_out[tt][i], kvt[0:n, tt % 2, DA * i:DA * i + DA]).then_inc(kv_st[tt % 2], 16)
            for tt, (a, n) in enumerate(TILES):
                if tt >= 2:
                    sp.wait_ge(kv_tr, 3 * (tt - 1))
                sp.dma_start(kvf[:, tt % 2, :].rearrange("p (m t) -> p m t", t=P)[:, :, 0:n],
                             proj_m[:, OK // P:OU // P, a:a + n]).then_inc(kv_in[tt % 2], 16)
                if tt:
                    store(tt - 1)
            store(NTT - 1)

        def kv_pe(pe):
            pe.wait_ge(s_gT, 1)
            pe.wait_ge(in_ev, 2 + G_IN)
            for tt, (a, n) in enumerate(TILES):
                pe.wait_ge(kv_in[tt % 2], 16 * (tt // 2 + 1))
                for b in range(3):
                    if tt >= 2:
                        pe.wait_ge(*((kv_act, 2 * (tt - 2) + b + 1) if b < 2 else (kv_dve, tt - 1)))
                    for k in range(4):
                        m = 4 * b + k
                        mm = pe.transpose(psum[0:n, 3 * (tt % 2) + b, P * k:P * k + P],
                                          kvf[:, tt % 2, P * m:P * m + n], ident)
                    mm.then_inc(kv_tr, 1)

        def kv_copies(eng, own, banks):
            for tt, (a, n) in enumerate(TILES):
                for b in banks:
                    eng.wait_ge(kv_tr, 3 * tt + b + 1)
                    if tt >= 2:
                        eng.wait_ge(kv_st[tt % 2], 32 * (tt // 2))
                    dst, src = kvt[0:n, tt % 2, 512 * b:512 * b + 512], psum[0:n, 3 * (tt % 2) + b, :]
                    ins = eng.activation(dst, src, ACT.Copy) if own is kv_act else eng.tensor_copy(dst, src)
                    ins.then_inc(own, 1)

        NS = UNIQ + 2 * DIL
        k_sb = area(5, DA, at=0)
        v_sb = area(5, DA)
        q_rep = area(2, DA)
        u_sb = area(2, DA)
        kT9 = area(DA)
        q_tok = area(DA)
        v_new = area(DA)
        junk = area(DA)
        o_sb = q_tok
        qf = area(HA, TS)
        kf = area(HA, TS)
        qs = qf
        s_dve = area(HA, NS)
        s_all = area(HA * TT)
        s_new = area(HA * TT)
        s_max_w = area(P)
        s_max = s_max_w[:, 0:HA * TT]
        s_tmp = area(HA * TT)
        s_tot = area(HA * TT)
        r_own = area(HA)
        r_oth = area(HA)
        diag = area(HA * TT)
        m_col = area(1)
        den_all = area(TB)
        den_tok = area(HA)

        dec_in = sem("decode_inputs_in")
        dec_z = sem("decode_padding_zero")
        dec_q = sem("decode_queries_ready")
        dec_qT = sem("decode_queries_transposed")
        dec_qt = sem("decode_queries_tokenmajor")
        dec_qd = sem("decode_queries_in_dram")
        dec_qd2 = sem("decode_queries_swapped")
        q_in = sem("decode_query_rows_in")
        k_in = [sem(f"k_in{i}") for i in range(5)]
        v_in = [sem(f"v_in{i}") for i in range(5)]
        k_used = sem("k_block_used")
        k9_used = sem("k_last_block_used")
        v_used = sem("v_block_used")
        kT9_done = sem("k_last_block_copied")
        sl_done = sem("last_scores_done")
        dd = sem("decode_dve_steps")
        mT_done = sem("decode_max_transposed")
        mb_done = sem("decode_max_spread")
        e_done = sem("decode_exp_done")
        den_done = sem("decode_den_done")
        o_ready = sem("decode_out_done")
        ob_done = sem("decode_out_copied")
        ob_out = sem("decode_out_stored")
        DVE_B, AT = 98, {"max": 10, "diag": 12, "arg": 20, "tot": 26, "u": 98}

        def hb(ap, rows=P):
            return ap.unsqueeze(1).to_broadcast([rows, HA, TT])

        def tb(ap, n=TT, rows=P):
            return ap.unsqueeze(2).to_broadcast([rows, HA, n])

        def v3(ap):
            return ap.rearrange("p (h t) -> p h t", h=HA)

        def dec_sp(sp):
            sp.wait_ge(kv_st[0], 32 * 3)
            sp.wait_ge(kv_st[1], 32 * 2)
            sp.wait_ge(kv_tr, 15)
            sp.dma_start(qf, proj_m[:, 0:HA, TP:T]).then_inc(dec_in, 16)
            sp.dma_start(kf, proj_m[:, HA:2 * HA, TP:T]).then_inc(dec_in, 16)
            sp.dma_start(v_new[0:TS, :], sv).then_inc(dec_in, 16)
            sp.wait_ge(dec_qt, 2)
            sp.dma_start(q_d[0], q_tok[0:TS, :]).then_inc(dec_qd, 16)
            sp.wait_ge(dec_qd, 16)
            for s in range(2):
                sp.dma_start(q_d[1].rearrange("(b s q) c -> s b q c", s=2, q=4)[1 - s],
                             q_d[0].rearrange("(b s q) c -> s b q c", s=2, q=4)[s]).then_inc(dec_qd2, 16)
            sp.wait_ge(dec_qd2, 32)

        def cache_rows(c, b, j):
            v = c[bass.ds(b, 1)].rearrange("o r c -> (o r) c")
            if j < UNIQ:
                return v[256 * j:256 * j + 256, :].rearrange("(n s) c -> n s c", s=16)[:, 0:TT, :]
            return v[1536 + P * (j - UNIQ):1536 + P * (j - UNIQ + 1), :]

        def dec_sp_b(sp, b):
            for j in range(NBLK):
                if j < 4:
                    sp.wait_ge(k_used, 9 * b + j + 6)
                elif j == 4:
                    sp.wait_ge(k9_used, b + 1)
                    sp.wait_ge(k_used, 9 * b + 9)
                    for i in range(2):
                        qv = q_d[i, bass.ds(b * TT, TT), :]
                        src = bass.AP(qv.tensor, qv.offset, [[0, P // TT], [DA, TT], [1, DA]])
                        sp.dma_start(q_rep[:, i], src).then_inc(q_in, 16)
                else:
                    sp.wait_ge(k_used, 9 * b + 9 + j - 4)
                sp.dma_start(k_sb[:, j % 5], cache_rows(ck, b, j)).then_inc(k_in[j % 5], 16)

        def dec_pool_b(pool, b):
            for j in range(NBLK):
                if j < 4:
                    pool.wait_ge(v_used, 9 * b + j + 6)
                elif j == 4:
                    pool.wait_ge(o_ready, b + 1)
                else:
                    pool.wait_ge(v_used, 9 * b + 9 + j - 4)
                pool.dma_start(v_sb[:, j % 5], cache_rows(cv, b, j)).then_inc(v_in[j % 5], 16)

        def dec_act(act):
            act.wait_ge(dec_in, 48)
            act.activation(qs, qf, ACT.Copy, scale=SCALE_A).then_inc(dec_q, 1)
            act.wait_ge(dec_qT, 2)
            act.activation(q_tok[0:TS, 0:512], psum[0:TS, 6, :], ACT.Copy).then_inc(dec_qt, 1)
            act.activation(q_tok[0:TS, 512:DA], psum[0:TS, 7, 0:256], ACT.Copy).then_inc(dec_qt, 1)

        def dec_pe(pe):
            pe.wait_ge(dec_q, 1)
            for h in range(HA):
                mm = pe.transpose(psum[0:TS, 6 + h // 4, P * (h % 4):P * (h % 4) + P], qs[:, h, :], ident)
                if h in (3, 5):
                    mm.then_inc(dec_qT, 1)
            pe.wait_ge(dec_qt, 2)
            pe.wait_ge(kv_act, 10)
            pe.wait_ge(kv_dve, 5)

        def dec_pe_scores(pe, b):
            pe.wait_ge(k_in[4], 32 * b + 32)
            for h in range(HA):
                mm = pe.transpose(psum[:, h // 4, P * (h % 4):P * (h % 4) + P], k_sb[:, 4, P * h:P * h + P], ident)
            mm.then_inc(k9_used, 1)
            pe.wait_ge(kT9_done, 2 * b + 2)
            for h in range(HA):
                q8 = qs[:, h, bass.ds(b * TT, TT)]
                pe.matmul(psum[:, 2, TT * h:TT * h + TT], kT9[:, P * h:P * h + P], q8, start=True, stop=True)
                mm = pe.matmul(psum[0:TS, 3, TT * h:TT * h + TT], kf[:, h, :], q8, start=True, stop=True)
            mm.then_inc(sl_done, 1)

        def dec_pe_max(pe, b):
            pe.wait_ge(dd, DVE_B * b + AT["max"])
            pe.transpose(psum[:, 4, 0:P], s_max_w, ident).then_inc(mT_done, 1)
            pe.wait_ge(dd, DVE_B * b + AT["diag"])
            pe.matmul(psum[:, 5, 0:HA * TT], ones[0:HA * TT, :], diag[0:HA * TT, :], start=True, stop=True).then_inc(mb_done, 1)

        def dec_pe_out(pe, b):
            pe.wait_ge(dd, DVE_B * b + AT["tot"])
            pe.wait_ge(ob_done, 3 * b + 1)
            pe.matmul(psum[0:HA * TT, 4, 0:1], s_tot, ones[:, 0:1], start=True, stop=False)
            pe.matmul(psum[0:HA * TT, 4, 0:1], s_new[0:TS, :], ones[0:TS, 0:1], start=False, stop=True).then_inc(den_done, 1)
            pe.wait_ge(v_in[4], 32 * b + 32)
            pe.wait_ge(dd, DVE_B * b + AT["u"])
            for bank, h0, h1 in ((6, 0, 4), (7, 4, 6)):
                for i, sel in ((0, "is_own"), (1, "is_oth")):
                    pe.matmul(psum[0:TT, bank, 0:P * (h1 - h0)], C(sel), u_sb[:, i, P * h0:P * h1], start=i == 0, stop=False,
                              skip_group_check=True)
                for h in range(h0, h1):
                    dst = psum[0:TT, bank, P * (h - h0):P * (h - h0) + P]
                    pe.matmul(dst, s_all[:, TT * h:TT * h + TT], v_sb[:, 4, P * h:P * h + P], start=False, stop=False,
                              skip_group_check=True)
                    mm = pe.matmul(dst, s_new[0:TS, TT * h:TT * h + TT], v_new[0:TS, P * h:P * h + P], start=False, stop=h == h1 - 1,
                                   skip_group_check=True)
            mm.then_inc(o_ready, 1)

        def dec_act_b(act, b):
            act.wait_ge(k9_used, b + 2)
            act.wait_ge(sl_done, b + 1)
            act.activation(kT9[:, 0:512], psum[:, 0, :], ACT.Copy).then_inc(kT9_done, 1)
            act.activation(kT9[:, 512:DA], psum[:, 1, 0:256], ACT.Copy).then_inc(kT9_done, 1)
            act.wait_ge(dd, DVE_B * b + AT["arg"])
            act.activation(s_dve, s_dve, ACT.Exp).then_inc(e_done, 1)
            act.activation(s_all, s_all, ACT.Exp).then_inc(e_done, 1)
            act.activation(s_new[0:TS, :], s_new[0:TS, :], ACT.Exp).then_inc(e_done, 1)
            act.wait_ge(den_done, b + 1)
            act.activation(den_all[0:HA * TT, bass.ds(b, 1)], psum[0:HA * TT, 4, 0:1], ACT.Copy).then_inc(ob_done, 1)
            act.wait_ge(o_ready, b + 2)
            act.wait_ge(ob_out, 16 * b + 16)
            act.activation(o_sb[0:TT, 0:512], psum[0:TT, 6, :], ACT.Copy).then_inc(ob_done, 1)
            act.activation(o_sb[0:TT, 512:DA], psum[0:TT, 7, 0:256], ACT.Copy).then_inc(ob_done, 1)
            act.wait_ge(ob_done, 3 * b + 4)
            act.dma_start(oa_d[bass.ds(b * TT, TT), :], o_sb[0:TT, :]).then_inc(ob_out, 16)

        def dec_dve_b(dve, b, base):
            st = Steps(dve, dd, base)
            at = {}
            dve.wait_ge(q_in, 32 * b + 32)
            junked = 0
            for j in range(UNIQ + DIL):
                dve.wait_ge(k_in[j % 5], 32 * b + 16 * (j // 5) + 16)
                for i in range(1 if j < UNIQ else 2):
                    col = j + (DIL if i else 0)
                    for h in range(HA):
                        kk = k_sb[:, j % 5, P * h:P * h + P]
                        last = j < UNIQ or i == 1
                        if not last and j > UNIQ:
                            dve.wait_ge(k_used, 9 * b + 9 + j)
                        ins = dve.tensor_tensor_reduce(kk if last else junk[:, P * h:P * h + P], kk, q_rep[:, i, P * h:P * h + P],
                                                       1.0, 0.0, ALU.mult, ALU.add, s_dve[:, h, col:col + 1])
                ins.then_inc(k_used, 1)
            dve.wait_ge(sl_done, b + 2)
            dve.wait_ge(k_used, 9 * b + 18)
            dve.wait_ge(o_ready, b + 1)
            st.done(dve.tensor_tensor(s_dve, s_dve, C("log_dve").unsqueeze(1).to_broadcast([P, HA, NS]), ALU.add))
            st.done(dve.tensor_tensor(v3(s_all), v3(psum[:, 2, 0:48]), hb(C("log_last")), ALU.add))
            st.done(dve.tensor_tensor(v3(s_new[0:TS, :]), v3(psum[0:TS, 3, 0:48]),
                                      hb(C("log_new", TS)[:, bass.ds(b * TT, TT)], TS), ALU.add))
            st.wait(1)
            st.done(dve.tensor_reduce(r_own, s_dve[:, :, 0:9], AX.X, ALU.max))
            st.done(dve.tensor_reduce(r_oth, s_dve[:, :, 9:NS], AX.X, ALU.max))
            st.last()
            st.done(dve.tensor_tensor(v3(s_max), tb(r_own), hb(C("neg_own")), ALU.add))
            st.done(dve.tensor_tensor(v3(s_tmp), tb(r_oth), hb(C("neg_oth")), ALU.add))
            st.last()
            st.done(dve.tensor_tensor(s_max, s_max, s_tmp, ALU.max))
            st.last()
            st.done(dve.tensor_tensor(s_max, s_max, s_all, ALU.max))
            st.last()
            at["max"] = st.done(dve.tensor_tensor(s_max[0:TS, :], s_max[0:TS, :], s_new[0:TS, :], ALU.max))
            dve.wait_ge(mT_done, b + 1)
            st.done(dve.tensor_reduce(m_col[0:48, :], psum[0:48, 4, 0:P], AX.X, ALU.max))
            st.last()
            at["diag"] = st.done(dve.tensor_scalar(diag[0:48, :], ident[0:48, 0:48], m_col[0:48, 0:1], -1.0, ALU.mult, ALU.mult))
            dve.wait_ge(mb_done, b + 1)
            mb = psum[:, 5, 0:48]
            st.done(dve.tensor_tensor(s_all, s_all, mb, ALU.add))
            st.done(dve.tensor_tensor(s_new[0:TS, :], s_new[0:TS, :], mb[0:TS, :], ALU.add))
            st.done(dve.tensor_tensor(v3(s_tmp), v3(mb), hb(C("is_own")), ALU.mult))
            st.done(dve.tensor_tensor(v3(s_tot), v3(mb), hb(C("is_oth")), ALU.mult))
            st.last()
            st.done(dve.tensor_reduce(r_own, v3(s_tmp), AX.X, ALU.add))
            st.done(dve.tensor_reduce(r_oth, v3(s_tot), AX.X, ALU.add))
            st.last()
            st.done(dve.tensor_tensor(s_dve[:, :, 0:9], s_dve[:, :, 0:9], tb(r_own, 9), ALU.add))
            at["arg"] = st.done(dve.tensor_tensor(s_dve[:, :, 9:NS], s_dve[:, :, 9:NS], tb(r_oth, 3), ALU.add))
            dve.wait_ge(e_done, 3 * b + 3)
            st.last()
            st.done(dve.tensor_reduce(r_own, s_dve[:, :, 0:9], AX.X, ALU.add))
            st.done(dve.tensor_reduce(r_oth, s_dve[:, :, 9:NS], AX.X, ALU.add))
            st.last()
            st.done(dve.tensor_tensor(v3(s_tmp), tb(r_own), hb(C("is_own")), ALU.mult))
            st.done(dve.tensor_tensor(v3(s_tot), tb(r_oth), hb(C("is_oth")), ALU.mult))
            st.last()
            st.done(dve.tensor_tensor(s_tot, s_tot, s_tmp, ALU.add))
            st.last()
            at["tot"] = st.done(dve.tensor_tensor(s_tot, s_tot, s_all, ALU.add))
            prev = None
            for j in range(UNIQ + DIL):
                dve.wait_ge(v_in[j % 5], 32 * b + 16 * (j // 5) + 16)
                for i in range(1 if j < UNIQ else 2):
                    for h in range(HA):
                        w = s_dve[:, h, j + (DIL if i else 0):j + (DIL if i else 0) + 1]
                        u, v = u_sb[:, i, P * h:P * h + P], v_sb[:, j % 5, P * h:P * h + P]
                        if (j == 0 and i == 0) or (j == UNIQ and i == 1):
                            ins = dve.tensor_scalar(u, v, w, None, ALU.mult)
                        else:
                            st.wait(prev[i, h])
                            ins = dve.scalar_tensor_tensor(out=u, in0=v, scalar=w, in1=u, op0=ALU.mult, op1=ALU.add)
                        n = st.done(ins)
                        prev = prev or {}
                        prev[i, h] = n
                st.last()
                dve.sem_inc(v_used, 1)
            at["u"] = st.n
            assert st.n == DVE_B and at == AT, (st.n, at)

        dt_in = sem("decode_results_in")
        dt_div = sem("decode_divided")
        dt_tr = sem("decode_results_transposed")
        dt_hi = sem("decode_results_high")
        dt_lo = sem("decode_results_low")
        dt_out = sem("decode_den_stored")
        o_tok = v_new

        def dtail_sp(sp):
            sp.wait_ge(ob_done, 3 * TB + 1)
            with nc.allow_non_contiguous_dma(reason="384 denominators"):
                for h in range(HA):
                    sp.dma_start(den_d[h].rearrange("(b t) -> t b", t=TT), den_all[TT * h:TT * h + TT, :]).then_inc(dt_out, 16)
            sp.wait_ge(dt_out, 16 * HA)
            sp.wait_ge(ob_out, 16 * TB + 16)
            sp.dma_start(o_tok[0:TS, :], oa_d).then_inc(dt_in, 16)
            with nc.allow_non_contiguous_dma(reason="384 denominators"):
                sp.dma_start(den_tok[0:TS, :], den_d.rearrange("h c -> c h")).then_inc(dt_in, 16)

        def dtail_dve(dve):
            dve.wait_ge(dt_in, 32)
            dve.reciprocal(den_tok[0:TS, :], den_tok[0:TS, :]).then_inc(dt_div, 1)
            dve.wait_ge(dt_div, 1)
            o3 = o_tok[0:TS, :].rearrange("p (h d) -> p h d", h=HA)
            dve.tensor_tensor(o3, o3, den_tok[0:TS, :].unsqueeze(2).to_broadcast([TS, HA, HD]), ALU.mult).then_inc(dt_div, 1)
            dve.wait_ge(dt_hi, 1)
            dve.tensor_tensor(lo[:, 0:HA, TP:T], psum[:, 0, 0:HA * TS].rearrange("p (h t) -> p h t", h=HA),
                              hi[:, 0:HA, TP:T].bitcast(F32), ALU.subtract).then_inc(dt_lo, 1)

        def dtail_pe(pe):
            pe.wait_ge(dt_div, 2)
            pe.wait_ge(kT9_done, 2 * TB)
            for h in range(HA):
                mm = pe.transpose(psum[:, 0, TS * h:TS * h + TS], o_tok[0:TS, P * h:P * h + P], ident[0:TS, 0:TS])
            mm.then_inc(dt_tr, 1)

        def dtail_act(act):
            act.wait_ge(dt_tr, 1)
            act.activation(hi[:, 0:HA, TP:T], psum[:, 0, 0:HA * TS].rearrange("p (h t) -> p h t", h=HA), ACT.Copy).then_inc(dt_hi, 1)

        NU = HA * 4
        vp = area(4, DA, at=0)
        qk = area(2, 2, TP)
        pr = area(2, TP)
        pT = area(2, TP)
        mx = area(2)
        dn = area(2)
        pa_v = sem("prompt_values_in")
        pa_in = [sem(f"prompt_qk_in{i}") for i in range(2)]
        pa_s = sem("prompt_scores_done")
        pa_m = sem("prompt_max_done")
        pa_e = sem("prompt_exp_done")
        pa_n = sem("prompt_probs_done")
        pa_t = sem("prompt_probs_transposed")
        pa_c = sem("prompt_probs_copied")
        pa_o = sem("prompt_out_done")
        pa_hi = sem("prompt_out_high")
        pa_lo = sem("prompt_out_low")

        def pa_sp(sp):
            sp.wait_ge(dt_tr, 1)
            sp.dma_start(vp, pv.rearrange("(n p) c -> p n c", p=P)).then_inc(pa_v, 16)
            for h in range(HA):
                if h >= 2:
                    sp.wait_ge(pa_s, 4 * (h - 1))
                for i in range(2):
                    sp.dma_start(qk[:, h % 2, i, :], proj_m[:, HA * i + h, 0:TP]).then_inc(pa_in[h % 2], 16)

        def pa_pe(pe):
            def scores(u):
                h, i = divmod(u, 4)
                pe.wait_ge(pa_in[h % 2], 32 * (h // 2 + 1))
                if u >= 2:
                    pe.wait_ge(pa_m, 2 * (u - 1))
                pe.matmul(psum[:, 2 + u % 2, 0:P * (i + 1)], qk[:, h % 2, 0, P * i:P * i + P], qk[:, h % 2, 1, 0:P * (i + 1)],
                          start=True, stop=True).then_inc(pa_s, 1)

            def turn(u):
                i = u % 4
                pe.wait_ge(pa_n, 2 * u + 2)
                if u >= 2:
                    pe.wait_ge(pa_c, u - 1)
                for j in range(i + 1):
                    mm = pe.transpose(psum[:, 4 + u % 2, P * j:P * j + P], pr[:, u % 2, P * j:P * j + P], ident)
                mm.then_inc(pa_t, 1)

            def out(u):
                h, i = divmod(u, 4)
                pe.wait_ge(pa_c, u + 1)
                if u == 0:
                    pe.wait_ge(pa_v, 16)
                if u >= 2:
                    pe.wait_ge(pa_lo, u - 1)
                for j in range(i + 1):
                    mm = pe.matmul(psum[:, 6 + u % 2, 0:P], vp[:, j, P * h:P * h + P], pT[:, u % 2, P * j:P * j + P],
                                   start=j == 0, stop=j == i)
                mm.then_inc(pa_o, 1)

            for u in range(NU + 2):
                if u < NU:
                    scores(u)
                if 1 <= u <= NU:
                    turn(u - 1)
                if u >= 2:
                    out(u - 2)

        def pa_act(act):
            for u in range(NU + 2):
                if u < NU:
                    n = P * (u % 4 + 1)
                    act.wait_ge(pa_m, 2 * u + 2)
                    act.activation(pr[:, u % 2, 0:n], pr[:, u % 2, 0:n], ACT.Exp, bias=mx[:, u % 2:u % 2 + 1],
                                   accum_out=dn[:, u % 2:u % 2 + 1]).then_inc(pa_e, 1)
                if 1 <= u <= NU:
                    w = u - 1
                    n = P * (w % 4 + 1)
                    act.wait_ge(pa_t, w + 1)
                    if w >= 2:
                        act.wait_ge(pa_o, w - 1)
                    act.activation(pT[:, w % 2, 0:n], psum[:, 4 + w % 2, 0:n], ACT.Copy).then_inc(pa_c, 1)
                if u >= 2:
                    w = u - 2
                    h, i = divmod(w, 4)
                    act.wait_ge(pa_o, w + 1)
                    act.activation(hi[:, h, P * i:P * i + P], psum[:, 6 + w % 2, 0:P], ACT.Copy).then_inc(pa_hi, 1)

        def pa_dve(dve):
            for u in range(NU + 3):
                if u < NU:
                    n = P * (u % 4 + 1)
                    dve.wait_ge(pa_s, u + 1)
                    if u >= 2:
                        dve.wait_ge(pa_t, u - 1)
                    dve.tensor_tensor_reduce(pr[:, u % 2, 0:n], psum[:, 2 + u % 2, 0:n], C("mask_a")[:, TP - n:TP], SCALE_A, NEG,
                                             ALU.add, ALU.max, mx[:, u % 2:u % 2 + 1]).then_inc(pa_m, 1)
                    dve.wait_ge(pa_m, 2 * u + 1)
                    dve.tensor_scalar(mx[:, u % 2:u % 2 + 1], mx[:, u % 2:u % 2 + 1], -1.0, None, ALU.mult).then_inc(pa_m, 1)
                if 1 <= u <= NU:
                    w = u - 1
                    n = P * (w % 4 + 1)
                    dve.wait_ge(pa_e, w + 1)
                    dve.reciprocal(dn[:, w % 2:w % 2 + 1], dn[:, w % 2:w % 2 + 1]).then_inc(pa_n, 1)
                    dve.wait_ge(pa_n, 2 * w + 1)
                    dve.tensor_scalar(pr[:, w % 2, 0:n], pr[:, w % 2, 0:n], dn[:, w % 2:w % 2 + 1], None, ALU.mult).then_inc(pa_n, 1)
                if u >= 3:
                    w = u - 3
                    h, i = divmod(w, 4)
                    dve.wait_ge(pa_hi, w + 1)
                    dve.tensor_tensor(lo[:, h, P * i:P * i + P], psum[:, 6 + w % 2, 0:P],
                                      hi[:, h, P * i:P * i + P].bitcast(F32), ALU.subtract).then_inc(pa_lo, 1)

        UW = PBUF + TP
        us = TT + PBUF
        ub = area(NPOOL, UW, at=pool_at[0])
        ubs = area(NPOOL, TB, us)
        acc = area(2, UW)
        accs = area(2, TB, us)
        pooled = area(T)
        ptmp = area(T)
        wp = area(NPOOL, P)
        hist = area(DB)
        rows_out = area(2, DB)
        cnt_tmp = area(16)
        pl_in = sem("pool_inputs_in")
        pl_z = sem("pool_padding_zero")
        pl_hist = sem("pool_history_transposed")
        pl_hc = sem("pool_history_copied")
        pl_d = sem("pool_dve_steps")
        pl_mm = sem("pool_product_done")
        pl_sc = sem("pool_scaled")
        pl_hi = sem("pool_high")
        pl_lo = sem("pool_low")
        pl_ro = sem("pool_rows_transposed")
        pl_rc = sem("pool_rows_copied")
        pl_out = sem("pool_rows_stored")

        def pool_sp(sp):
            for g in range(NPOOL):
                sp.dma_start(ub[:, g, PBUF:UW], proj_m[:, OU // P + g, 0:TP]).then_inc(pl_in, 16)
                sp.dma_start(ptmp_s[:, g, :], proj_m[:, OU // P + g, TP:T]).then_inc(pl_in, 16)
            sp.dma_start(wp, w_pool[0].rearrange("g c d -> c g d")).then_inc(pl_in, 16)
            sp.dma_start(hist[0:TB * PBUF, :], state_pool[0].rearrange("b r c -> (b r) c")).then_inc(pl_in, 16)
            sp.dma_start(o_sp[0, :, 0:PBUF - TT, :], state_pool[0, :, TT:PBUF, :]).then_inc(pl_out, 16)
            sp.wait_ge(pl_rc, 2)
            sp.dma_start(o_pp[0, 0], rows_out[0:PBUF, 0, :]).then_inc(pl_out, 16)
            sp.dma_start(o_sp[0, :, PBUF - TT:PBUF, :], rows_out[0:TS, 1, :]).then_inc(pl_out, 16)

        ptmp_s = area(NPOOL, TS)
        POOL_IN = 16 * (2 * NPOOL + 2)

        def pool_pe(pe):
            pe.wait_ge(pl_in, POOL_IN)
            pe.wait_ge(dt_lo, 1)
            for g in range(NPOOL):
                mm = pe.transpose(psum[:, 1, P * g:P * g + TB * PBUF], hist[0:TB * PBUF, P * g:P * g + P], ident[0:TB * PBUF, 0:TB * PBUF])
            mm.then_inc(pl_hist, 1)
            pe.wait_ge(pa_m, 2 * NU)
            for g in range(NPOOL):
                mm = pe.transpose(psum[0:PBUF, 2, P * g:P * g + P], ub[:, g, TP:UW], ident)
            mm.then_inc(pl_ro, 1)
            for g in range(NPOOL):
                mm = pe.transpose(psum[0:TS, 3, P * g:P * g + P], ptmp_s[:, g, :], ident)
            mm.then_inc(pl_ro, 1)
            pe.wait_ge(pa_lo, NU)
            pe.wait_ge(pa_c, NU)
            for g in range(NPOOL):
                pe.wait_ge(pl_d, PD[g])
                for half in range(2):
                    if g >= 1:
                        pe.wait_ge(pl_sc, g)
                    mm = pe.matmul(psum[:, 4 + half, 0:HALF], wp[:, g, :], pooled[:, half * HALF:(half + 1) * HALF], start=True, stop=True)
                mm.then_inc(pl_mm, 1)

        PD = {}

        def pool_dve(dve):
            st = Steps(dve, pl_d)
            st.done(dve.memset(ub[:, :, 0:PBUF], 0.0))
            dve.wait_ge(pl_in, POOL_IN)
            for g in range(NPOOL):
                st.done(dve.tensor_copy(ubs[:, g, :, PBUF:us], ptmp_s[:, g, :].rearrange("p (b t) -> p b t", t=TT)))
            dve.wait_ge(pl_hist, 1)
            for g in range(NPOOL):
                st.done(dve.tensor_copy(ubs[:, g, :, 0:PBUF], psum[:, 1, P * g:P * g + TB * PBUF].rearrange("p (b r) -> p b r", r=PBUF)))
            for g in range(NPOOL):
                w = 2 << g
                a, s = ub[:, g, :], ubs[:, g]
                for lev in range(g + 1):
                    sh = 1 << lev
                    first = 2 * sh - 1
                    st.last()
                    na, ns = acc[:, lev % 2, :], accs[:, lev % 2]
                    st.done(dve.tensor_tensor(na[:, first:UW], a[:, first:UW], a[:, first - sh:UW - sh], ALU.add))
                    st.done(dve.tensor_tensor(ns[:, :, first:us], s[:, :, first:us], s[:, :, first - sh:us - sh], ALU.add))
                    a, s = na, ns
                st.last()
                if g >= 1:
                    dve.wait_ge(pl_mm, g)
                st.done(dve.tensor_tensor(cnt_tmp, a[:, PBUF:PBUF + 16], C("inv_count")[:, 16 * g:16 * g + 16], ALU.mult))
                st.done(dve.scalar_tensor_tensor(out=pooled[:, 16:TP], in0=a[:, PBUF + 16:UW], scalar=1.0 / w, in1=ub[:, g, PBUF + 16:UW],
                                                 op0=ALU.mult, op1=ALU.subtract))
                st.done(dve.scalar_tensor_tensor(out=pooled[:, TP:T].rearrange("p (b t) -> p b t", t=TT), in0=s[:, :, PBUF:us], scalar=1.0 / w,
                                                 in1=ubs[:, g, :, PBUF:us], op0=ALU.mult, op1=ALU.subtract))
                st.last()
                PD[g] = st.done(dve.tensor_tensor(pooled[:, 0:16], cnt_tmp, ub[:, g, PBUF:PBUF + 16], ALU.subtract))
                if g >= 1:
                    low(dve, g - 1)
            low(dve, NPOOL - 1)
            dve.wait_ge(pl_ro, 2)
            dve.tensor_copy(rows_out[0:PBUF, 0, :], psum[0:PBUF, 2, :]).then_inc(pl_rc, 1)
            dve.tensor_copy(rows_out[0:TS, 1, :], psum[0:TS, 3, :]).then_inc(pl_rc, 1)

        def low(dve, g):
            dve.wait_ge(pl_hi, g + 1)
            dve.tensor_tensor(lo[:, MIX_B + g, :], ptmp, hi[:, MIX_B + g, :].bitcast(F32), ALU.subtract).then_inc(pl_lo, 1)

        def pool_act(act):
            for g in range(NPOOL):
                act.wait_ge(pl_mm, g + 1)
                if g >= 1:
                    act.wait_ge(pl_lo, g)
                act.activation(ptmp.rearrange("p (a t) -> p a t", a=2), psum[:, 4:6, 0:HALF], ACT.Copy, scale=GS[:, g:g + 1]).then_inc(pl_sc, 1)
                act.wait_ge(pl_sc, g + 1)
                act.activation(hi[:, MIX_B + g, :], ptmp, ACT.Copy).then_inc(pl_hi, 1)

        rcf = area(6, P, at=0)
        qkv = area(12, P)
        az = area(CK)
        lg = area(CK)
        qd = area(HC, TB * (TS + TT), at=6 * P)
        zs = area(CK)
        gg = area(CK)
        eb = area(CK)
        enb = area(CK)
        ebd = area(CK)
        qe = area(CK)
        ke = area(CK)
        kd = area(CK)
        vt = area(CV)
        qeT = area(HC, P)
        keT = area(HC, P)
        am = area(HC, P)
        am_s = area(HC, TS)
        st_at = pool_at[0]
        S = area(5, CV)
        s0 = area(2, CV, at=st_at)
        sn = area(2, CV)
        kdm = area(2, CK)
        ebl = area(32)
        oc = area(CV)
        rs = area(HC)
        wg2 = area(CK)
        gjunk = g_sb[:, 0:CV]
        _e = 6 * P + 12 * P + 2 * CK + 2 * CK
        gjunk = g_sb[:, _e:_e + CV]
        _e = 6 * P + 12 * P
        out6 = g_sb[:, _e:_e + 6 * P].rearrange("p (m t) -> p m t", m=6)

        gl_w = sem("gla_gate_weights_in")
        gl_in = sem("gla_inputs_in")
        gl_z0 = sem("gla_zeros_done")
        gp = sem("gla_pe_steps")
        ga_ = sem("gla_act_steps")
        gv = sem("gla_dve_steps")
        s0_in = [sem(f"gla_state_in{i}") for i in range(2)]
        sn_out = [sem(f"gla_state_stored{i}") for i in range(2)]
        pg_out = sem("gla_prompt_state_stored")
        s_mix = sem("mix_split")

        NT = NTT
        GP, GA, GV = {}, {}, {}

        def gla_names():
            def number(names, into):
                n = 0
                for name in names:
                    n += 1
                    into[name] = n
            pe_n, act_n, dve_n = [], [], []
            for tt in range(NT):
                smp = tt == NT - 1
                pe_n += [(tt, "z"), (tt, "qk"), (tt, "v"), (tt, "sums"), (tt, "turn"), (tt, "scores")]
                if smp:
                    pe_n += [(tt, "intra")]
                    for b in range(TB):
                        pe_n += [(tt, "state", b), (tt, "inter", b)]
                else:
                    pe_n += [(tt, "state", c) for c in range(4)]
                    pe_n += [(tt, "out")]
                pe_n += [(tt, "oT")]
                act_n += [(tt, "e"), (tt, "l"), (tt, "v0"), (tt, "v1"), (tt, "eb"), (tt, "enb"), (tt, "ebd"), (tt, "ebl"), (tt, "qeT"), (tt, "keT")]
                act_n += [(tt, "sq", h) for h in range(HC)] + [(tt, "rms"), (tt, "silu"), (tt, "hi")]
                dve_n += [(tt, "zs"), (tt, "az"), (tt, "g"), (tt, "qe"), (tt, "ke"), (tt, "kd"), (tt, "mask")]
                if smp:
                    dve_n += [(tt, "qd")]
                    for b in range(TB):
                        dve_n += [(tt, "kdm", b)] + [(tt, "S", b, h) for h in range(HC)]
                else:
                    dve_n += [(tt, "S", c, h) for c in range(4) for h in range(HC)]
                dve_n += [(tt, "oc", 0), (tt, "oc", 1), (tt, "rs"), (tt, "on")] + [(tt, "out", m) for m in range(6)] + [(tt, "lo")]
            number(pe_n, GP)
            number(act_n, GA)
            number(dve_n, GV)

        gla_names()

        class Named:

            def __init__(self, eng, sem_, table_):
                self.eng, self.sem, self.table, self.n = eng, sem_, table_, 0

            def done(self, ins, *name):
                self.n += 1
                assert self.table[name] == self.n, (name, self.n, self.table[name])
                ins.then_inc(self.sem, 1)

            def after_pe(self, *name):
                self.eng.wait_ge(gp, GP[name])

            def after_act(self, *name):
                self.eng.wait_ge(ga_, GA[name])

            def after_dve(self, *name):
                self.eng.wait_ge(gv, GV[name])

        def sfx(tt):
            return "_s" if tt == NT - 1 else "_p"

        def gla_sp(sp):
            sp.wait_ge(pa_lo, NU)
            sp.wait_ge(pl_lo, NPOOL)
            sp.wait_ge(pl_out, 48)
            sp.dma_start(wg2[0:RANK, :], w_gate2[0]).then_inc(gl_w, 16)
            sp.dma_start(wg2[RANK:RANK + 1, :], b_gate).then_inc(gl_w, 16)
            for tt, (a, n) in enumerate(TILES):
                if tt:
                    sp.wait_ge(gv, GV[tt - 1, "lo"])
                sp.dma_start(rcf[:, :, 0:n], proj_m[:, ORC // P:OGA // P, a:a + n]).then_inc(gl_in, 16)
                sp.dma_start(qkv[:, :, 0:n], proj_m[:, OQC // P:ORC // P, a:a + n]).then_inc(gl_in, 16)
            sp.wait_ge(gv, GV[3, "S", 3, HC - 1])
            last = S[0:DK, 16 % 5, :].rearrange("p (h v) -> p h v", h=HC)
            sp.dma_start(o_pg[0, 0].rearrange("h k v -> k h v"), last).then_inc(pg_out, 16)
            sp.wait_ge(pg_out, 16)
            sp.wait_ge(gp, GP[3, "out"])
            for b in range(TB):
                if b >= 2:
                    sp.wait_ge(gv, GV[4, "S", b - 2, HC - 1])
                    sp.wait_ge(gp, GP[4, "inter", b - 2])
                sp.dma_start(s0[0:DK, b % 2, :].rearrange("p (h v) -> p h v", h=HC), state_gla[0, b].rearrange("h k v -> k h v")).then_inc(s0_in[b % 2], 16)
                if b:
                    gla_store(sp, b - 1)
            gla_store(sp, TB - 1)

        def gla_store(sp, b):
            sp.wait_ge(gv, GV[4, "S", b, HC - 1])
            sp.dma_start(o_sg[0, b].rearrange("h k v -> k h v"), sn[0:DK, b % 2, :].rearrange("p (h v) -> p h v", h=HC)).then_inc(sn_out[b % 2], 16)

        def gla_pe(pe):
            nd = Named(pe, gp, GP)
            pe.wait_ge(gl_w, 32)
            pe.wait_ge(s_gT, 1)
            pe.wait_ge(pl_lo, NPOOL)
            pe.wait_ge(pl_rc, 2)
            pe.wait_ge(pa_lo, NU)
            for tt, (a, n) in enumerate(TILES):
                smp = tt == NT - 1
                nch = TB if smp else 4
                if tt:
                    nd.after_dve(tt - 1, "out", 5)
                nd.done(pe.matmul(psum[0:n, 4, 0:CK], gaT[0:RANK + 1, a:a + n], wg2[0:RANK + 1, :], start=True, stop=True), tt, "z")
                pe.wait_ge(gl_in, 32 * tt + 32)
                for m in range(6):
                    mm = pe.transpose(psum[0:n, m // 3, P * (m % 3):P * (m % 3) + P], qkv[:, m, 0:n], ident)
                nd.done(mm, tt, "qk")
                for m in range(6):
                    mm = pe.transpose(psum[0:n, 2 + m // 4, P * (m % 4):P * (m % 4) + P], qkv[:, 6 + m, 0:n], ident)
                nd.done(mm, tt, "v")
                nd.after_dve(tt, "g")
                pe.matmul(psum[0:n, 5, 0:CK], C("upto" + sfx(tt), n), gg[0:n, :], start=True, stop=True)
                pe.matmul(psum[0:n, 6, 0:CK], C("after" + sfx(tt), n), gg[0:n, :], start=True, stop=True)
                for h in range(HC):
                    mm = pe.matmul(psum[0:DK, 7, nch * h:nch * h + nch], gg[0:n, DK * h:DK * h + DK], C("chunk" + sfx(tt), n), start=True, stop=True)
                nd.done(mm, tt, "sums")
                nd.after_dve(tt, "kd")
                for b, src in ((0, qe), (1, ke)):
                    for h in range(HC):
                        mm = pe.transpose(psum[0:DK, b, P * h:P * h + n], src[0:n, DK * h:DK * h + DK], ident[0:n, 0:n])
                nd.done(mm, tt, "turn")
                nd.after_act(tt, "keT")
                nd.after_act(tt, "v1")
                for h in range(HC):
                    mm = pe.matmul(psum[0:n, 2, P * h:P * h + n], keT[0:DK, h, 0:n], qeT[0:DK, h, 0:n], start=True, stop=True)
                nd.done(mm, tt, "scores")
                nd.after_act(tt, "ebl")
                ubanks = ((5, 6), (7, 0))

                def intra():
                    nd.after_dve(tt, "mask")
                    for h in range(HC):
                        mm = pe.matmul(psum[0:n, 3 + h // 2, DV * (h % 2):DV * (h % 2) + DV], (am_s if smp else am)[0:n, h, 0:n],
                                       vt[0:n, DV * h:DV * h + DV], start=h % 2 == 0, stop=False, skip_group_check=True)
                    return mm

                if smp:
                    nd.done(intra(), tt, "intra")
                    for b in range(TB):
                        nd.after_dve(tt, "kdm", b)
                        if b >= 2:
                            nd.after_dve(tt, "S", b - 2, HC - 1)
                        for h in range(HC):
                            mm = pe.matmul(psum[0:DK, ubanks[b % 2][h // 2], DV * (h % 2):DV * (h % 2) + DV],
                                           kdm[0:n, b % 2, DK * h:DK * h + DK], vt[0:n, DV * h:DV * h + DV], start=True, stop=True)
                        nd.done(mm, tt, "state", b)
                        nd.after_dve(tt, "qd")
                        pe.wait_ge(s0_in[b % 2], 16 * (b // 2) + 16)
                        for h in range(HC):
                            mm = pe.matmul(psum[0:n, 3 + h // 2, DV * (h % 2):DV * (h % 2) + DV], qd[0:DK, h, TS * b:TS * b + TS],
                                           s0[0:DK, b % 2, DV * h:DV * h + DV], start=False, stop=b == TB - 1, skip_group_check=True)
                        nd.done(mm, tt, "inter", b)
                else:
                    for c in range(4):
                        if c >= 2:
                            nd.after_dve(tt, "S", c - 2, HC - 1)
                        r = slice(CHUNK_P * c, CHUNK_P * c + CHUNK_P)
                        for h in range(HC):
                            mm = pe.matmul(psum[0:DK, ubanks[c % 2][h // 2], DV * (h % 2):DV * (h % 2) + DV],
                                           kd[r, DK * h:DK * h + DK], vt[r, DV * h:DV * h + DV], start=True, stop=True)
                        nd.done(mm, tt, "state", c)
                    intra()
                    for c in range(4):
                        if c:
                            nd.after_dve(tt, "S", c - 1, HC - 1)
                        r = slice(CHUNK_P * c, CHUNK_P * c + CHUNK_P)
                        for h in range(HC):
                            mm = pe.matmul(psum[r, 3 + h // 2, DV * (h % 2):DV * (h % 2) + DV], qeT[0:DK, h, r],
                                           S[0:DK, (4 * tt + c) % 5, DV * h:DV * h + DV], start=False, stop=True, skip_group_check=True)
                    nd.done(mm, tt, "out")
                nd.after_dve(tt, "on")
                for m in range(6):
                    mm = pe.transpose(psum[:, 1 + m // 4, P * (m % 4):P * (m % 4) + n], oc[0:n, P * m:P * m + P], ident[0:n, 0:n])
                nd.done(mm, tt, "oT")

        def gla_act(act):
            nd = Named(act, ga_, GA)
            for tt, (a, n) in enumerate(TILES):
                smp = tt == NT - 1
                nch = TB if smp else 4
                nd.after_dve(tt, "az")
                nd.done(act.activation(az[0:n, :], az[0:n, :], ACT.Exp, scale=-1.0), tt, "e")
                act.wait_ge(ga_, GA[tt, "e"])
                nd.done(act.activation(lg[0:n, :], az[0:n, :], ACT.Ln, bias=ones[0:n, 0:1]), tt, "l")
                nd.after_pe(tt, "v")
                nd.done(act.activation(vt[0:n, 0:512], psum[0:n, 2, :], ACT.Copy), tt, "v0")
                nd.done(act.activation(vt[0:n, 512:CV], psum[0:n, 3, 0:256], ACT.Copy), tt, "v1")
                nd.after_pe(tt, "sums")
                nd.done(act.activation(eb[0:n, :], psum[0:n, 5, 0:CK], ACT.Exp), tt, "eb")
                nd.done(act.activation(enb[0:n, :], psum[0:n, 5, 0:CK], ACT.Exp, scale=-1.0), tt, "enb")
                nd.done(act.activation(ebd[0:n, :], psum[0:n, 6, 0:CK], ACT.Exp), tt, "ebd")
                nd.done(act.activation(ebl[0:DK, 0:HC * nch], psum[0:DK, 7, 0:HC * nch], ACT.Exp), tt, "ebl")
                nd.after_pe(tt, "turn")
                v = lambda ap: ap.rearrange("p (h t) -> p h t", h=HC)[:, :, 0:n]
                nd.done(act.activation(qeT[0:DK, :, 0:n], v(psum[0:DK, 0, :]), ACT.Copy), tt, "qeT")
                nd.done(act.activation(keT[0:DK, :, 0:n], v(psum[0:DK, 1, :]), ACT.Copy), tt, "keT")
                nd.after_dve(tt, "oc", 1)
                for h in range(HC):
                    nd.done(act.activation(gjunk[0:n, DV * h:DV * h + DV], oc[0:n, DV * h:DV * h + DV], ACT.Square,
                                           accum_out=rs[0:n, h:h + 1]), tt, "sq", h)
                act.wait_ge(ga_, GA[tt, "sq", HC - 1])
                nd.done(act.activation(rs[0:n, :], rs[0:n, :], ACT.Sqrt, bias=eps_c[0:n], scale=1.0 / DV), tt, "rms")
                nd.done(act.activation(rcf[:, :, 0:n], rcf[:, :, 0:n], ACT.Silu), tt, "silu")
                nd.after_dve(tt, "out", 5)
                nd.done(act.activation(hi[:, MIX_C:KT, a:a + n], out6[:, :, 0:n], ACT.Copy), tt, "hi")

        def gla_dve(dve):
            nd = Named(dve, gv, GV)
            dve.wait_ge(pa_o, NU)
            dve.wait_ge(pl_mm, NPOOL)
            dve.wait_ge(pl_lo, NPOOL)
            dve.wait_ge(pl_out, 48)
            dve.wait_ge(pa_lo, NU)
            dve.memset(am, 0.0).then_inc(gl_z0, 1)
            dve.memset(am_s, 0.0).then_inc(gl_z0, 1)
            dve.memset(S[:, 0, :], 0.0).then_inc(gl_z0, 1)
            dve.wait_ge(gl_z0, 3)
            for tt, (a, n) in enumerate(TILES):
                smp = tt == NT - 1
                nd.after_pe(tt, "z")
                nd.done(dve.tensor_copy(zs[0:n, :], psum[0:n, 4, 0:CK]), tt, "zs")
                nd.after_dve(tt, "zs")
                nd.done(dve.scalar_tensor_tensor(out=az[0:n, :], in0=zs[0:n, :], scalar=-1.0, in1=zs[0:n, :], op0=ALU.mult, op1=ALU.max), tt, "az")
                nd.after_act(tt, "l")
                nd.done(dve.scalar_tensor_tensor(out=gg[0:n, :], in0=zs[0:n, :], scalar=0.0, in1=lg[0:n, :], op0=ALU.min, op1=ALU.subtract), tt, "g")
                nd.after_act(tt, "ebd")
                nd.after_pe(tt, "qk")
                nd.done(dve.scalar_tensor_tensor(out=qe[0:n, :], in0=psum[0:n, 0, 0:CK], scalar=SCALE_C, in1=eb[0:n, :], op0=ALU.mult, op1=ALU.mult), tt, "qe")
                nd.done(dve.tensor_tensor(ke[0:n, :], psum[0:n, 1, 0:CK], enb[0:n, :], ALU.mult), tt, "ke")
                nd.done(dve.tensor_tensor(kd[0:n, :], psum[0:n, 1, 0:CK], ebd[0:n, :], ALU.mult), tt, "kd")
                nd.after_pe(tt, "scores")
                m = C("upto" + sfx(tt), n).bitcast(I32)
                nd.done(dve.copy_predicated((am_s if smp else am)[0:n, :, 0:n], m.unsqueeze(1).to_broadcast([n, HC, n]),
                                            psum[0:n, 2, :].rearrange("p (h t) -> p h t", h=HC)[:, :, 0:n]), tt, "mask")
                ubanks = ((5, 6), (7, 0))
                if smp:
                    dve.memset(qd[0:DK], 0.0).then_inc(gl_z0, 1)
                    dve.wait_ge(gl_z0, 4)
                    nd.done(dve.tensor_copy(qd[0:DK].rearrange("p h (b s) -> p h b s", b=TB)[:, :, :, 0:TT],
                                            qeT[0:DK, :, 0:n].rearrange("p h (b t) -> p h b t", b=TB)), tt, "qd")
                    dve.wait_ge(pg_out, 16)
                for c in range(TB if smp else 4):
                    if smp:
                        nd.done(dve.tensor_scalar(kdm[0:n, c % 2, :], kd[0:n, :], C("chunk_s", n)[:, c:c + 1], GATE_NORM, ALU.mult, ALU.mult), tt, "kdm", c)
                        src, dst = s0[:, c % 2, :], sn[:, c % 2, :]
                        dve.wait_ge(s0_in[c % 2], 16 * (c // 2) + 16)
                        if c >= 2:
                            dve.wait_ge(sn_out[c % 2], 16 * (c // 2))
                        nch = TB
                    else:
                        src, dst = S[:, (4 * tt + c) % 5, :], S[:, (4 * tt + c + 1) % 5, :]
                        if c:
                            nd.after_dve(tt, "S", c - 1, HC - 1)
                        nch = 4
                    nd.after_pe(tt, "state", c)
                    for h in range(HC):
                        x = slice(DV * h, DV * h + DV)
                        nd.done(dve.scalar_tensor_tensor(out=dst[0:DK, x], in0=src[0:DK, x], scalar=ebl[0:DK, nch * h + c:nch * h + c + 1],
                                                         in1=psum[0:DK, ubanks[c % 2][h // 2], DV * (h % 2):DV * (h % 2) + DV],
                                                         op0=ALU.mult, op1=ALU.add), tt, "S", c, h)
                nd.after_pe(tt, *(("inter", TB - 1) if smp else ("out",)))
                for i in range(2):
                    nd.done(dve.tensor_copy(oc[0:n, 2 * DV * i:2 * DV * (i + 1)], psum[0:n, 3 + i, 0:2 * DV]), tt, "oc", i)
                nd.after_act(tt, "rms")
                nd.done(dve.reciprocal(rs[0:n, :], rs[0:n, :]), tt, "rs")
                nd.after_dve(tt, "rs")
                o4 = oc[0:n, :].rearrange("p (h v) -> p h v", h=HC)
                nd.done(dve.tensor_tensor(o4, o4, rs[0:n, :].unsqueeze(2).to_broadcast([n, HC, DV]), ALU.mult), tt, "on")
                nd.after_pe(tt, "oT")
                nd.after_act(tt, "silu")
                for m in range(6):
                    nd.done(dve.scalar_tensor_tensor(out=out6[:, m, 0:n], in0=psum[:, 1 + m // 4, P * (m % 4):P * (m % 4) + n], scalar=GN[:, m:m + 1],
                                                     in1=rcf[:, m, 0:n], op0=ALU.mult, op1=ALU.mult), tt, "out", m)
                nd.after_act(tt, "hi")
                nd.done(dve.tensor_tensor(lo[:, MIX_C:KT, a:a + n], out6[:, :, 0:n], hi[:, MIX_C:KT, a:a + n].bitcast(F32), ALU.subtract), tt, "lo")
            dve.wait_ge(gv, GV[NT - 1, "lo"])
            dve.sem_inc(s_mix, 1)

        @block.sync
        def _(sp):
            sp_start(sp)
            with sp.Fori(1, G_IN) as g:
                load_group(sp, g, cols(win_v, g))
            load_group(sp, G_IN, cols(wo_v, 0))
            kv_sp(sp)
            dec_sp(sp)
            with sp.Fori(0, TB) as b:
                dec_sp_b(sp, b)
            dtail_sp(sp)
            pa_sp(sp)
            pool_sp(sp)
            gla_sp(sp)
            sp.wait_ge(s_mix, 1)
            for i in range(2):
                sp.wait_ge(sn_out[i], 64)
            sp.wait_ge(xt_out, 16)
            sp.dma_start(xT.rearrange("p k t -> p (k t)"), xT_d).then_inc(xt_in, 16)
            with sp.Fori(1, G_O) as g:
                load_group(sp, G_IN + g, cols(wo_v, g))
            sp_ffn(sp)
            final_sp(sp)
            sp.wait_ge(kv_st[0], 32 * 3)
            sp.wait_ge(kv_st[1], 32 * 2)

        @block.gpsimd
        def _(pool):
            norm_pool(pool, 0)
            in_pool(pool)
            pool.wait_ge(kv_tr, 15)
            pool.wait_ge(kv_st[0], 32 * 3)
            pool.wait_ge(kv_st[1], 32 * 2)
            with pool.Fori(0, TB) as b:
                dec_pool_b(pool, b)
            norm_pool(pool, 1)

        @block.scalar
        def _(act):
            copies_in(act, xt_act, 0)
            act.wait_ge(xt_dve, 10)
            act.wait_ge(xt_act, 10)
            act.wait_ge(s_ready, 3)
            norm_act(act, 0)
            in_act(act)
            in_act_loop(act)
            kv_copies(act, kv_act, (0, 1))
            dec_act(act)
            with act.Fori(0, TB) as b:
                dec_act_b(act, b)
            dtail_act(act)
            pa_act(act)
            pool_act(act)
            gla_act(act)
            o_act(act)
            act.wait_ge(o_added, 2 + G_O)
            norm_act(act, 1)
            ffn_act(act)
            act.wait_ge(dn_added, 8 * NJ)
            final_act(act)

        @block.vector
        def _(dve):
            dve.memset(ones[:, :], 1.0).then_inc(s_ready, 1)
            dve.memset(misc[:, :], EPS).then_inc(s_ready, 1)
            dve.memset(gaT[:, :], 1.0).then_inc(s_ready, 1)
            for s_ in (k_used, v_used):
                dve.sem_inc(s_, 9)
            for s_ in (o_ready, k9_used, sl_done, ob_done):
                dve.sem_inc(s_, 1)
            dve.sem_inc(ob_out, 16)
            for s_ in (in_ev, o_added):
                dve.sem_inc(s_, 2)
            copies_in(dve, xt_dve, 1)
            dve.wait_ge(s_vt, 1)
            dve.tensor_copy(vecs[:, 0:58], psum[:, 4, 0:58]).then_inc(s_vc, 1)
            dve.wait_ge(s_vc, 1)
            norm_dve(dve, 0, G1)
            in_dve(dve)
            in_dve_loop(dve)
            kv_copies(dve, kv_dve, (2,))
            dve.wait_ge(dec_in, 48)
            dve.memset(s_max_w, 0.0).then_inc(dec_z, 1)
            dve.wait_ge(dec_z, 1)
            with dve.Fori(0, TB) as b:
                dec_dve_b(dve, b, DVE_B * b)
            dtail_dve(dve)
            pa_dve(dve)
            pool_dve(dve)
            gla_dve(dve)
            o_dve(dve)
            dve.wait_ge(o_added, 2 + G_O)
            norm_dve(dve, 1, G2)
            ffn_dve(dve)
            final_dve(dve)

        @block.tensor
        def _(pe):
            transposes_in(pe)
            pe.wait_ge(s_ready, 3)
            norm_pe(pe, 0)
            pe.wait_ge(s_vc, 1)
            in_pe(pe)
            kv_pe(pe)
            dec_pe(pe)
            with pe.Fori(0, TB) as b:
                dec_pe_scores(pe, b)
                dec_pe_max(pe, b)
                dec_pe_out(pe, b)
            dtail_pe(pe)
            pa_pe(pe)
            pool_pe(pe)
            gla_pe(pe)
            o_pe(pe)
            norm_pe(pe, 1)
            ffn_pe(pe)
            final_pe(pe)


_INS = ['x_prompt', 'x_sample', 'cache_win_k', 'cache_win_v', 'state_pool', 'state_gla', 'norm1_g', 'w_in', 'w_gate2', 'b_gate',
        'w_pool', 'pool_scale', 'gla_norm_g', 'w_o', 'norm2_g', 'w_ffn_gate', 'w_ffn_up', 'w_ffn_down', 'final_norm_g']
_OUTS = [(1, TP, D), (TB, TT, D), (1, 1, TP, HA, HD), (1, 1, TP, HA, HD), (1, 1, PBUF, DB), (1, 1, HC, DK, DV),
         (1, TB, TT, HA, HD), (1, TB, TT, HA, HD), (1, TB, PBUF, DB), (1, TB, HC, DK, DV)]


def kernel(**inputs):
    import numpy as _np
    import concourse.bacc as _bacc
    from concourse.bass_utils import run_bass_kernel_spmd as _run

    nc = _bacc.Bacc("TRN2", target_bir_lowering=False, num_devices=1)
    arrays, args = {}, []
    data = {name: _np.ascontiguousarray(inputs[name]) for name in _INS}
    data["table"] = table_columns()
    for name, a in data.items():
        arrays[f"in_{name}"] = a
        args.append(nc.dram_tensor(f"in_{name}", a.shape, mybir.dt.from_np(a.dtype), kind="ExternalInput").ap())
    for i, shape in enumerate(_OUTS):
        args.append(nc.dram_tensor(f"out_{i}", shape, F32, kind="ExternalOutput").ap())
    build(nc, *args)
    r = _run(nc, [arrays], core_ids=[0])
    return tuple(r.results[0][f"out_{i}"] for i in range(len(_OUTS)))
```

```python
import concourse.bass as bass
from concourse import mybir
from contextlib import ExitStack

F32 = mybir.dt.float32
F32R = mybir.dt.float32r
I32 = mybir.dt.int32
ALU = mybir.AluOpType
ACT = mybir.ActivationFunctionType
AX = mybir.AxisListType

P = 128
D = 2048
KT = D // P
TP, TB, TT = 512, 8, 8
TS = TB * TT
T = TP + TS
HALF = T // 2
NTT = -(-T // P)
TILES = [(n * P, min(P, T - n * P)) for n in range(-(-T // P))]
HA, HD = 6, 128
DA = HA * HD
HC, DK, DV = 4, 96, 192
CK, CV = HC * DK, HC * DV
DB, NPOOL, PBUF = 512, 4, 15
RANK = 16
PAST = 2048
FF = 5632
NJ = FF // 256
EPS = 1e-6
GATE_NORM = 16.0
OQ, OK, OV, OU = 0, DA, 2 * DA, 3 * DA
OQC = OU + DB
OKC = OQC + CK
OVC = OKC + CK
ORC = OVC + CV
OGA = ORC + CV
G_IN, G_O = OGA // 256, D // 256
MIX_B, MIX_C = DA // P, (DA + DB) // P
NEG = -1e30
LN2 = 0.6931471805599453
LN3 = 1.0986122886681098
UNIQ, DIL, LAST = 6, 3, 1
NBLK = UNIQ + DIL + LAST
SCALE_A = HD ** -0.5
SCALE_C = DK ** -0.5
CHUNK_P, CHUNK_S = 32, TT


def count_log(dist, window_ok=True):
    n = int(0 <= dist <= 128) + int(dist >= 0 and dist % 4 == 0 and dist <= 512) \
        + int(dist >= 0 and dist % 16 == 0 and dist <= 2048)
    return [NEG, 0.0, LN2, LN3][n]


TABLE = {}
_at = 0
for _name, _w in (("ident", P), ("mask_a", TP), ("log_dve", UNIQ + 2 * DIL), ("log_last", TT), ("log_new", TS),
                  ("neg_own", TT), ("neg_oth", TT), ("is_own", TT), ("is_oth", TT),
                  ("upto_p", P), ("after_p", P), ("chunk_p", P // CHUNK_P),
                  ("upto_s", TS), ("after_s", TS), ("chunk_s", TB), ("inv_count", NPOOL * 16)):
    TABLE[_name] = (_at, _w)
    _at += _w
TABLE_W = _at


def table_columns():
    import numpy as np
    t = np.zeros((P, TABLE_W), np.float32)

    def col(name):
        a, w = TABLE[name]
        return t[:, a:a + w]

    col("ident")[:] = np.eye(P)
    for p in range(P):
        for c in range(TP):
            col("mask_a")[p, c] = count_log(p + TP - P - c) / SCALE_A
        own, oth = p % TT, (p + 4) % TT
        for j in range(DIL):
            r = 1536 + P * j + p
            col("log_dve")[p, UNIQ + j] = count_log(PAST + own - r)
            col("log_dve")[p, UNIQ + DIL + j] = count_log(PAST + oth - r)
        for q in range(TT):
            col("log_last")[p, q] = count_log(PAST + q - (PAST - P + p))
            col("neg_own")[p, q] = 0.0 if q == own else NEG
            col("neg_oth")[p, q] = 0.0 if q == oth else NEG
            col("is_own")[p, q] = q == own
            col("is_oth")[p, q] = q == oth
    for r in range(TS):
        for c in range(TS):
            same = r // TT == c // TT
            col("log_new")[r, c] = count_log(c - r) if same else NEG
            col("upto_s")[r, c] = (same and r <= c) / GATE_NORM
            col("after_s")[r, c] = (same and r > c) / GATE_NORM
        col("chunk_s")[r, r // TT] = 1 / GATE_NORM
    for r in range(P):
        for c in range(P):
            same = r // CHUNK_P == c // CHUNK_P
            col("upto_p")[r, c] = (same and r <= c) / GATE_NORM
            col("after_p")[r, c] = (same and r > c) / GATE_NORM
        col("chunk_p")[r, r // CHUNK_P] = 1 / GATE_NORM
    for g in range(NPOOL):
        for c in range(16):
            col("inv_count")[:, 16 * g + c] = 1.0 / min(2 << g, c + 1)
    return t


class Steps:

    def __init__(self, eng, sem, base=0):
        self.eng, self.sem, self.base, self.n = eng, sem, base, 0

    def done(self, ins):
        ins.then_inc(self.sem, 1)
        self.n += 1
        return self.n

    def wait(self, n):
        self.eng.wait_ge(self.sem, self.base + n)

    def last(self):
        self.wait(self.n)


def build(nc, x_prompt, x_sample, cache_k, cache_v, state_pool, state_gla, norm1_g, w_in, w_gate2, b_gate,
          w_pool, pool_scale, gla_norm_g, w_o, norm2_g, w_gate, w_up, w_down, final_g, table,
          y_p, y_s, o_pk, o_pv, o_pp, o_pg, o_sk, o_sv, o_sp, o_sg):
    proj_d = nc.dram_tensor("proj_scratch", (OGA, T), F32).ap()
    xT_d = nc.dram_tensor("xT_scratch", (P, KT * T), F32).ap()
    q_d = nc.dram_tensor("q_scratch", (2, TS, DA), F32).ap()
    oa_d = nc.dram_tensor("decode_out_scratch", (TS, DA), F32).ap()
    den_d = nc.dram_tensor("decode_den_scratch", (HA, TS), F32).ap()
    proj_m = proj_d.rearrange("(m p) t -> p m t", p=P)

    x_d = [x_prompt[0, a:a + n, :] if a < TP else x_sample.rearrange("b t d -> (b t) d") for a, n in TILES]
    y_d = [y_p[0, a:a + n, :] if a < TP else y_s.rearrange("b t d -> (b t) d") for a, n in TILES]
    ck = cache_k[0].rearrange("b r h d -> b r (h d)")
    cv = cache_v[0].rearrange("b r h d -> b r (h d)")
    pk, pv = (a[0, 0].rearrange("r h d -> r (h d)") for a in (o_pk, o_pv))
    sk, sv = (a[0].rearrange("b t h d -> (b t) (h d)") for a in (o_sk, o_sv))
    kv_out = [[pk[a:a + n, :], pv[a:a + n, :]] if a < TP else [sk, sv] for a, n in TILES]

    ctx = ExitStack()
    with ctx:
        def sb(name, shape, dt=F32):
            return ctx.enter_context(nc.sbuf_tensor(name, shape, dt))[tuple(slice(None) for _ in shape)]

        def sem(name):
            return ctx.enter_context(nc.semaphore(name))

        act_r = sb("act_r", [P, 2, KT, T], F32R)
        w_hi = sb("w_hi", [P, 4, 1024], F32R)
        w_lo = sb("w_lo", [P, 4, 1024], F32R)
        w_raw = sb("w_raw", [P, 4, 1024])
        ffn_r = sb("ffn_r", [P, 2, 2, 2, T], F32R)
        tab = sb("tab", [P, TABLE_W])
        ones = sb("ones", [P, P])
        vecs = sb("vecs", [P, 64])
        misc = sb("misc", [P, 8])
        GW = 15200
        g_sb = sb("general", [P, GW])
        psum = ctx.enter_context(nc.psum_tensor("psum", [P, 8, 512], F32))
        pool_at = [0]

        def area(*shape, at=None):
            n = 1
            for s in shape:
                n *= s
            a = pool_at[0] if at is None else at
            pool_at[0] = a + n
            assert a + n <= GW, (a, n)
            v = g_sb[:, a:a + n]
            if len(shape) == 2:
                v = v.rearrange("p (a b) -> p a b", a=shape[0])
            if len(shape) == 3:
                v = v.rearrange("p (a b c) -> p a b c", a=shape[0], b=shape[1])
            return v

        def C(name, rows=P):
            a, w = TABLE[name]
            return tab[0:rows, a:a + w]

        ident = C("ident")
        eps_c = misc[:, 0:1]
        hi, lo = act_r[:, 0], act_r[:, 1]
        G1, G2, GF, GS, GN = (vecs[:, a:b] for a, b in ((0, 16), (16, 32), (32, 48), (48, 52), (52, 58)))

        xT = area(KT, T, at=0)
        tmp2 = area(2, T)
        rstd = area(T)
        xs = area(2, D)
        sil = area(2, T, at=KT * T + 3 * T)
        ftmp = area(2, T)
        stage_in = area(2, T, at=GW - 2 * T)

        s_const = sem("consts_in")
        s_ready = sem("consts_ready")
        x_in = [sem(f"x_in{i}") for i in range(2)]
        xt_tr = sem("xt_transposed")
        xt_act = sem("xt_copied_act")
        xt_dve = sem("xt_copied_dve")
        xt_out = sem("xt_spilled")
        xt_in = sem("xt_back")
        sq_done = sem("squares_done")
        acc_done = sem("squares_added")
        ss_done = sem("square_sums_done")
        rms_done = sem("rms_done")
        rstd_done = sem("rstd_done")
        h_done = sem("h_done")
        hhi_done = sem("h_high_done")
        hlo_done = sem("h_low_done")
        raw_in = [sem(f"raw_in{i}") for i in range(4)]
        whi_done = sem("w_high_done")
        wlo_done = sem("w_low_done")
        w_used = sem("w_chunk_used")
        in_ev = sem("in_group_copied")
        in_out = sem("in_group_stored")
        o_added = sem("o_group_added")
        sil_done = sem("silu_done")
        f_done = sem("gated_done")
        fhi_done = sem("gated_high_done")
        flo_done = sem("gated_low_done")
        dn_done = sem("down_pair_done")
        dn_added = sem("down_pair_added")
        y_tr = sem("y_transposed")
        y_ev = [sem("y_copied_act"), sem("y_copied_dve")]
        y_out = [sem(f"y_stored{i}") for i in range(2)]
        yn_done = sem("y_normalised")

        block = ctx.enter_context(nc.Block())

        win_v = w_in[0, :, 0:OGA].rearrange("(q k p) e -> q p k e", k=4, p=P)
        wo_v = w_o[0].rearrange("(q k p) e -> q p k e", k=4, p=P)
        wg_v = w_gate[0].rearrange("(q k p) e -> q p k e", k=4, p=P)
        wu_v = w_up[0].rearrange("(q k p) e -> q p k e", k=4, p=P)
        wd_v = w_down[0].rearrange("(j k p) e -> j p k e", k=2, p=P)

        def load_group(sp, g, src, qs=range(4)):
            for q in qs:
                if not (isinstance(g, int) and g == 0):
                    sp.wait_ge(wlo_done, 4 * (g - 1) + q + 1)
                k, e = (4, 256) if src(q).shape[1] == 4 else (2, 512)
                sp.dma_start(w_raw[:, q].rearrange("p (k e) -> p k e", k=k), src(q)).then_inc(raw_in[q], 16)

        def cols(v, g):
            return lambda q: v[q, :, :, bass.ds(g * 256, 256)]

        def down_src(j):
            return lambda q: wd_v[bass.ds(j, 1), :, :, 512 * q:512 * q + 512].rearrange("o p k e -> (o p) k e")

        def split_high(act, g, q):
            act.wait_ge(raw_in[q], 16 * (g + 1))
            if not (isinstance(g, int) and g == 0):
                act.wait_ge(w_used, 4 * (g - 1) + q + 1)
            act.activation(w_hi[:, q], w_raw[:, q], ACT.Copy).then_inc(whi_done, 1)

        def split_low(dve, g, q):
            dve.wait_ge(whi_done, 4 * g + q + 1)
            dve.tensor_tensor(w_lo[:, q], w_raw[:, q], w_hi[:, q].bitcast(F32), ALU.subtract).then_inc(wlo_done, 1)

        def product(pe, out2, wslot, c0, rhs_hi, rhs_lo, first, last):
            for w, r, n in ((w_hi, rhs_hi, 0), (w_hi, rhs_lo, 1), (w_lo, rhs_hi, 2)):
                for half in range(2):
                    mm = pe.matmul(psum[:, out2 + half, 0:HALF], w[:, wslot, c0:c0 + P],
                                   r[:, half * HALF:(half + 1) * HALF],
                                   start=first and n == 0, stop=last and n == 2)
            return mm

        def chunk(pe, g, bank, q, norm=None, half=None):
            pe.wait_ge(wlo_done, 4 * g + q + 1)
            for k in range(4) if half is None else range(2 * half, 2 * half + 2):
                kk = 4 * q + k
                if norm is not None:
                    pe.wait_ge(hlo_done, KT * norm + kk + 1)
                for m in range(2):
                    mm = product(pe, bank + 2 * m, q, 256 * k + P * m, hi[:, kk], lo[:, kk], kk == 0, kk == KT - 1)
            if half != 0:
                mm.then_inc(w_used, 1)

        def full_group(pe, g, bank, norm=None):
            for q in range(4):
                chunk(pe, g, bank, q, norm)

        def two(bank):
            return psum[:, bank:bank + 4, 0:HALF]

        def sp_start(sp):
            sp.dma_start(tab[:, :], table).then_inc(s_const, 16)
            for tt, (a, n) in enumerate(TILES):
                if tt >= 2:
                    sp.wait_ge(xt_tr, 4 * (tt - 1))
                sp.dma_start(xs[0:n, tt % 2, :], x_d[tt]).then_inc(x_in[tt % 2], 16)
                if tt == 0:
                    rows = vrow[0:16, :], vrow[16:32, :], vrow[32:48, :], vrow[48:52, :]
                    for dst, src in zip(rows, (norm1_g[0], norm2_g[0], final_g, pool_scale[0])):
                        sp.dma_start(dst, src.rearrange("(k p) -> k p", p=P)).then_inc(s_vec, 16)
                    gn = gla_norm_g[0:1, :]
                    for half in range(2):
                        r = 52 + 3 * half
                        for dst, src in ((vrow[r:r + 1, :], gn[:, 0:P]), (vrow[r + 1:r + 2, 0:DV - P], gn[:, P:DV]),
                                         (vrow[r + 1:r + 2, DV - P:P], gn[:, 0:2 * P - DV]),
                                         (vrow[r + 2:r + 3, :], gn[:, 2 * P - DV:DV])):
                            sp.dma_start(dst, src).then_inc(s_vec, 16)
                    load_group(sp, 0, cols(win_v, 0))
                    sp.dma_start(ga_raw, w_in[0, :, OGA:OGA + RANK].rearrange("(k p) e -> p k e", p=P)).then_inc(s_ga, 16)
            sp.wait_ge(xt_act, 10)
            sp.wait_ge(xt_dve, 10)
            sp.dma_start(xT_d, xT.rearrange("p k t -> p (k t)")).then_inc(xt_out, 16)

        s_vec = sem("gain_rows_in")
        s_vt = sem("gain_rows_transposed")
        s_vc = sem("gain_columns_done")
        s_ga = sem("gate_columns_in")
        s_gs = sem("gate_columns_split")
        s_gm = sem("gate_product_done")
        s_gT = sem("gate_inputs_done")
        vrow = sb("vrow", [64, P])
        ga_raw = sb("ga_raw", [P, KT, RANK])
        ga_hi = ffn_r[:, 0, 0, 0, 0:KT * RANK].rearrange("p (k e) -> p k e", k=KT)
        ga_lo = ffn_r[:, 0, 1, 0, 0:KT * RANK].rearrange("p (k e) -> p k e", k=KT)
        gaT = sb("gaT", [32, T])

        def transposes_in(pe):
            pe.wait_ge(s_const, 16)
            for tt, (a, n) in enumerate(TILES):
                pe.wait_ge(x_in[tt % 2], 16 * (tt // 2 + 1))
                for g in range(4):
                    u = 4 * tt + g
                    if u >= 8:
                        pe.wait_ge(xt_act if u % 2 == 0 else xt_dve, (u - 8) // 2 + 1)
                    for k in range(4):
                        mm = pe.transpose(psum[:, u % 8, P * k:P * k + n], xs[0:n, tt % 2, P * (4 * g + k):P * (4 * g + k + 1)],
                                          ident[0:n, 0:n])
                    mm.then_inc(xt_tr, 1)
            pe.wait_ge(s_vec, 16 * 12)
            pe.wait_ge(xt_act, 7)
            pe.transpose(psum[:, 4, 0:58], vrow[0:58, :], ident[0:58, 0:58]).then_inc(s_vt, 1)

        def copies_in(eng, own, parity):
            for u in range(parity, 4 * NTT, 2):
                tt, g = divmod(u, 4)
                a, n = TILES[tt]
                eng.wait_ge(xt_tr, u + 1)
                dst = xT[:, 4 * g:4 * g + 4, a:a + n]
                src = psum[:, u % 8, :].rearrange("p (k t) -> p k t", k=4)[:, :, 0:n]
                ins = eng.activation(dst, src, ACT.Copy) if own is xt_act else eng.tensor_copy(dst, src)
                ins.then_inc(own, 1)

        def norm_act(act, nrm, hi_out=True):
            for k in range(KT):
                n = KT * nrm + k
                if k >= 2:
                    act.wait_ge(acc_done, n - 1)
                elif nrm and k < 2:
                    act.wait_ge(hlo_done, KT * nrm)
                act.activation(tmp2[:, k % 2], xT[:, k], ACT.Square).then_inc(sq_done, 1)
            act.wait_ge(ss_done, nrm + 1)
            act.activation(rstd.rearrange("p (a t) -> p a t", a=2), psum[:, 0:2, 0:HALF], ACT.Sqrt, bias=eps_c, scale=1.0 / D).then_inc(rms_done, 1)
            if hi_out:
                for k in range(KT):
                    n = KT * nrm + k
                    act.wait_ge(h_done, n + 1)
                    act.activation(hi[:, k], tmp2[:, k % 2], ACT.Copy).then_inc(hhi_done, 1)

        def norm_dve(dve, nrm, gain, hi_out=True):
            for k in range(KT):
                n = KT * nrm + k
                dve.wait_ge(sq_done, n + 1)
                if k:
                    dve.wait_ge(acc_done, n)
                    ins = dve.tensor_tensor(rstd, rstd, tmp2[:, k % 2], ALU.add)
                else:
                    ins = dve.tensor_copy(rstd, tmp2[:, 0])
                ins.then_inc(acc_done, 1)
            dve.wait_ge(rms_done, nrm + 1)
            dve.reciprocal(rstd, rstd).then_inc(rstd_done, 1)
            dve.wait_ge(rstd_done, nrm + 1)
            if hi_out:
                for k in range(KT):
                    n = KT * nrm + k
                    if k >= 2:
                        dve.wait_ge(hlo_done, n - 1)
                    dve.scalar_tensor_tensor(out=tmp2[:, k % 2], in0=xT[:, k], scalar=gain[:, k:k + 1], in1=rstd,
                                             op0=ALU.mult, op1=ALU.mult).then_inc(h_done, 1)

        def norm_pool(pool, nrm):
            for k in range(KT):
                n = KT * nrm + k
                pool.wait_ge(hhi_done, n + 1)
                pool.tensor_tensor(lo[:, k], tmp2[:, k % 2], hi[:, k].bitcast(F32), ALU.subtract).then_inc(hlo_done, 1)

        def norm_pe(pe, nrm):
            pe.wait_ge(acc_done, KT * (nrm + 1))
            for half in range(2):
                mm = pe.matmul(psum[:, half, 0:HALF], ones[:, :], rstd[:, half * HALF:(half + 1) * HALF], start=True, stop=True)
            mm.then_inc(ss_done, 1)

        G_ROW, G_LAST = 11, G_IN - 1
        PAIRS = (G_ROW - 1) // 2

        def in_store(pool, g):
            pool.wait_ge(in_ev, 2 + g + 1)
            pool.dma_start(proj_m[:, bass.ds(2 * g, 2), :], stage_in).then_inc(in_out, 16)

        def in_copy(eng, g, bank):
            eng.wait_ge(w_used, 4 * g + 4)
            if not (isinstance(g, int) and g == 0):
                eng.wait_ge(in_out, 16 * g)
            dst = stage_in.rearrange("p m (a t) -> p (m a) t", a=2)
            ins = eng.tensor_copy(dst, two(bank)) if eng is nc.vector else eng.activation(dst, two(bank), ACT.Copy)
            ins.then_inc(in_ev, 1)

        def in_pe(pe):
            pe.wait_ge(rms_done, 1)
            for g in range(2):
                full_group(pe, g, 4 * g, norm=0)
            with pe.Fori(1, PAIRS) as i:
                for s in range(2):
                    pe.wait_ge(in_ev, 2 * i + s + 1)
                    full_group(pe, 2 * i + s, 4 * s)
            pe.wait_ge(in_ev, G_ROW)
            chunk(pe, G_ROW - 1, 0, 0)
            dec_pe(pe)
            for q in range(1, 4):
                chunk(pe, G_ROW - 1, 0, q)

        def ga_pe(pe):
            pe.wait_ge(s_gs, 2)
            pe.wait_ge(in_ev, 2 + G_IN)
            for k in range(KT):
                for w, r, n in ((ga_hi, hi, 0), (ga_hi, lo, 1), (ga_lo, hi, 2)):
                    for half in range(2):
                        mm = pe.matmul(psum[0:RANK, half, 0:HALF], w[:, k, :], r[:, k, half * HALF:(half + 1) * HALF],
                                       start=k == 0 and n == 0, stop=k == KT - 1 and n == 2)
            mm.then_inc(s_gm, 1)

        def in_act(act):
            for q in range(4):
                split_high(act, 0, q)
            act.wait_ge(s_ga, 16)
            act.activation(ga_hi, ga_raw, ACT.Copy).then_inc(s_gs, 1)

        def in_act_loop(act):
            with act.Fori(1, G_ROW) as g:
                for q in range(4):
                    split_high(act, g, q)
            dec_act_scale(act)
            split_high(act, G_ROW, 0)
            dec_act_copies(act)
            for q in range(1, 4):
                split_high(act, G_ROW, q)

        def ga_act(act):
            act.wait_ge(s_gm, 1)
            act.wait_ge(s_ready, 3)
            act.activation(gaT[0:RANK, :].rearrange("p (a t) -> p a t", a=2), psum[0:RANK, 0:2, 0:HALF], ACT.Copy).then_inc(s_gT, 1)

        def in_dve(dve):
            for q in range(4):
                split_low(dve, 0, q)
            dve.wait_ge(s_gs, 1)
            dve.tensor_tensor(ga_lo, ga_raw, ga_hi.bitcast(F32), ALU.subtract).then_inc(s_gs, 1)

        def in_dve_loop(dve):
            def pair(i):
                for s in range(2):
                    g = 2 * i + s
                    for q in range(4):
                        split_low(dve, g + 1, q)
                    in_copy(dve, g, 4 * s)

            pair(0)
            with dve.Fori(1, PAIRS) as i:
                pair(i)
            for q in range(4):
                split_low(dve, G_ROW, q)
            in_copy(dve, G_ROW - 1, 0)

        def in_pool(pool):
            with pool.Fori(0, G_ROW) as g:
                in_store(pool, g)

        def o_pe(pe):
            pe.wait_ge(s_mix, 1)
            with pe.Fori(0, G_O // 2) as i:
                for s in range(2):
                    pe.wait_ge(o_added, 2 * i + s + 1)
                    full_group(pe, G_IN + 2 * i + s, 4 * s)

        def o_dve(dve):
            dve.wait_ge(xt_in, 16)
            with dve.Fori(0, G_O // 2) as i:
                for s in range(2):
                    g = 2 * i + s
                    for q in range(4):
                        split_low(dve, G_IN + g + 1, q)
                    dve.wait_ge(w_used, 4 * (G_IN + g) + 4)
                    x2 = xT[:, bass.ds(2 * g, 2), :].rearrange("p m (a t) -> p (m a) t", a=2)
                    dve.tensor_tensor(x2, two(4 * s), x2, ALU.add).then_inc(o_added, 1)

        def o_act(act):
            with act.Fori(0, G_O) as g:
                for q in range(4):
                    split_high(act, G_IN + g + 1, q)

        def g_gate(j):
            return G_IN + G_O + (3 * j - 1 if not (isinstance(j, int) and j == 0) else 0)

        def g_up(j):
            return g_gate(j) + 1

        def g_down(j):
            return G_IN + G_O + 3 * (j + 1) + (1 if not (isinstance(j, int) and j == NJ - 1) else -1)

        def sp_ffn(sp):
            load_group(sp, g_gate(0), cols(wg_v, 0))
            load_group(sp, g_up(0), cols(wu_v, 0))
            with sp.Fori(1, NJ) as j:
                load_group(sp, g_gate(j), cols(wg_v, j))
                load_group(sp, g_up(j), cols(wu_v, j))
                load_group(sp, g_down(j - 1), down_src(j - 1))
            load_group(sp, g_down(NJ - 1), down_src(NJ - 1))

        def down_group(pe, j, s, last=False):
            g = g_down(j)
            fh, fl = ffn_r[:, s, 0], ffn_r[:, s, 1]
            pe.wait_ge(flo_done, 2 * j + 2)
            for q in range(4):
                pe.wait_ge(wlo_done, 4 * g + q + 1)
                for pair in range(2):
                    n = 2 * q + pair
                    if n >= 2 or last:
                        pe.wait_ge(dn_added, 8 * j + n - 1)
                    for k in range(2):
                        for m in range(2):
                            mm = product(pe, 4 * pair + 2 * m, q, 512 * k + 256 * pair + P * m, fh[:, k], fl[:, k], k == 0, k == 1)
                    mm.then_inc(dn_done if pair == 0 else w_used, 1)

        def gate_up(pe, j, norm=None):
            pe.wait_ge(dn_added, 8 * (j - 1) - 1) if not (isinstance(j, int) and j <= 1) else None
            full_group(pe, g_gate(j), 0, norm)
            pe.wait_ge(dn_added, 8 * (j - 1)) if not (isinstance(j, int) and j <= 1) else None
            full_group(pe, g_up(j), 4)

        def before_down(pe, j):
            pe.wait_ge(sil_done, 2 * j + 2)
            pe.wait_ge(f_done, 2 * j + 2)

        def ffn_pe(pe):
            gate_up(pe, 0, norm=1)
            gate_up(pe, 1)
            before_down(pe, 1)
            down_group(pe, 0, 0)
            with pe.Fori(0, NJ // 2 - 1) as i:
                for s in range(2):
                    gate_up(pe, 2 * i + 2 + s)
                    before_down(pe, 2 * i + 2 + s)
                    down_group(pe, 2 * i + 1 + s, 1 - s)
            down_group(pe, NJ - 1, 1, last=True)

        def act_silu(act, j):
            act.wait_ge(w_used, 4 * g_gate(j) + 4)
            for t in range(2):
                if not (isinstance(j, int) and j == 0):
                    act.wait_ge(f_done, 2 * (j - 1) + t + 1)
                act.activation(sil[:, t].rearrange("p (a t) -> p a t", a=2), psum[:, 2 * t:2 * t + 2, 0:HALF], ACT.Silu).then_inc(sil_done, 1)

        def act_fhigh(act, j, s):
            for t in range(2):
                act.wait_ge(f_done, 2 * j + t + 1)
                if not (isinstance(j, int) and j < 2):
                    act.wait_ge(w_used, 4 * g_down(j - 2) + 4)
                act.activation(ffn_r[:, s, 0, t], ftmp[:, t], ACT.Copy).then_inc(fhi_done, 1)

        def dve_gated(dve, j):
            dve.wait_ge(w_used, 4 * g_up(j) + 4)
            for t in range(2):
                dve.wait_ge(sil_done, 2 * j + t + 1)
                if not (isinstance(j, int) and j == 0):
                    dve.wait_ge(flo_done, 2 * (j - 1) + t + 1)
                dve.tensor_tensor(ftmp[:, t].rearrange("p (a t) -> p a t", a=2), psum[:, 4 + 2 * t:6 + 2 * t, 0:HALF],
                                  sil[:, t].rearrange("p (a t) -> p a t", a=2), ALU.mult).then_inc(f_done, 1)

        def dve_flow(dve, j, s):
            for t in range(2):
                dve.wait_ge(fhi_done, 2 * j + t + 1)
                dve.tensor_tensor(ffn_r[:, s, 1, t], ftmp[:, t], ffn_r[:, s, 0, t].bitcast(F32), ALU.subtract).then_inc(flo_done, 1)

        def dve_add_down(dve, j, n):
            if n % 2 == 0:
                dve.wait_ge(dn_done, 4 * j + n // 2 + 1)
            else:
                dve.wait_ge(w_used, 4 * g_down(j) + n // 2 + 1)
            if not (isinstance(j, int) and j == 0):
                dve.wait_ge(dn_added, 8 * (j - 1) + n + 1)
            x2 = xT[:, 2 * n:2 * n + 2, :].rearrange("p m (a t) -> p (m a) t", a=2)
            dve.tensor_tensor(x2, two(4 * (n % 2)), x2, ALU.add).then_inc(dn_added, 1)

        def ffn_act(act):
            def split(g, qs):
                for q in qs:
                    split_high(act, g, q)

            def step(j, s, nxt):
                split(g_up(j), range(3))
                act_silu(act, j)
                split(g_up(j), [3])
                split(g_down(j - 1), range(4))
                act_fhigh(act, j, s)
                split(nxt, range(4))

            split(g_up(0), range(3))
            act_silu(act, 0)
            split(g_up(0), [3])
            split(g_gate(1), range(4))
            act_fhigh(act, 0, 0)
            step(1, 1, g_gate(2))
            with act.Fori(0, NJ // 2 - 2) as i:
                for s in range(2):
                    step(2 * i + 2 + s, s, g_gate(2 * i + 3 + s))
            step(NJ - 2, 0, g_gate(NJ - 1))
            step(NJ - 1, 1, g_down(NJ - 1))

        def ffn_dve(dve):
            def split(g, qs):
                for q in qs:
                    split_low(dve, g, q)

            def step(j, s, nxt):
                split(g_up(j), range(4))
                split(g_down(j - 1), range(3))
                dve_gated(dve, j)
                split(g_down(j - 1), [3])
                dve_flow(dve, j, s)
                for q in range(4):
                    dve_add_down(dve, j - 1, 2 * q)
                    dve_add_down(dve, j - 1, 2 * q + 1)
                    split(nxt, [q])

            split(g_up(0), range(4))
            split(g_gate(1), range(3))
            dve_gated(dve, 0)
            split(g_gate(1), [3])
            dve_flow(dve, 0, 0)
            step(1, 1, g_gate(2))
            with dve.Fori(0, NJ // 2 - 2) as i:
                for s in range(2):
                    step(2 * i + 2 + s, s, g_gate(2 * i + 3 + s))
            step(NJ - 2, 0, g_gate(NJ - 1))
            step(NJ - 1, 1, g_down(NJ - 1))
            for n in range(8):
                dve_add_down(dve, NJ - 1, n)

        ysb = area(2, D, at=KT * T + 3 * T)

        def final_dve(dve):
            norm_dve(dve, 2, GF, hi_out=False)
            for k in range(KT):
                dve.scalar_tensor_tensor(out=xT[:, k], in0=xT[:, k], scalar=GF[:, k:k + 1], in1=rstd,
                                         op0=ALU.mult, op1=ALU.mult).then_inc(yn_done, 1)
            final_copies(dve, 1)

        def final_act(act):
            norm_act(act, 2, hi_out=False)
            final_copies(act, 0)

        def final_copies(eng, parity):
            for u in range(parity, 4 * NTT, 2):
                tt, g = divmod(u, 4)
                a, n = TILES[tt]
                eng.wait_ge(y_tr, u + 1)
                if tt >= 2:
                    eng.wait_ge(y_out[tt % 2], 16 * (tt // 2))
                dst, src = ysb[0:n, tt % 2, 512 * g:512 * g + 512], psum[0:n, u % 8, :]
                ins = eng.activation(dst, src, ACT.Copy) if parity == 0 else eng.tensor_copy(dst, src)
                ins.then_inc(y_ev[parity], 1)

        def final_pe(pe):
            norm_pe(pe, 2)
            for tt, (a, n) in enumerate(TILES):
                for g in range(4):
                    u = 4 * tt + g
                    pe.wait_ge(yn_done, 4 * g + 4)
                    if u >= 8:
                        pe.wait_ge(y_ev[u % 2], (u - 8) // 2 + 1)
                    for k in range(4):
                        mm = pe.transpose(psum[0:n, u % 8, P * k:P * k + P], xT[:, 4 * g + k, a:a + n], ident)
                    mm.then_inc(y_tr, 1)

        def final_sp(sp):
            for tt, (a, n) in enumerate(TILES):
                for par in range(2):
                    sp.wait_ge(y_ev[par], 2 * tt + 2)
                sp.dma_start(y_d[tt], ysb[0:n, tt % 2, :]).then_inc(y_out[tt % 2], 16)
            sp.wait_ge(y_out[0], 48)
            sp.wait_ge(y_out[1], 32)

        kvf = area(2, 2 * HA * P, at=0)
        kvt = area(2, 2 * DA)
        kv_in = [sem(f"kv_in{i}") for i in range(2)]
        kv_tr = sem("kv_transposed")
        kv_act = sem("kv_copied_act")
        kv_dve = sem("kv_copied_dve")
        kv_st = [sem(f"kv_stored{i}") for i in range(2)]

        def kv_sp(sp):
            sp.wait_ge(o_ready, TB + 1)
            def store(tt):
                a, n = TILES[tt]
                sp.wait_ge(kv_act, 2 * tt + 2)
                sp.wait_ge(kv_dve, tt + 1)
                for i in range(2):
                    sp.dma_start(kv_out[tt][i], kvt[0:n, tt % 2, DA * i:DA * i + DA]).then_inc(kv_st[tt % 2], 16)
            for tt, (a, n) in enumerate(TILES):
                if tt >= 2:
                    sp.wait_ge(kv_tr, 3 * (tt - 1))
                sp.dma_start(kvf[:, tt % 2, :].rearrange("p (m t) -> p m t", t=P)[:, :, 0:n],
                             proj_m[:, OK // P:OU // P, a:a + n]).then_inc(kv_in[tt % 2], 16)
                if tt:
                    store(tt - 1)
            store(NTT - 1)

        def kv_bank(tt, b):
            return 4 + (3 * tt + b) % 4

        def kv_pe(pe, tt):
            a, n = TILES[tt]
            pe.wait_ge(kv_in[tt % 2], 16 * (tt // 2 + 1))
            for b in range(3):
                u = 3 * tt + b - 4
                if u >= 0:
                    pe.wait_ge(*((kv_act, 2 * (u // 3) + u % 3 + 1) if u % 3 < 2 else (kv_dve, u // 3 + 1)))
                for k in range(4):
                    m = 4 * b + k
                    mm = pe.transpose(psum[0:n, kv_bank(tt, b), P * k:P * k + P], kvf[:, tt % 2, P * m:P * m + n], ident)
                mm.then_inc(kv_tr, 1)

        def kv_copies(eng, own, banks, tt):
            a, n = TILES[tt]
            for b in banks:
                eng.wait_ge(kv_tr, 3 * tt + b + 1)
                if tt >= 2:
                    eng.wait_ge(kv_st[tt % 2], 32 * (tt // 2))
                dst, src = kvt[0:n, tt % 2, 512 * b:512 * b + 512], psum[0:n, kv_bank(tt, b), :]
                ins = eng.activation(dst, src, ACT.Copy) if own is kv_act else eng.tensor_copy(dst, src)
                ins.then_inc(own, 1)

        def kv_stage_pe(pe):
            pe.wait_ge(in_ev, 2 + G_LAST)
            for q in range(4):
                chunk(pe, G_LAST, 0, q)
                if q == 0:
                    pe.wait_ge(ob_done, 3 * TB + 1)
                kv_pe(pe, q)
            kv_pe(pe, NTT - 1)

        def kv_stage_act(act):
            for q in range(4):
                split_high(act, G_IN, q)
                kv_copies(act, kv_act, (0, 1), q)
            kv_copies(act, kv_act, (0, 1), NTT - 1)

        def kv_stage_dve(dve):
            dve.wait_ge(wlo_done, 4 * G_IN)
            for q in range(4):
                split_low(dve, G_IN, q)
                kv_copies(dve, kv_dve, (2,), q)
            in_copy(dve, G_LAST, 0)
            kv_copies(dve, kv_dve, (2,), NTT - 1)

        NS = UNIQ + 2 * DIL
        k_sb = area(5, DA, at=0)
        v_sb = area(5, DA)
        q_rep = area(2, DA)
        u_sb = area(DA)
        kT9 = area(DA)
        q_tok = area(DA)
        v_new = area(DA)
        junk = u_sb
        o_sb = q_tok
        qf = area(HA, TS)
        kf = area(HA, TS)
        vf = kT9[:, 0:HA * TS].rearrange("p (h t) -> p h t", h=HA)
        qs = qf
        s_dve = area(HA, NS)
        s_all = area(HA * TT)
        s_new = area(HA * TT)
        p_exp = area(DIL, HA * TT)
        p_oth = area(DIL, HA * TT)
        s_max_w = area(P)
        s_max = s_max_w[:, 0:HA * TT]
        s_tmp = area(HA * TT)
        s_tot = area(HA * TT)
        r_own = area(HA)
        r_oth = area(HA)
        diag = area(HA * TT)
        m_col = area(1)
        den_all = area(TB)
        den_tok = area(HA)
        assert pool_at[0] <= GW - 2 * T

        dec_in = sem("decode_inputs_in")
        dec_z = sem("decode_padding_zero")
        dec_q = sem("decode_queries_ready")
        dec_qT = sem("decode_queries_transposed")
        dec_qt = sem("decode_queries_tokenmajor")
        dec_vT = sem("decode_values_transposed")
        dec_vt = sem("decode_values_tokenmajor")
        dec_qd = sem("decode_queries_in_dram")
        dec_qd2 = sem("decode_queries_swapped")
        q_in = sem("decode_query_rows_in")
        k_in = [sem(f"k_in{i}") for i in range(5)]
        v_in = [sem(f"v_in{i}") for i in range(5)]
        k_used = sem("k_block_used")
        k9_used = sem("k_last_block_used")
        v_used = sem("v_block_used")
        kT9_done = sem("k_last_block_copied")
        sl_done = sem("last_scores_done")
        dd = sem("decode_dve_steps")
        mT_done = sem("decode_max_transposed")
        mb_done = sem("decode_max_spread")
        e_done = sem("decode_exp_done")
        den_done = sem("decode_den_done")
        o_ready = sem("decode_out_done")
        ob_done = sem("decode_out_copied")
        ob_out = sem("decode_out_stored")
        DVE_B, AT = 65, {"max": 10, "diag": 12, "arg": 20, "tot": 26, "exp": 29, "u": 65}

        def hb(ap, rows=P):
            return ap.unsqueeze(1).to_broadcast([rows, HA, TT])

        def tb(ap, n=TT, rows=P):
            return ap.unsqueeze(2).to_broadcast([rows, HA, n])

        def v3(ap):
            return ap.rearrange("p (h t) -> p h t", h=HA)

        def dec_sp(sp):
            sp.wait_ge(in_out, 16 * (G_ROW - 2))
            for dst, m in ((qf, 0), (kf, HA), (vf, 2 * HA)):
                sp.dma_start(dst, proj_m[:, m:m + HA, TP:T]).then_inc(dec_in, 16)
            load_group(sp, G_ROW, cols(win_v, G_ROW))
            for j in (0, 1, 2, 3, 9):
                sp.dma_start(k_sb[:, k_slot(j)], cache_rows(ck, 0, j)).then_inc(k_in[k_slot(j)], 16)
            sp.dma_start(v_sb[:, 0], cache_rows(cv, 0, 0)).then_inc(v_in[0], 16)
            sp.wait_ge(dec_qt, 2)
            sp.dma_start(q_d[0], q_tok[0:TS, :]).then_inc(dec_qd, 16)
            sp.wait_ge(dec_qd, 16)
            for s in range(2):
                sp.dma_start(q_d[1].rearrange("(b s q) c -> s b q c", s=2, q=4)[1 - s],
                             q_d[0].rearrange("(b s q) c -> s b q c", s=2, q=4)[s]).then_inc(dec_qd2, 16)
            sp.wait_ge(dec_qd2, 32)
            query_rows(sp, 0)
            load_group(sp, G_ROW + 1, cols(win_v, G_ROW + 1), range(3))

        def query_rows(sp, b):
            for i in range(2):
                qv = q_d[i, bass.ds(b * TT, TT), :]
                src = bass.AP(qv.tensor, qv.offset, [[0, P // TT], [DA, TT], [1, DA]])
                sp.dma_start(q_rep[:, i], src).then_inc(q_in, 16)

        def k_slot(j):
            return 4 if j == 9 else j % 4

        def cache_rows(c, b, j):
            v = c[bass.ds(b, 1)].rearrange("o r c -> (o r) c")
            if j < UNIQ:
                return v[256 * j:256 * j + 256, :].rearrange("(n s) c -> n s c", s=16)[:, 0:TT, :]
            return v[1536 + P * (j - UNIQ):1536 + P * (j - UNIQ + 1), :]

        def dec_sp_b(sp, b, last=False):
            def weights(q, g, src):
                sp.wait_ge(wlo_done, 4 * (g - 1) + q + 1)
                sp.dma_start(w_raw[:, q].rearrange("p (k e) -> p k e", k=4), src(q)).then_inc(raw_in[q], 16)

            g = G_ROW + 2 + b
            src = cols(wo_v, 0) if last else cols(win_v, g)

            def keys(r, j):
                sp.dma_start(k_sb[:, k_slot(j)], cache_rows(ck, r, j)).then_inc(k_in[k_slot(j)], 16)

            def values(r, j):
                sp.dma_start(v_sb[:, j % 5], cache_rows(cv, r, j)).then_inc(v_in[j % 5], 16)

            for j in range(4, 8):
                sp.wait_ge(k_used, 9 * b + j - 3)
                keys(b, j)
            weights(3, g - 1, cols(win_v, g - 1))
            sp.wait_ge(o_ready, b + 1)
            for j in range(1, 5):
                values(b, j)
            sp.wait_ge(k_used, 9 * b + 5)
            keys(b, 8)
            weights(0, g, src)
            if not last:
                for j in range(1, 4):
                    sp.wait_ge(k_used, 9 * b + j + 5)
                    keys(b + 1, j)
                sp.wait_ge(k9_used, b + 1)
                keys(b + 1, 9)
                sp.wait_ge(k_used, 9 * b + 9)
                query_rows(sp, b + 1)
                keys(b + 1, 0)
            weights(1, g, src)
            for j in range(5, 9):
                sp.wait_ge(v_used, UNIQ * b + j - 4)
                values(b, j)
            sp.wait_ge(v_used, UNIQ * b + 5)
            values(b, 9)
            weights(2, g, src)
            if not last:
                sp.wait_ge(v_used, UNIQ * b + 6)
                values(b + 1, 0)
            if last:
                weights(3, g, src)

        def dec_pool_b(pool, b):
            g = G_ROW + b
            for q in range(4):
                split_low(pool, g + 1, q)
            in_store(pool, g)

        def dec_act_scale(act):
            act.wait_ge(dec_in, 48)
            act.activation(qs, qf, ACT.Copy, scale=SCALE_A).then_inc(dec_q, 1)

        def dec_act_copies(act):
            act.wait_ge(dec_qT, 2)
            act.activation(q_tok[0:TS, 0:512], psum[0:TS, 6, :], ACT.Copy).then_inc(dec_qt, 1)
            act.activation(q_tok[0:TS, 512:DA], psum[0:TS, 7, 0:256], ACT.Copy).then_inc(dec_qt, 1)
            act.wait_ge(dec_vT, 2)
            act.activation(v_new[0:TS, 0:512], psum[0:TS, 4, :], ACT.Copy).then_inc(dec_vt, 1)
            act.activation(v_new[0:TS, 512:DA], psum[0:TS, 5, 0:256], ACT.Copy).then_inc(dec_vt, 1)

        def dec_pe(pe):
            pe.wait_ge(in_ev, 2 + G_ROW - 1)
            pe.wait_ge(dec_q, 1)
            for bank, src, done in ((6, qs, dec_qT), (4, vf, dec_vT)):
                for h in range(HA):
                    mm = pe.transpose(psum[0:TS, bank + h // 4, P * (h % 4):P * (h % 4) + P], src[:, h, :], ident)
                    if h in (3, 5):
                        mm.then_inc(done, 1)

        def dec_pe_b(pe, b):
            g = G_ROW + b
            pe.wait_ge(in_ev, 2 + g)
            chunk(pe, g, 0, 0, half=0)
            pe.wait_ge(k_in[4], 16 * b + 16)
            pe.wait_ge(ob_done, 3 * b + 1)
            for h in range(HA):
                mm = pe.transpose(psum[:, 4 + h // 4, P * (h % 4):P * (h % 4) + P], k_sb[:, 4, P * h:P * h + P], ident)
            mm.then_inc(k9_used, 1)
            chunk(pe, g, 0, 0, half=1)
            pe.wait_ge(kT9_done, 2 * b + 2)
            for h in range(HA):
                q8 = qs[:, h, bass.ds(b * TT, TT)]
                pe.matmul(psum[:, 6, TT * h:TT * h + TT], kT9[:, P * h:P * h + P], q8, start=True, stop=True)
                mm = pe.matmul(psum[0:TS, 6, 64 + TT * h:64 + TT * h + TT], kf[:, h, :], q8, start=True, stop=True)
            mm.then_inc(sl_done, 1)
            chunk(pe, g, 0, 1, half=0)
            pe.wait_ge(dd, DVE_B * b + AT["max"])
            pe.transpose(psum[:, 7, 0:P], s_max_w, ident).then_inc(mT_done, 1)
            pe.wait_ge(dd, DVE_B * b + AT["diag"])
            pe.matmul(psum[:, 7, P:P + HA * TT], ones[0:HA * TT, :], diag[0:HA * TT, :], start=True, stop=True).then_inc(mb_done, 1)
            chunk(pe, g, 0, 1, half=1)
            chunk(pe, g, 0, 2)
            chunk(pe, g, 0, 3)
            pe.wait_ge(dd, DVE_B * b + AT["exp"])
            pe.matmul(psum[0:HA * TT, 7, 192:193], s_tot, ones[:, 0:1], start=True, stop=False)
            pe.matmul(psum[0:HA * TT, 7, 192:193], s_new[0:TS, :], ones[0:TS, 0:1], start=False, stop=True).then_inc(den_done, 1)
            def weighted(w, v, first=False):
                for h in range(HA):
                    pe.matmul(psum[0:TT, 4 + h // 4, P * (h % 4):P * (h % 4) + P], w[:, TT * h:TT * h + TT], v[:, P * h:P * h + P],
                              start=first and h % 4 == 0, stop=False, skip_group_check=True)

            weighted(s_new[0:TS, :], v_new[0:TS, :], first=True)
            for j in range(DIL):
                pe.wait_ge(v_in[1 + j], 32 * b + 32)
                weighted(p_exp[:, j], v_sb[:, 1 + j])
            pe.wait_ge(v_in[4], 32 * b + 32)
            weighted(s_all, v_sb[:, 4])
            pe.wait_ge(dd, DVE_B * b + AT["u"])
            for bank, h0, h1 in ((4, 0, 4), (5, 4, 6)):
                mm = pe.matmul(psum[0:TT, bank, 0:P * (h1 - h0)], C("is_own"), u_sb[:, P * h0:P * h1], start=False, stop=True,
                               skip_group_check=True)
            mm.then_inc(o_ready, 1)

        def dec_act_b(act, b):
            g = G_ROW + b
            act.wait_ge(k9_used, b + 1)
            act.wait_ge(sl_done, b + 1)
            act.activation(kT9[:, 0:512], psum[:, 4, :], ACT.Copy).then_inc(kT9_done, 1)
            act.activation(kT9[:, 512:DA], psum[:, 5, 0:256], ACT.Copy).then_inc(kT9_done, 1)
            split_high(act, g + 1, 0)
            act.wait_ge(dd, DVE_B * b + AT["arg"])
            act.activation(s_dve, s_dve, ACT.Exp).then_inc(e_done, 1)
            act.activation(s_all, s_all, ACT.Exp).then_inc(e_done, 1)
            act.activation(s_new[0:TS, :], s_new[0:TS, :], ACT.Exp).then_inc(e_done, 1)
            for q in range(1, 4):
                split_high(act, g + 1, q)
            in_copy(act, g, 0)
            act.wait_ge(den_done, b + 1)
            act.activation(den_all[0:HA * TT, bass.ds(b, 1)], psum[0:HA * TT, 7, 192:193], ACT.Copy).then_inc(ob_done, 1)
            act.wait_ge(o_ready, b + 2)
            act.wait_ge(ob_out, 16 * b + 16)
            act.activation(o_sb[0:TT, 0:512], psum[0:TT, 4, :], ACT.Copy).then_inc(ob_done, 1)
            act.activation(o_sb[0:TT, 512:DA], psum[0:TT, 5, 0:256], ACT.Copy).then_inc(ob_done, 1)
            act.wait_ge(ob_done, 3 * b + 4)
            act.dma_start(oa_d[bass.ds(b * TT, TT), :], o_sb[0:TT, :]).then_inc(ob_out, 16)

        def dec_dve_b(dve, b, base):
            st = Steps(dve, dd, base)
            at = {}
            dve.wait_ge(q_in, 32 * b + 32)
            junked = 0
            for j in range(UNIQ + DIL):
                s = k_slot(j)
                dve.wait_ge(k_in[s], (48 if s == 0 else 32) * b + 16 * (j // 4) + 16)
                for i in range(1 if j < UNIQ else 2):
                    col = j + (DIL if i else 0)
                    for h in range(HA):
                        kk = k_sb[:, s, P * h:P * h + P]
                        last = j < UNIQ or i == 1
                        if not last and j == UNIQ:
                            dve.wait_ge(o_ready, b + 1)
                        if not last and j > UNIQ:
                            dve.wait_ge(k_used, 9 * b + j)
                        ins = dve.tensor_tensor_reduce(kk if last else junk[:, P * h:P * h + P], kk, q_rep[:, i, P * h:P * h + P],
                                                       1.0, 0.0, ALU.mult, ALU.add, s_dve[:, h, col:col + 1])
                ins.then_inc(k_used, 1)
            dve.wait_ge(sl_done, b + 2)
            dve.wait_ge(k_used, 9 * b + 9)
            dve.wait_ge(o_ready, b + 1)
            st.done(dve.tensor_tensor(s_dve, s_dve, C("log_dve").unsqueeze(1).to_broadcast([P, HA, NS]), ALU.add))
            st.done(dve.tensor_tensor(v3(s_all), v3(psum[:, 6, 0:48]), hb(C("log_last")), ALU.add))
            st.done(dve.tensor_tensor(v3(s_new[0:TS, :]), v3(psum[0:TS, 6, 64:112]),
                                      hb(C("log_new", TS)[:, bass.ds(b * TT, TT)], TS), ALU.add))
            st.wait(1)
            st.done(dve.tensor_reduce(r_own, s_dve[:, :, 0:9], AX.X, ALU.max))
            st.done(dve.tensor_reduce(r_oth, s_dve[:, :, 9:NS], AX.X, ALU.max))
            st.last()
            st.done(dve.tensor_tensor(v3(s_max), tb(r_own), hb(C("neg_own")), ALU.add))
            st.done(dve.tensor_tensor(v3(s_tmp), tb(r_oth), hb(C("neg_oth")), ALU.add))
            st.last()
            st.done(dve.tensor_tensor(s_max, s_max, s_tmp, ALU.max))
            st.last()
            st.done(dve.tensor_tensor(s_max, s_max, s_all, ALU.max))
            st.last()
            at["max"] = st.done(dve.tensor_tensor(s_max[0:TS, :], s_max[0:TS, :], s_new[0:TS, :], ALU.max))
            dve.wait_ge(mT_done, b + 1)
            st.done(dve.tensor_reduce(m_col[0:48, :], psum[0:48, 7, 0:P], AX.X, ALU.max))
            st.last()
            at["diag"] = st.done(dve.tensor_scalar(diag[0:48, :], ident[0:48, 0:48], m_col[0:48, 0:1], -1.0, ALU.mult, ALU.mult))
            dve.wait_ge(mb_done, b + 1)
            mb = psum[:, 7, P:P + 48]
            st.done(dve.tensor_tensor(s_all, s_all, mb, ALU.add))
            st.done(dve.tensor_tensor(s_new[0:TS, :], s_new[0:TS, :], mb[0:TS, :], ALU.add))
            st.done(dve.tensor_tensor(v3(s_tmp), v3(mb), hb(C("is_own")), ALU.mult))
            st.done(dve.tensor_tensor(v3(s_tot), v3(mb), hb(C("is_oth")), ALU.mult))
            st.last()
            st.done(dve.tensor_reduce(r_own, v3(s_tmp), AX.X, ALU.add))
            st.done(dve.tensor_reduce(r_oth, v3(s_tot), AX.X, ALU.add))
            st.last()
            st.done(dve.tensor_tensor(s_dve[:, :, 0:9], s_dve[:, :, 0:9], tb(r_own, 9), ALU.add))
            at["arg"] = st.done(dve.tensor_tensor(s_dve[:, :, 9:NS], s_dve[:, :, 9:NS], tb(r_oth, 3), ALU.add))
            dve.wait_ge(e_done, 3 * b + 3)
            st.last()
            st.done(dve.tensor_reduce(r_own, s_dve[:, :, 0:9], AX.X, ALU.add))
            st.done(dve.tensor_reduce(r_oth, s_dve[:, :, 9:NS], AX.X, ALU.add))
            st.last()
            st.done(dve.tensor_tensor(v3(s_tmp), tb(r_own), hb(C("is_own")), ALU.mult))
            st.done(dve.tensor_tensor(v3(s_tot), tb(r_oth), hb(C("is_oth")), ALU.mult))
            st.last()
            st.done(dve.tensor_tensor(s_tot, s_tot, s_tmp, ALU.add))
            st.last()
            at["tot"] = st.done(dve.tensor_tensor(s_tot, s_tot, s_all, ALU.add))
            pj = lambda a: a.rearrange("p j (h t) -> p j h t", h=HA)
            wj = lambda a: a.rearrange("p h j -> p j h").unsqueeze(3).to_broadcast([P, DIL, HA, TT])
            sel = lambda name: C(name).unsqueeze(1).unsqueeze(1).to_broadcast([P, DIL, HA, TT])
            st.done(dve.tensor_tensor(pj(p_exp), wj(s_dve[:, :, UNIQ:UNIQ + DIL]), sel("is_own"), ALU.mult))
            st.done(dve.tensor_tensor(pj(p_oth), wj(s_dve[:, :, UNIQ + DIL:NS]), sel("is_oth"), ALU.mult))
            st.last()
            at["exp"] = st.done(dve.tensor_tensor(p_exp, p_exp, p_oth, ALU.add))
            prev = {}
            for j in range(UNIQ):
                dve.wait_ge(v_in[j % 5], 32 * b + 16 * (j // 5) + 16)
                for h in range(HA):
                    w = s_dve[:, h, j:j + 1]
                    u, v = u_sb[:, P * h:P * h + P], v_sb[:, j % 5, P * h:P * h + P]
                    if j == 0:
                        ins = dve.tensor_scalar(u, v, w, None, ALU.mult)
                    else:
                        st.wait(prev[h])
                        ins = dve.scalar_tensor_tensor(out=u, in0=v, scalar=w, in1=u, op0=ALU.mult, op1=ALU.add)
                    prev[h] = st.done(ins)
                st.last()
                dve.sem_inc(v_used, 1)
            at["u"] = st.n
            assert st.n == DVE_B and at == AT, (st.n, at)

        dt_in = sem("decode_results_in")
        dt_div = sem("decode_divided")
        dt_tr = sem("decode_results_transposed")
        dt_hi = sem("decode_results_high")
        dt_lo = sem("decode_results_low")
        dt_out = sem("decode_den_stored")
        o_tok = v_new

        def dtail_sp(sp, part):
            if part == 0:
                sp.wait_ge(ob_done, 3 * TB + 1)
                with nc.allow_non_contiguous_dma(reason="384 denominators"):
                    for h in range(HA):
                        sp.dma_start(den_d[h].rearrange("(b t) -> t b", t=TT), den_all[TT * h:TT * h + TT, :]).then_inc(dt_out, 16)
                return
            sp.wait_ge(dt_out, 16 * HA)
            sp.wait_ge(ob_out, 16 * TB + 16)
            sp.dma_start(o_tok[0:TS, :], oa_d).then_inc(dt_in, 16)
            with nc.allow_non_contiguous_dma(reason="384 denominators"):
                sp.dma_start(den_tok[0:TS, :], den_d.rearrange("h c -> c h")).then_inc(dt_in, 16)

        def dtail_dve(dve):
            dve.wait_ge(dt_in, 32)
            dve.reciprocal(den_tok[0:TS, :], den_tok[0:TS, :]).then_inc(dt_div, 1)
            dve.wait_ge(dt_div, 1)
            o3 = o_tok[0:TS, :].rearrange("p (h d) -> p h d", h=HA)
            dve.tensor_tensor(o3, o3, den_tok[0:TS, :].unsqueeze(2).to_broadcast([TS, HA, HD]), ALU.mult).then_inc(dt_div, 1)
            dve.wait_ge(dt_hi, 1)
            dve.tensor_tensor(lo[:, 0:HA, TP:T], psum[:, 4, 0:HA * TS].rearrange("p (h t) -> p h t", h=HA),
                              hi[:, 0:HA, TP:T].bitcast(F32), ALU.subtract).then_inc(dt_lo, 1)

        def dtail_pe(pe):
            pe.wait_ge(dt_div, 2)
            pe.wait_ge(kv_act, 9)
            for h in range(HA):
                mm = pe.transpose(psum[:, 4, TS * h:TS * h + TS], o_tok[0:TS, P * h:P * h + P], ident[0:TS, 0:TS])
            mm.then_inc(dt_tr, 1)

        def dtail_act(act):
            act.wait_ge(dt_tr, 1)
            act.activation(hi[:, 0:HA, TP:T], psum[:, 4, 0:HA * TS].rearrange("p (h t) -> p h t", h=HA), ACT.Copy).then_inc(dt_hi, 1)

        NU = HA * 4
        vp = area(4, DA, at=0)
        qk = area(2, 2, TP)
        pr = area(2, TP)
        pT = area(2, TP)
        mx = area(2)
        dn = area(2)
        pa_v = sem("prompt_values_in")
        pa_in = [sem(f"prompt_qk_in{i}") for i in range(2)]
        pa_s = sem("prompt_scores_done")
        pa_m = sem("prompt_max_done")
        pa_e = sem("prompt_exp_done")
        pa_n = sem("prompt_probs_done")
        pa_t = sem("prompt_probs_transposed")
        pa_c = sem("prompt_probs_copied")
        pa_o = sem("prompt_out_done")
        pa_hi = sem("prompt_out_high")
        pa_lo = sem("prompt_out_low")

        def pa_sp(sp):
            sp.wait_ge(dt_tr, 1)
            sp.wait_ge(kv_st[0], 32 * 3)
            sp.wait_ge(kv_st[1], 32 * 2)
            sp.wait_ge(in_out, 16 * G_IN)
            sp.dma_start(vp, pv.rearrange("(n p) c -> p n c", p=P)).then_inc(pa_v, 16)
            for h in range(HA):
                if h >= 2:
                    sp.wait_ge(pa_s, 4 * (h - 1))
                for i in range(2):
                    sp.dma_start(qk[:, h % 2, i, :], proj_m[:, HA * i + h, 0:TP]).then_inc(pa_in[h % 2], 16)

        def pa_pe(pe):
            def scores(u):
                h, i = divmod(u, 4)
                pe.wait_ge(pa_in[h % 2], 32 * (h // 2 + 1))
                if u >= 2:
                    pe.wait_ge(pa_m, 2 * (u - 1))
                pe.matmul(psum[:, 2 + u % 2, 0:P * (i + 1)], qk[:, h % 2, 0, P * i:P * i + P], qk[:, h % 2, 1, 0:P * (i + 1)],
                          start=True, stop=True).then_inc(pa_s, 1)

            def turn(u):
                i = u % 4
                pe.wait_ge(pa_n, 2 * u + 2)
                if u >= 2:
                    pe.wait_ge(pa_c, u - 1)
                for j in range(i + 1):
                    mm = pe.transpose(psum[:, 4 + u % 2, P * j:P * j + P], pr[:, u % 2, P * j:P * j + P], ident)
                mm.then_inc(pa_t, 1)

            def out(u):
                h, i = divmod(u, 4)
                pe.wait_ge(pa_c, u + 1)
                if u == 0:
                    pe.wait_ge(pa_v, 16)
                if u >= 2:
                    pe.wait_ge(pa_lo, u - 1)
                for j in range(i + 1):
                    mm = pe.matmul(psum[:, 6 + u % 2, 0:P], vp[:, j, P * h:P * h + P], pT[:, u % 2, P * j:P * j + P],
                                   start=j == 0, stop=j == i)
                mm.then_inc(pa_o, 1)

            pe.wait_ge(in_ev, 2 + G_IN)
            pe.wait_ge(dt_lo, 1)
            pe.wait_ge(kv_act, 10)
            pe.wait_ge(kv_dve, 5)
            for u in range(NU + 2):
                if u < NU:
                    scores(u)
                if 1 <= u <= NU:
                    turn(u - 1)
                if u >= 2:
                    out(u - 2)

        def pa_act(act):
            for u in range(NU + 2):
                if u < NU:
                    n = P * (u % 4 + 1)
                    act.wait_ge(pa_m, 2 * u + 2)
                    act.activation(pr[:, u % 2, 0:n], pr[:, u % 2, 0:n], ACT.Exp, bias=mx[:, u % 2:u % 2 + 1],
                                   accum_out=dn[:, u % 2:u % 2 + 1]).then_inc(pa_e, 1)
                if 1 <= u <= NU:
                    w = u - 1
                    n = P * (w % 4 + 1)
                    act.wait_ge(pa_t, w + 1)
                    if w >= 2:
                        act.wait_ge(pa_o, w - 1)
                    act.activation(pT[:, w % 2, 0:n], psum[:, 4 + w % 2, 0:n], ACT.Copy).then_inc(pa_c, 1)
                if u >= 2:
                    w = u - 2
                    h, i = divmod(w, 4)
                    act.wait_ge(pa_o, w + 1)
                    act.activation(hi[:, h, P * i:P * i + P], psum[:, 6 + w % 2, 0:P], ACT.Copy).then_inc(pa_hi, 1)

        def pa_dve(dve):
            for u in range(NU + 3):
                if u < NU:
                    n = P * (u % 4 + 1)
                    dve.wait_ge(pa_s, u + 1)
                    if u >= 2:
                        dve.wait_ge(pa_t, u - 1)
                    dve.tensor_tensor_reduce(pr[:, u % 2, 0:n], psum[:, 2 + u % 2, 0:n], C("mask_a")[:, TP - n:TP], SCALE_A, NEG,
                                             ALU.add, ALU.max, mx[:, u % 2:u % 2 + 1]).then_inc(pa_m, 1)
                    dve.wait_ge(pa_m, 2 * u + 1)
                    dve.tensor_scalar(mx[:, u % 2:u % 2 + 1], mx[:, u % 2:u % 2 + 1], -1.0, None, ALU.mult).then_inc(pa_m, 1)
                if 1 <= u <= NU:
                    w = u - 1
                    n = P * (w % 4 + 1)
                    dve.wait_ge(pa_e, w + 1)
                    dve.reciprocal(dn[:, w % 2:w % 2 + 1], dn[:, w % 2:w % 2 + 1]).then_inc(pa_n, 1)
                    dve.wait_ge(pa_n, 2 * w + 1)
                    dve.tensor_scalar(pr[:, w % 2, 0:n], pr[:, w % 2, 0:n], dn[:, w % 2:w % 2 + 1], None, ALU.mult).then_inc(pa_n, 1)
                if u >= 3:
                    w = u - 3
                    h, i = divmod(w, 4)
                    dve.wait_ge(pa_hi, w + 1)
                    dve.tensor_tensor(lo[:, h, P * i:P * i + P], psum[:, 6 + w % 2, 0:P],
                                      hi[:, h, P * i:P * i + P].bitcast(F32), ALU.subtract).then_inc(pa_lo, 1)

        UW = PBUF + TP
        us = TT + PBUF
        ub = area(NPOOL, UW, at=pool_at[0])
        ubs = area(NPOOL, TB, us)
        acc = area(2, UW)
        accs = area(2, TB, us)
        pooled = area(T)
        ptmp = area(T)
        wp = area(NPOOL, P)
        hist = area(DB)
        rows_out = area(2, DB)
        cnt_tmp = area(16)
        pl_in = sem("pool_inputs_in")
        pl_z = sem("pool_padding_zero")
        pl_hist = sem("pool_history_transposed")
        pl_hc = sem("pool_history_copied")
        pl_d = sem("pool_dve_steps")
        pl_mm = sem("pool_product_done")
        pl_sc = sem("pool_scaled")
        pl_hi = sem("pool_high")
        pl_lo = sem("pool_low")
        pl_ro = sem("pool_rows_transposed")
        pl_rc = sem("pool_rows_copied")
        pl_out = sem("pool_rows_stored")

        def pool_sp(sp):
            for g in range(NPOOL):
                sp.dma_start(ub[:, g, PBUF:UW], proj_m[:, OU // P + g, 0:TP]).then_inc(pl_in, 16)
                sp.dma_start(ptmp_s[:, g, :], proj_m[:, OU // P + g, TP:T]).then_inc(pl_in, 16)
            sp.dma_start(wp, w_pool[0].rearrange("g c d -> c g d")).then_inc(pl_in, 16)
            sp.dma_start(hist[0:TB * PBUF, :], state_pool[0].rearrange("b r c -> (b r) c")).then_inc(pl_in, 16)
            sp.dma_start(o_sp[0, :, 0:PBUF - TT, :], state_pool[0, :, TT:PBUF, :]).then_inc(pl_out, 16)
            sp.wait_ge(pl_rc, 2)
            sp.dma_start(o_pp[0, 0], rows_out[0:PBUF, 0, :]).then_inc(pl_out, 16)
            sp.dma_start(o_sp[0, :, PBUF - TT:PBUF, :], rows_out[0:TS, 1, :]).then_inc(pl_out, 16)

        ptmp_s = area(NPOOL, TS)
        POOL_IN = 16 * (2 * NPOOL + 2)

        def pool_pe(pe):
            pe.wait_ge(pl_in, POOL_IN)
            pe.wait_ge(s_gT, 1)
            for g in range(NPOOL):
                mm = pe.transpose(psum[:, 1, P * g:P * g + TB * PBUF], hist[0:TB * PBUF, P * g:P * g + P], ident[0:TB * PBUF, 0:TB * PBUF])
            mm.then_inc(pl_hist, 1)
            pe.wait_ge(pa_m, 2 * NU)
            for g in range(NPOOL):
                mm = pe.transpose(psum[0:PBUF, 2, P * g:P * g + P], ub[:, g, TP:UW], ident)
            mm.then_inc(pl_ro, 1)
            for g in range(NPOOL):
                mm = pe.transpose(psum[0:TS, 3, P * g:P * g + P], ptmp_s[:, g, :], ident)
            mm.then_inc(pl_ro, 1)
            pe.wait_ge(pa_lo, NU)
            pe.wait_ge(pa_c, NU)
            for g in range(NPOOL):
                pe.wait_ge(pl_d, PD[g])
                for half in range(2):
                    if g >= 1:
                        pe.wait_ge(pl_sc, g)
                    mm = pe.matmul(psum[:, 4 + half, 0:HALF], wp[:, g, :], pooled[:, half * HALF:(half + 1) * HALF], start=True, stop=True)
                mm.then_inc(pl_mm, 1)

        PD = {}

        def pool_dve(dve):
            st = Steps(dve, pl_d)
            st.done(dve.memset(ub[:, :, 0:PBUF], 0.0))
            dve.wait_ge(pl_in, POOL_IN)
            for g in range(NPOOL):
                st.done(dve.tensor_copy(ubs[:, g, :, PBUF:us], ptmp_s[:, g, :].rearrange("p (b t) -> p b t", t=TT)))
            dve.wait_ge(pl_hist, 1)
            for g in range(NPOOL):
                st.done(dve.tensor_copy(ubs[:, g, :, 0:PBUF], psum[:, 1, P * g:P * g + TB * PBUF].rearrange("p (b r) -> p b r", r=PBUF)))
            for g in range(NPOOL):
                w = 2 << g
                a, s = ub[:, g, :], ubs[:, g]
                for lev in range(g + 1):
                    sh = 1 << lev
                    first = 2 * sh - 1
                    st.last()
                    na, ns = acc[:, lev % 2, :], accs[:, lev % 2]
                    st.done(dve.tensor_tensor(na[:, first:UW], a[:, first:UW], a[:, first - sh:UW - sh], ALU.add))
                    st.done(dve.tensor_tensor(ns[:, :, first:us], s[:, :, first:us], s[:, :, first - sh:us - sh], ALU.add))
                    a, s = na, ns
                st.last()
                if g >= 1:
                    dve.wait_ge(pl_mm, g)
                st.done(dve.tensor_tensor(cnt_tmp, a[:, PBUF:PBUF + 16], C("inv_count")[:, 16 * g:16 * g + 16], ALU.mult))
                st.done(dve.scalar_tensor_tensor(out=pooled[:, 16:TP], in0=a[:, PBUF + 16:UW], scalar=1.0 / w, in1=ub[:, g, PBUF + 16:UW],
                                                 op0=ALU.mult, op1=ALU.subtract))
                st.done(dve.scalar_tensor_tensor(out=pooled[:, TP:T].rearrange("p (b t) -> p b t", t=TT), in0=s[:, :, PBUF:us], scalar=1.0 / w,
                                                 in1=ubs[:, g, :, PBUF:us], op0=ALU.mult, op1=ALU.subtract))
                st.last()
                PD[g] = st.done(dve.tensor_tensor(pooled[:, 0:16], cnt_tmp, ub[:, g, PBUF:PBUF + 16], ALU.subtract))
                if g >= 1:
                    low(dve, g - 1)
            low(dve, NPOOL - 1)
            dve.wait_ge(pl_ro, 2)
            dve.tensor_copy(rows_out[0:PBUF, 0, :], psum[0:PBUF, 2, :]).then_inc(pl_rc, 1)
            dve.tensor_copy(rows_out[0:TS, 1, :], psum[0:TS, 3, :]).then_inc(pl_rc, 1)

        def low(dve, g):
            dve.wait_ge(pl_hi, g + 1)
            dve.tensor_tensor(lo[:, MIX_B + g, :], ptmp, hi[:, MIX_B + g, :].bitcast(F32), ALU.subtract).then_inc(pl_lo, 1)

        def pool_act(act):
            for g in range(NPOOL):
                act.wait_ge(pl_mm, g + 1)
                if g >= 1:
                    act.wait_ge(pl_lo, g)
                act.activation(ptmp.rearrange("p (a t) -> p a t", a=2), psum[:, 4:6, 0:HALF], ACT.Copy, scale=GS[:, g:g + 1]).then_inc(pl_sc, 1)
                act.wait_ge(pl_sc, g + 1)
                act.activation(hi[:, MIX_B + g, :], ptmp, ACT.Copy).then_inc(pl_hi, 1)

        rcf = area(6, P, at=0)
        qkv = area(12, P)
        az = area(CK)
        lg = area(CK)
        qd = area(HC, TB * (TS + TT), at=6 * P)
        zs = area(CK)
        gg = area(CK)
        eb = area(CK)
        enb = area(CK)
        ebd = area(CK)
        qe = area(CK)
        ke = area(CK)
        kd = area(CK)
        vt = area(CV)
        qeT = area(HC, P)
        keT = area(HC, P)
        am = area(HC, P)
        am_s = area(HC, TS)
        st_at = pool_at[0]
        S = area(5, CV)
        s0 = area(2, CV, at=st_at)
        sn = area(2, CV)
        kdm = area(2, CK)
        ebl = area(32)
        oc = area(CV)
        rs = area(HC)
        wg2 = area(CK)
        gjunk = g_sb[:, 0:CV]
        _e = 6 * P + 12 * P + 2 * CK + 2 * CK
        gjunk = g_sb[:, _e:_e + CV]
        _e = 6 * P + 12 * P
        out6 = g_sb[:, _e:_e + 6 * P].rearrange("p (m t) -> p m t", m=6)

        gl_w = sem("gla_gate_weights_in")
        gl_in = sem("gla_inputs_in")
        gl_z0 = sem("gla_zeros_done")
        gp = sem("gla_pe_steps")
        ga_ = sem("gla_act_steps")
        gv = sem("gla_dve_steps")
        s0_in = [sem(f"gla_state_in{i}") for i in range(2)]
        sn_out = [sem(f"gla_state_stored{i}") for i in range(2)]
        pg_out = sem("gla_prompt_state_stored")
        s_mix = sem("mix_split")

        NT = NTT
        GP, GA, GV = {}, {}, {}

        def gla_names():
            def number(names, into):
                n = 0
                for name in names:
                    n += 1
                    into[name] = n
            pe_n, act_n, dve_n = [], [], []
            for tt in range(NT):
                smp = tt == NT - 1
                pe_n += [(tt, "z"), (tt, "qk"), (tt, "v"), (tt, "sums"), (tt, "turn"), (tt, "scores")]
                if smp:
                    pe_n += [(tt, "intra")]
                    for b in range(TB):
                        pe_n += [(tt, "state", b), (tt, "inter", b)]
                else:
                    pe_n += [(tt, "state", c) for c in range(4)]
                    pe_n += [(tt, "out")]
                pe_n += [(tt, "oT")]
                act_n += [(tt, "e"), (tt, "l"), (tt, "v0"), (tt, "v1"), (tt, "eb"), (tt, "enb"), (tt, "ebd"), (tt, "ebl"), (tt, "qeT"), (tt, "keT")]
                act_n += [(tt, "sq", h) for h in range(HC)] + [(tt, "rms"), (tt, "silu"), (tt, "hi")]
                dve_n += [(tt, "zs"), (tt, "az"), (tt, "g"), (tt, "qe"), (tt, "ke"), (tt, "kd"), (tt, "mask")]
                if smp:
                    dve_n += [(tt, "qd")]
                    for b in range(TB):
                        dve_n += [(tt, "kdm", b)] + [(tt, "S", b, h) for h in range(HC)]
                else:
                    dve_n += [(tt, "S", c, h) for c in range(4) for h in range(HC)]
                dve_n += [(tt, "oc", 0), (tt, "oc", 1), (tt, "rs"), (tt, "on")] + [(tt, "out", m) for m in range(6)] + [(tt, "lo")]
            number(pe_n, GP)
            number(act_n, GA)
            number(dve_n, GV)

        gla_names()

        class Named:

            def __init__(self, eng, sem_, table_):
                self.eng, self.sem, self.table, self.n = eng, sem_, table_, 0

            def done(self, ins, *name):
                self.n += 1
                assert self.table[name] == self.n, (name, self.n, self.table[name])
                ins.then_inc(self.sem, 1)

            def after_pe(self, *name):
                self.eng.wait_ge(gp, GP[name])

            def after_act(self, *name):
                self.eng.wait_ge(ga_, GA[name])

            def after_dve(self, *name):
                self.eng.wait_ge(gv, GV[name])

        def sfx(tt):
            return "_s" if tt == NT - 1 else "_p"

        def gla_sp(sp):
            sp.wait_ge(pa_lo, NU)
            sp.wait_ge(pl_lo, NPOOL)
            sp.wait_ge(pl_out, 48)
            sp.dma_start(wg2[0:RANK, :], w_gate2[0]).then_inc(gl_w, 16)
            sp.dma_start(wg2[RANK:RANK + 1, :], b_gate).then_inc(gl_w, 16)
            for tt, (a, n) in enumerate(TILES):
                if tt:
                    sp.wait_ge(gv, GV[tt - 1, "lo"])
                sp.dma_start(rcf[:, :, 0:n], proj_m[:, ORC // P:OGA // P, a:a + n]).then_inc(gl_in, 16)
                sp.dma_start(qkv[:, :, 0:n], proj_m[:, OQC // P:ORC // P, a:a + n]).then_inc(gl_in, 16)
            sp.wait_ge(gv, GV[3, "S", 3, HC - 1])
            last = S[0:DK, 16 % 5, :].rearrange("p (h v) -> p h v", h=HC)
            sp.dma_start(o_pg[0, 0].rearrange("h k v -> k h v"), last).then_inc(pg_out, 16)
            sp.wait_ge(pg_out, 16)
            sp.wait_ge(gp, GP[3, "out"])
            for b in range(TB):
                if b >= 2:
                    sp.wait_ge(gv, GV[4, "S", b - 2, HC - 1])
                    sp.wait_ge(gp, GP[4, "inter", b - 2])
                sp.dma_start(s0[0:DK, b % 2, :].rearrange("p (h v) -> p h v", h=HC), state_gla[0, b].rearrange("h k v -> k h v")).then_inc(s0_in[b % 2], 16)
                if b:
                    gla_store(sp, b - 1)
            gla_store(sp, TB - 1)

        def gla_store(sp, b):
            sp.wait_ge(gv, GV[4, "S", b, HC - 1])
            sp.dma_start(o_sg[0, b].rearrange("h k v -> k h v"), sn[0:DK, b % 2, :].rearrange("p (h v) -> p h v", h=HC)).then_inc(sn_out[b % 2], 16)

        def gla_pe(pe):
            nd = Named(pe, gp, GP)
            pe.wait_ge(gl_w, 32)
            pe.wait_ge(s_gT, 1)
            pe.wait_ge(pl_lo, NPOOL)
            pe.wait_ge(pl_rc, 2)
            pe.wait_ge(pa_lo, NU)
            for tt, (a, n) in enumerate(TILES):
                smp = tt == NT - 1
                nch = TB if smp else 4
                if tt:
                    nd.after_dve(tt - 1, "out", 5)
                nd.done(pe.matmul(psum[0:n, 4, 0:CK], gaT[0:RANK + 1, a:a + n], wg2[0:RANK + 1, :], start=True, stop=True), tt, "z")
                pe.wait_ge(gl_in, 32 * tt + 32)
                for m in range(6):
                    mm = pe.transpose(psum[0:n, m // 3, P * (m % 3):P * (m % 3) + P], qkv[:, m, 0:n], ident)
                nd.done(mm, tt, "qk")
                for m in range(6):
                    mm = pe.transpose(psum[0:n, 2 + m // 4, P * (m % 4):P * (m % 4) + P], qkv[:, 6 + m, 0:n], ident)
                nd.done(mm, tt, "v")
                nd.after_dve(tt, "g")
                pe.matmul(psum[0:n, 5, 0:CK], C("upto" + sfx(tt), n), gg[0:n, :], start=True, stop=True)
                pe.matmul(psum[0:n, 6, 0:CK], C("after" + sfx(tt), n), gg[0:n, :], start=True, stop=True)
                for h in range(HC):
                    mm = pe.matmul(psum[0:DK, 7, nch * h:nch * h + nch], gg[0:n, DK * h:DK * h + DK], C("chunk" + sfx(tt), n), start=True, stop=True)
                nd.done(mm, tt, "sums")
                nd.after_dve(tt, "kd")
                for b, src in ((0, qe), (1, ke)):
                    for h in range(HC):
                        mm = pe.transpose(psum[0:DK, b, P * h:P * h + n], src[0:n, DK * h:DK * h + DK], ident[0:n, 0:n])
                nd.done(mm, tt, "turn")
                nd.after_act(tt, "keT")
                nd.after_act(tt, "v1")
                for h in range(HC):
                    mm = pe.matmul(psum[0:n, 2, P * h:P * h + n], keT[0:DK, h, 0:n], qeT[0:DK, h, 0:n], start=True, stop=True)
                nd.done(mm, tt, "scores")
                nd.after_act(tt, "ebl")
                ubanks = ((5, 6), (7, 0))

                def intra():
                    nd.after_dve(tt, "mask")
                    for h in range(HC):
                        mm = pe.matmul(psum[0:n, 3 + h // 2, DV * (h % 2):DV * (h % 2) + DV], (am_s if smp else am)[0:n, h, 0:n],
                                       vt[0:n, DV * h:DV * h + DV], start=h % 2 == 0, stop=False, skip_group_check=True)
                    return mm

                if smp:
                    nd.done(intra(), tt, "intra")
                    for b in range(TB):
                        nd.after_dve(tt, "kdm", b)
                        if b >= 2:
                            nd.after_dve(tt, "S", b - 2, HC - 1)
                        for h in range(HC):
                            mm = pe.matmul(psum[0:DK, ubanks[b % 2][h // 2], DV * (h % 2):DV * (h % 2) + DV],
                                           kdm[0:n, b % 2, DK * h:DK * h + DK], vt[0:n, DV * h:DV * h + DV], start=True, stop=True)
                        nd.done(mm, tt, "state", b)
                        nd.after_dve(tt, "qd")
                        pe.wait_ge(s0_in[b % 2], 16 * (b // 2) + 16)
                        for h in range(HC):
                            mm = pe.matmul(psum[0:n, 3 + h // 2, DV * (h % 2):DV * (h % 2) + DV], qd[0:DK, h, TS * b:TS * b + TS],
                                           s0[0:DK, b % 2, DV * h:DV * h + DV], start=False, stop=b == TB - 1, skip_group_check=True)
                        nd.done(mm, tt, "inter", b)
                else:
                    for c in range(4):
                        if c >= 2:
                            nd.after_dve(tt, "S", c - 2, HC - 1)
                        r = slice(CHUNK_P * c, CHUNK_P * c + CHUNK_P)
                        for h in range(HC):
                            mm = pe.matmul(psum[0:DK, ubanks[c % 2][h // 2], DV * (h % 2):DV * (h % 2) + DV],
                                           kd[r, DK * h:DK * h + DK], vt[r, DV * h:DV * h + DV], start=True, stop=True)
                        nd.done(mm, tt, "state", c)
                    intra()
                    for c in range(4):
                        if c:
                            nd.after_dve(tt, "S", c - 1, HC - 1)
                        r = slice(CHUNK_P * c, CHUNK_P * c + CHUNK_P)
                        for h in range(HC):
                            mm = pe.matmul(psum[r, 3 + h // 2, DV * (h % 2):DV * (h % 2) + DV], qeT[0:DK, h, r],
                                           S[0:DK, (4 * tt + c) % 5, DV * h:DV * h + DV], start=False, stop=True, skip_group_check=True)
                    nd.done(mm, tt, "out")
                nd.after_dve(tt, "on")
                for m in range(6):
                    mm = pe.transpose(psum[:, 1 + m // 4, P * (m % 4):P * (m % 4) + n], oc[0:n, P * m:P * m + P], ident[0:n, 0:n])
                nd.done(mm, tt, "oT")

        def gla_act(act):
            nd = Named(act, ga_, GA)
            for tt, (a, n) in enumerate(TILES):
                smp = tt == NT - 1
                nch = TB if smp else 4
                nd.after_dve(tt, "az")
                nd.done(act.activation(az[0:n, :], az[0:n, :], ACT.Exp, scale=-1.0), tt, "e")
                act.wait_ge(ga_, GA[tt, "e"])
                nd.done(act.activation(lg[0:n, :], az[0:n, :], ACT.Ln, bias=ones[0:n, 0:1]), tt, "l")
                nd.after_pe(tt, "v")
                nd.done(act.activation(vt[0:n, 0:512], psum[0:n, 2, :], ACT.Copy), tt, "v0")
                nd.done(act.activation(vt[0:n, 512:CV], psum[0:n, 3, 0:256], ACT.Copy), tt, "v1")
                nd.after_pe(tt, "sums")
                nd.done(act.activation(eb[0:n, :], psum[0:n, 5, 0:CK], ACT.Exp), tt, "eb")
                nd.done(act.activation(enb[0:n, :], psum[0:n, 5, 0:CK], ACT.Exp, scale=-1.0), tt, "enb")
                nd.done(act.activation(ebd[0:n, :], psum[0:n, 6, 0:CK], ACT.Exp), tt, "ebd")
                nd.done(act.activation(ebl[0:DK, 0:HC * nch], psum[0:DK, 7, 0:HC * nch], ACT.Exp), tt, "ebl")
                nd.after_pe(tt, "turn")
                v = lambda ap: ap.rearrange("p (h t) -> p h t", h=HC)[:, :, 0:n]
                nd.done(act.activation(qeT[0:DK, :, 0:n], v(psum[0:DK, 0, :]), ACT.Copy), tt, "qeT")
                nd.done(act.activation(keT[0:DK, :, 0:n], v(psum[0:DK, 1, :]), ACT.Copy), tt, "keT")
                nd.after_dve(tt, "oc", 1)
                for h in range(HC):
                    nd.done(act.activation(gjunk[0:n, DV * h:DV * h + DV], oc[0:n, DV * h:DV * h + DV], ACT.Square,
                                           accum_out=rs[0:n, h:h + 1]), tt, "sq", h)
                act.wait_ge(ga_, GA[tt, "sq", HC - 1])
                nd.done(act.activation(rs[0:n, :], rs[0:n, :], ACT.Sqrt, bias=eps_c[0:n], scale=1.0 / DV), tt, "rms")
                nd.done(act.activation(rcf[:, :, 0:n], rcf[:, :, 0:n], ACT.Silu), tt, "silu")
                nd.after_dve(tt, "out", 5)
                nd.done(act.activation(hi[:, MIX_C:KT, a:a + n], out6[:, :, 0:n], ACT.Copy), tt, "hi")

        def gla_dve(dve):
            nd = Named(dve, gv, GV)
            dve.wait_ge(pa_o, NU)
            dve.wait_ge(pl_mm, NPOOL)
            dve.wait_ge(pl_lo, NPOOL)
            dve.wait_ge(pl_out, 48)
            dve.wait_ge(pa_lo, NU)
            dve.memset(am, 0.0).then_inc(gl_z0, 1)
            dve.memset(am_s, 0.0).then_inc(gl_z0, 1)
            dve.memset(S[:, 0, :], 0.0).then_inc(gl_z0, 1)
            dve.wait_ge(gl_z0, 3)
            for tt, (a, n) in enumerate(TILES):
                smp = tt == NT - 1
                nd.after_pe(tt, "z")
                nd.done(dve.tensor_copy(zs[0:n, :], psum[0:n, 4, 0:CK]), tt, "zs")
                nd.after_dve(tt, "zs")
                nd.done(dve.scalar_tensor_tensor(out=az[0:n, :], in0=zs[0:n, :], scalar=-1.0, in1=zs[0:n, :], op0=ALU.mult, op1=ALU.max), tt, "az")
                nd.after_act(tt, "l")
                nd.done(dve.scalar_tensor_tensor(out=gg[0:n, :], in0=zs[0:n, :], scalar=0.0, in1=lg[0:n, :], op0=ALU.min, op1=ALU.subtract), tt, "g")
                nd.after_act(tt, "ebd")
                nd.after_pe(tt, "qk")
                nd.done(dve.scalar_tensor_tensor(out=qe[0:n, :], in0=psum[0:n, 0, 0:CK], scalar=SCALE_C, in1=eb[0:n, :], op0=ALU.mult, op1=ALU.mult), tt, "qe")
                nd.done(dve.tensor_tensor(ke[0:n, :], psum[0:n, 1, 0:CK], enb[0:n, :], ALU.mult), tt, "ke")
                nd.done(dve.tensor_tensor(kd[0:n, :], psum[0:n, 1, 0:CK], ebd[0:n, :], ALU.mult), tt, "kd")
                nd.after_pe(tt, "scores")
                m = C("upto" + sfx(tt), n).bitcast(I32)
                nd.done(dve.copy_predicated((am_s if smp else am)[0:n, :, 0:n], m.unsqueeze(1).to_broadcast([n, HC, n]),
                                            psum[0:n, 2, :].rearrange("p (h t) -> p h t", h=HC)[:, :, 0:n]), tt, "mask")
                ubanks = ((5, 6), (7, 0))
                if smp:
                    dve.memset(qd[0:DK], 0.0).then_inc(gl_z0, 1)
                    dve.wait_ge(gl_z0, 4)
                    nd.done(dve.tensor_copy(qd[0:DK].rearrange("p h (b s) -> p h b s", b=TB)[:, :, :, 0:TT],
                                            qeT[0:DK, :, 0:n].rearrange("p h (b t) -> p h b t", b=TB)), tt, "qd")
                    dve.wait_ge(pg_out, 16)
                for c in range(TB if smp else 4):
                    if smp:
                        nd.done(dve.tensor_scalar(kdm[0:n, c % 2, :], kd[0:n, :], C("chunk_s", n)[:, c:c + 1], GATE_NORM, ALU.mult, ALU.mult), tt, "kdm", c)
                        src, dst = s0[:, c % 2, :], sn[:, c % 2, :]
                        dve.wait_ge(s0_in[c % 2], 16 * (c // 2) + 16)
                        if c >= 2:
                            dve.wait_ge(sn_out[c % 2], 16 * (c // 2))
                        nch = TB
                    else:
                        src, dst = S[:, (4 * tt + c) % 5, :], S[:, (4 * tt + c + 1) % 5, :]
                        if c:
                            nd.after_dve(tt, "S", c - 1, HC - 1)
                        nch = 4
                    nd.after_pe(tt, "state", c)
                    for h in range(HC):
                        x = slice(DV * h, DV * h + DV)
                        nd.done(dve.scalar_tensor_tensor(out=dst[0:DK, x], in0=src[0:DK, x], scalar=ebl[0:DK, nch * h + c:nch * h + c + 1],
                                                         in1=psum[0:DK, ubanks[c % 2][h // 2], DV * (h % 2):DV * (h % 2) + DV],
                                                         op0=ALU.mult, op1=ALU.add), tt, "S", c, h)
                nd.after_pe(tt, *(("inter", TB - 1) if smp else ("out",)))
                for i in range(2):
                    nd.done(dve.tensor_copy(oc[0:n, 2 * DV * i:2 * DV * (i + 1)], psum[0:n, 3 + i, 0:2 * DV]), tt, "oc", i)
                nd.after_act(tt, "rms")
                nd.done(dve.reciprocal(rs[0:n, :], rs[0:n, :]), tt, "rs")
                nd.after_dve(tt, "rs")
                o4 = oc[0:n, :].rearrange("p (h v) -> p h v", h=HC)
                nd.done(dve.tensor_tensor(o4, o4, rs[0:n, :].unsqueeze(2).to_broadcast([n, HC, DV]), ALU.mult), tt, "on")
                nd.after_pe(tt, "oT")
                nd.after_act(tt, "silu")
                for m in range(6):
                    nd.done(dve.scalar_tensor_tensor(out=out6[:, m, 0:n], in0=psum[:, 1 + m // 4, P * (m % 4):P * (m % 4) + n], scalar=GN[:, m:m + 1],
                                                     in1=rcf[:, m, 0:n], op0=ALU.mult, op1=ALU.mult), tt, "out", m)
                nd.after_act(tt, "hi")
                nd.done(dve.tensor_tensor(lo[:, MIX_C:KT, a:a + n], out6[:, :, 0:n], hi[:, MIX_C:KT, a:a + n].bitcast(F32), ALU.subtract), tt, "lo")
            dve.wait_ge(gv, GV[NT - 1, "lo"])
            dve.sem_inc(s_mix, 1)

        @block.sync
        def _(sp):
            sp_start(sp)
            with sp.Fori(1, G_ROW) as g:
                load_group(sp, g, cols(win_v, g))
            dec_sp(sp)
            with sp.Fori(0, TB - 1) as b:
                dec_sp_b(sp, b)
            dec_sp_b(sp, TB - 1, last=True)
            dtail_sp(sp, 0)
            kv_sp(sp)
            dtail_sp(sp, 1)
            pa_sp(sp)
            pool_sp(sp)
            gla_sp(sp)
            sp.wait_ge(s_mix, 1)
            for i in range(2):
                sp.wait_ge(sn_out[i], 64)
            sp.wait_ge(xt_out, 16)
            sp.dma_start(xT.rearrange("p k t -> p (k t)"), xT_d).then_inc(xt_in, 16)
            with sp.Fori(1, G_O) as g:
                load_group(sp, G_IN + g, cols(wo_v, g))
            sp_ffn(sp)
            final_sp(sp)
            sp.wait_ge(kv_st[0], 32 * 3)
            sp.wait_ge(kv_st[1], 32 * 2)

        @block.gpsimd
        def _(pool):
            norm_pool(pool, 0)
            in_pool(pool)
            pool.wait_ge(wlo_done, 4 * (G_ROW + 1))
            with pool.Fori(0, TB) as b:
                dec_pool_b(pool, b)
            in_store(pool, G_LAST)
            norm_pool(pool, 1)

        @block.scalar
        def _(act):
            copies_in(act, xt_act, 0)
            act.wait_ge(xt_dve, 10)
            act.wait_ge(xt_act, 10)
            act.wait_ge(s_ready, 3)
            norm_act(act, 0)
            in_act(act)
            in_act_loop(act)
            with act.Fori(0, TB) as b:
                dec_act_b(act, b)
            kv_stage_act(act)
            ga_act(act)
            dtail_act(act)
            pa_act(act)
            pool_act(act)
            gla_act(act)
            o_act(act)
            act.wait_ge(o_added, 2 + G_O)
            norm_act(act, 1)
            ffn_act(act)
            act.wait_ge(dn_added, 8 * NJ)
            final_act(act)

        @block.vector
        def _(dve):
            dve.memset(ones[:, :], 1.0).then_inc(s_ready, 1)
            dve.memset(misc[:, :], EPS).then_inc(s_ready, 1)
            dve.memset(gaT[:, :], 1.0).then_inc(s_ready, 1)
            for s_ in (o_ready, sl_done, ob_done):
                dve.sem_inc(s_, 1)
            dve.sem_inc(ob_out, 16)
            for s_ in (in_ev, o_added):
                dve.sem_inc(s_, 2)
            copies_in(dve, xt_dve, 1)
            dve.wait_ge(s_vt, 1)
            dve.tensor_copy(vecs[:, 0:58], psum[:, 4, 0:58]).then_inc(s_vc, 1)
            dve.wait_ge(s_vc, 1)
            norm_dve(dve, 0, G1)
            in_dve(dve)
            dve.wait_ge(xt_out, 16)
            in_dve_loop(dve)
            dve.memset(s_max_w, 0.0).then_inc(dec_z, 1)
            dve.wait_ge(dec_z, 1)
            with dve.Fori(0, TB) as b:
                dec_dve_b(dve, b, DVE_B * b)
            kv_stage_dve(dve)
            dtail_dve(dve)
            pa_dve(dve)
            pool_dve(dve)
            gla_dve(dve)
            o_dve(dve)
            dve.wait_ge(o_added, 2 + G_O)
            norm_dve(dve, 1, G2)
            ffn_dve(dve)
            final_dve(dve)

        @block.tensor
        def _(pe):
            transposes_in(pe)
            pe.wait_ge(s_ready, 3)
            norm_pe(pe, 0)
            pe.wait_ge(s_vc, 1)
            in_pe(pe)
            with pe.Fori(0, TB) as b:
                dec_pe_b(pe, b)
            kv_stage_pe(pe)
            ga_pe(pe)
            dtail_pe(pe)
            pa_pe(pe)
            pool_pe(pe)
            gla_pe(pe)
            o_pe(pe)
            norm_pe(pe, 1)
            ffn_pe(pe)
            final_pe(pe)


_INS = ['x_prompt', 'x_sample', 'cache_win_k', 'cache_win_v', 'state_pool', 'state_gla', 'norm1_g', 'w_in', 'w_gate2', 'b_gate',
        'w_pool', 'pool_scale', 'gla_norm_g', 'w_o', 'norm2_g', 'w_ffn_gate', 'w_ffn_up', 'w_ffn_down', 'final_norm_g']
_OUTS = [(1, TP, D), (TB, TT, D), (1, 1, TP, HA, HD), (1, 1, TP, HA, HD), (1, 1, PBUF, DB), (1, 1, HC, DK, DV),
         (1, TB, TT, HA, HD), (1, TB, TT, HA, HD), (1, TB, PBUF, DB), (1, TB, HC, DK, DV)]


def kernel(**inputs):
    import numpy as _np
    import concourse.bacc as _bacc
    from concourse.bass_utils import run_bass_kernel_spmd as _run

    nc = _bacc.Bacc("TRN2", target_bir_lowering=False, num_devices=1)
    arrays, args = {}, []
    data = {name: _np.ascontiguousarray(inputs[name]) for name in _INS}
    data["table"] = table_columns()
    for name, a in data.items():
        arrays[f"in_{name}"] = a
        args.append(nc.dram_tensor(f"in_{name}", a.shape, mybir.dt.from_np(a.dtype), kind="ExternalInput").ap())
    for i, shape in enumerate(_OUTS):
        args.append(nc.dram_tensor(f"out_{i}", shape, F32, kind="ExternalOutput").ap())
    build(nc, *args)
    r = _run(nc, [arrays], core_ids=[0])
    return tuple(r.results[0][f"out_{i}"] for i in range(len(_OUTS)))
```

```python
import concourse.bass as bass
from concourse import mybir
from contextlib import ExitStack

F32 = mybir.dt.float32
F32R = mybir.dt.float32r
I32 = mybir.dt.int32
ALU = mybir.AluOpType
ACT = mybir.ActivationFunctionType
AX = mybir.AxisListType

P = 128
D = 2048
KT = D // P
TP, TB, TT = 512, 8, 8
TS = TB * TT
T = TP + TS
HALF = T // 2
NTT = -(-T // P)
TILES = [(n * P, min(P, T - n * P)) for n in range(-(-T // P))]
HA, HD = 6, 128
DA = HA * HD
HC, DK, DV = 4, 96, 192
CK, CV = HC * DK, HC * DV
DB, NPOOL, PBUF = 512, 4, 15
RANK = 16
PAST = 2048
FF = 5632
NJ = FF // 256
EPS = 1e-6
GATE_NORM = 16.0
OQ, OK, OV, OU = 0, DA, 2 * DA, 3 * DA
OQC = OU + DB
OKC = OQC + CK
OVC = OKC + CK
ORC = OVC + CV
OGA = ORC + CV
G_IN, G_O = OGA // 256, D // 256
MIX_B, MIX_C = DA // P, (DA + DB) // P
NEG = -1e30
LN2 = 0.6931471805599453
LN3 = 1.0986122886681098
UNIQ, DIL, LAST = 6, 3, 1
NBLK = UNIQ + DIL + LAST
SCALE_A = HD ** -0.5
SCALE_C = DK ** -0.5
CHUNK_P, CHUNK_S = 32, TT


def count_log(dist, window_ok=True):
    n = int(0 <= dist <= 128) + int(dist >= 0 and dist % 4 == 0 and dist <= 512) \
        + int(dist >= 0 and dist % 16 == 0 and dist <= 2048)
    return [NEG, 0.0, LN2, LN3][n]


TABLE = {}
_at = 0
for _name, _w in (("ident", P), ("mask_a", TP), ("log_dve", UNIQ + 2 * DIL), ("log_last", TT), ("log_new", TS),
                  ("neg_own", TT), ("neg_oth", TT), ("is_own", TT), ("is_oth", TT),
                  ("upto_p", P), ("after_p", P), ("chunk_p", P // CHUNK_P),
                  ("upto_s", TS), ("after_s", TS), ("chunk_s", TB), ("inv_count", NPOOL * 16)):
    TABLE[_name] = (_at, _w)
    _at += _w
TABLE_W = _at


def table_columns():
    import numpy as np
    t = np.zeros((P, TABLE_W), np.float32)

    def col(name):
        a, w = TABLE[name]
        return t[:, a:a + w]

    col("ident")[:] = np.eye(P)
    for p in range(P):
        for c in range(TP):
            col("mask_a")[p, c] = count_log(p + TP - P - c) / SCALE_A
        own, oth = p % TT, (p + 4) % TT
        for j in range(DIL):
            r = 1536 + P * j + p
            col("log_dve")[p, UNIQ + j] = count_log(PAST + own - r)
            col("log_dve")[p, UNIQ + DIL + j] = count_log(PAST + oth - r)
        for q in range(TT):
            col("log_last")[p, q] = count_log(PAST + q - (PAST - P + p))
            col("neg_own")[p, q] = 0.0 if q == own else NEG
            col("neg_oth")[p, q] = 0.0 if q == oth else NEG
            col("is_own")[p, q] = q == own
            col("is_oth")[p, q] = q == oth
    for r in range(TS):
        for c in range(TS):
            same = r // TT == c // TT
            col("log_new")[r, c] = count_log(c - r) if same else NEG
            col("upto_s")[r, c] = (same and r <= c) / GATE_NORM
            col("after_s")[r, c] = (same and r > c) / GATE_NORM
        col("chunk_s")[r, r // TT] = 1 / GATE_NORM
    for r in range(P):
        for c in range(P):
            same = r // CHUNK_P == c // CHUNK_P
            col("upto_p")[r, c] = (same and r <= c) / GATE_NORM
            col("after_p")[r, c] = (same and r > c) / GATE_NORM
        col("chunk_p")[r, r // CHUNK_P] = 1 / GATE_NORM
    for g in range(NPOOL):
        for c in range(16):
            col("inv_count")[:, 16 * g + c] = 1.0 / min(2 << g, c + 1)
    return t


class Steps:

    def __init__(self, eng, sem, base=0):
        self.eng, self.sem, self.base, self.n = eng, sem, base, 0

    def done(self, ins):
        ins.then_inc(self.sem, 1)
        self.n += 1
        return self.n

    def wait(self, n):
        self.eng.wait_ge(self.sem, self.base + n)

    def last(self):
        self.wait(self.n)


def build(nc, x_prompt, x_sample, cache_k, cache_v, state_pool, state_gla, norm1_g, w_in, w_gate2, b_gate,
          w_pool, pool_scale, gla_norm_g, w_o, norm2_g, w_gate, w_up, w_down, final_g, table,
          y_p, y_s, o_pk, o_pv, o_pp, o_pg, o_sk, o_sv, o_sp, o_sg):
    proj_d = nc.dram_tensor("proj_scratch", (OGA, T), F32).ap()
    xT_d = nc.dram_tensor("xT_scratch", (P, KT * T), F32).ap()
    q_d = nc.dram_tensor("q_scratch", (2, TS, DA), F32).ap()
    oa_d = nc.dram_tensor("decode_out_scratch", (TS, DA), F32).ap()
    den_d = nc.dram_tensor("decode_den_scratch", (HA, TS), F32).ap()
    proj_m = proj_d.rearrange("(m p) t -> p m t", p=P)

    x_d = [x_prompt[0, a:a + n, :] if a < TP else x_sample.rearrange("b t d -> (b t) d") for a, n in TILES]
    y_d = [y_p[0, a:a + n, :] if a < TP else y_s.rearrange("b t d -> (b t) d") for a, n in TILES]
    ck = cache_k[0].rearrange("b r h d -> b r (h d)")
    cv = cache_v[0].rearrange("b r h d -> b r (h d)")
    pk, pv = (a[0, 0].rearrange("r h d -> r (h d)") for a in (o_pk, o_pv))
    sk, sv = (a[0].rearrange("b t h d -> (b t) (h d)") for a in (o_sk, o_sv))
    kv_out = [[pk[a:a + n, :], pv[a:a + n, :]] if a < TP else [sk, sv] for a, n in TILES]

    ctx = ExitStack()
    with ctx:
        def sb(name, shape, dt=F32):
            return ctx.enter_context(nc.sbuf_tensor(name, shape, dt))[tuple(slice(None) for _ in shape)]

        def sem(name):
            return ctx.enter_context(nc.semaphore(name))

        act_r = sb("act_r", [P, 2, KT, T], F32R)
        w_hi = sb("w_hi", [P, 4, 1024], F32R)
        w_lo = sb("w_lo", [P, 4, 1024], F32R)
        w_raw = sb("w_raw", [P, 4, 1024])
        ffn_r = sb("ffn_r", [P, 2, 2, 2, T], F32R)
        tab = sb("tab", [P, TABLE_W])
        ones = sb("ones", [P, P])
        vecs = sb("vecs", [P, 64])
        misc = sb("misc", [P, 8])
        GW = 15200
        g_sb = sb("general", [P, GW])
        psum = ctx.enter_context(nc.psum_tensor("psum", [P, 8, 512], F32))
        pool_at = [0]

        def area(*shape, at=None):
            n = 1
            for s in shape:
                n *= s
            a = pool_at[0] if at is None else at
            pool_at[0] = a + n
            assert a + n <= GW, (a, n)
            v = g_sb[:, a:a + n]
            if len(shape) == 2:
                v = v.rearrange("p (a b) -> p a b", a=shape[0])
            if len(shape) == 3:
                v = v.rearrange("p (a b c) -> p a b c", a=shape[0], b=shape[1])
            return v

        def C(name, rows=P):
            a, w = TABLE[name]
            return tab[0:rows, a:a + w]

        ident = C("ident")
        eps_c = misc[:, 0:1]
        hi, lo = act_r[:, 0], act_r[:, 1]
        G1, G2, GS, GN = (vecs[:, a:b] for a, b in ((0, 16), (16, 32), (32, 36), (36, 42)))

        xT = area(KT, T, at=0)
        tmp2 = area(2, T)
        diag_t = g_sb[:, KT * T:KT * T + NTT * P].rearrange("p (n t) -> p n t", n=NTT)
        rstd = area(T)
        rtok = misc[:, 1:1 + NTT]
        xs = area(2, D)
        sil = area(2, T, at=KT * T + 3 * T)
        ftmp = area(2, T)
        stage_in = area(2, T, at=GW - 2 * T)

        s_const = sem("consts_in")
        s_ready = sem("consts_ready")
        x_in = [sem(f"x_in{i}") for i in range(2)]
        xt_tr = sem("xt_transposed")
        xt_act = sem("xt_copied_act")
        xt_dve = sem("xt_copied_dve")
        xt_out = sem("xt_spilled")
        xt_in = sem("xt_back")
        sq_done = sem("squares_done")
        acc_done = sem("squares_added")
        xsq_done = sem("x_square_sums_done")
        ss_done = sem("square_sums_done")
        rcp_done = sem("token_scales_done")
        diag_done = sem("token_scales_on_diagonal")
        spread_done = sem("token_scales_spread")
        rms_done = sem("rms_done")
        rstd_done = sem("rstd_done")
        h_done = sem("h_done")
        hhi_done = sem("h_high_done")
        hlo_done = sem("h_low_done")
        raw_in = [sem(f"raw_in{i}") for i in range(4)]
        whi_done = sem("w_high_done")
        wlo_done = sem("w_low_done")
        w_used = sem("w_chunk_used")
        in_ev = sem("in_group_copied")
        in_out = sem("in_group_stored")
        o_added = sem("o_group_added")
        sil_done = sem("silu_done")
        f_done = sem("gated_done")
        fhi_done = sem("gated_high_done")
        flo_done = sem("gated_low_done")
        dn_done = sem("down_pair_done")
        dn_added = sem("down_pair_added")
        y_tr = sem("y_transposed")
        y_ev = sem("y_scaled")
        y_out = [sem(f"y_stored{i}") for i in range(3)]

        block = ctx.enter_context(nc.Block())

        win_v = w_in[0, :, 0:OGA].rearrange("(q k p) e -> q p k e", k=4, p=P)
        wo_v = w_o[0].rearrange("(q k p) e -> q p k e", k=4, p=P)
        wg_v = w_gate[0].rearrange("(q k p) e -> q p k e", k=4, p=P)
        wu_v = w_up[0].rearrange("(q k p) e -> q p k e", k=4, p=P)
        wd_v = w_down[0].rearrange("(j k p) e -> j p k e", k=2, p=P)

        def load_group(sp, g, src, qs=range(4)):
            for q in qs:
                if not (isinstance(g, int) and g == 0):
                    sp.wait_ge(wlo_done, 4 * (g - 1) + q + 1)
                k, e = (4, 256) if src(q).shape[1] == 4 else (2, 512)
                sp.dma_start(w_raw[:, q].rearrange("p (k e) -> p k e", k=k), src(q)).then_inc(raw_in[q], 16)

        def cols(v, g):
            return lambda q: v[q, :, :, bass.ds(g * 256, 256)]

        def down_src(j):
            return lambda q: wd_v[bass.ds(j, 1), :, :, 512 * q:512 * q + 512].rearrange("o p k e -> (o p) k e")

        def split_high(act, g, q):
            act.wait_ge(raw_in[q], 16 * (g + 1))
            if not (isinstance(g, int) and g == 0):
                act.wait_ge(w_used, 4 * (g - 1) + q + 1)
            act.activation(w_hi[:, q], w_raw[:, q], ACT.Copy).then_inc(whi_done, 1)

        def split_low(dve, g, q):
            dve.wait_ge(whi_done, 4 * g + q + 1)
            dve.tensor_tensor(w_lo[:, q], w_raw[:, q], w_hi[:, q].bitcast(F32), ALU.subtract).then_inc(wlo_done, 1)

        def product(pe, out2, wslot, c0, rhs_hi, rhs_lo, first, last):
            for w, r, n in ((w_hi, rhs_hi, 0), (w_hi, rhs_lo, 1), (w_lo, rhs_hi, 2)):
                for half in range(2):
                    mm = pe.matmul(psum[:, out2 + half, 0:HALF], w[:, wslot, c0:c0 + P],
                                   r[:, half * HALF:(half + 1) * HALF],
                                   start=first and n == 0, stop=last and n == 2)
            return mm

        def chunk(pe, g, bank, q, norm=None, half=None):
            pe.wait_ge(wlo_done, 4 * g + q + 1)
            for k in range(4) if half is None else range(2 * half, 2 * half + 2):
                kk = 4 * q + k
                if norm is not None:
                    pe.wait_ge(hlo_done, KT * norm + kk + 1)
                for m in range(2):
                    mm = product(pe, bank + 2 * m, q, 256 * k + P * m, hi[:, kk], lo[:, kk], kk == 0, kk == KT - 1)
            if half != 0:
                mm.then_inc(w_used, 1)

        def full_group(pe, g, bank, norm=None):
            for q in range(4):
                chunk(pe, g, bank, q, norm)

        def two(bank):
            return psum[:, bank:bank + 4, 0:HALF]

        def sp_start(sp):
            sp.dma_start(tab[:, :], table).then_inc(s_const, 16)
            for tt, (a, n) in enumerate(TILES):
                if tt >= 2:
                    sp.wait_ge(xt_tr, 4 * (tt - 1))
                    sp.wait_ge(xsq_done, tt - 1)
                sp.dma_start(xs[0:n, tt % 2, :], x_d[tt]).then_inc(x_in[tt % 2], 16)
                if tt == 0:
                    rows = vrow[0:16, :], vrow[16:32, :], vrow[32:36, :]
                    for dst, src in zip(rows, (norm1_g[0], norm2_g[0], pool_scale[0])):
                        sp.dma_start(dst, src.rearrange("(k p) -> k p", p=P)).then_inc(s_vec, 16)
                    gn = gla_norm_g[0:1, :]
                    for half in range(2):
                        r = 36 + 3 * half
                        for dst, src in ((vrow[r:r + 1, :], gn[:, 0:P]), (vrow[r + 1:r + 2, 0:DV - P], gn[:, P:DV]),
                                         (vrow[r + 1:r + 2, DV - P:P], gn[:, 0:2 * P - DV]),
                                         (vrow[r + 2:r + 3, :], gn[:, 2 * P - DV:DV])):
                            sp.dma_start(dst, src).then_inc(s_vec, 16)
                    load_group(sp, 0, cols(win_v, 0))
                    sp.dma_start(ga_raw, w_in[0, :, OGA:OGA + RANK].rearrange("(k p) e -> p k e", p=P)).then_inc(s_ga, 16)
            sp.wait_ge(xt_act, 10)
            sp.wait_ge(xt_dve, 10)
            sp.dma_start(xT_d, xT.rearrange("p k t -> p (k t)")).then_inc(xt_out, 16)

        s_vec = sem("gain_rows_in")
        s_vt = sem("gain_rows_transposed")
        s_vc = sem("gain_columns_done")
        s_ga = sem("gate_columns_in")
        s_gs = sem("gate_columns_split")
        s_gm = sem("gate_product_done")
        s_gT = sem("gate_inputs_done")
        vrow = sb("vrow", [64, P])
        ga_raw = sb("ga_raw", [P, KT, RANK])
        ga_hi = ffn_r[:, 0, 0, 0, 0:KT * RANK].rearrange("p (k e) -> p k e", k=KT)
        ga_lo = ffn_r[:, 0, 1, 0, 0:KT * RANK].rearrange("p (k e) -> p k e", k=KT)
        gaT = sb("gaT", [32, T])

        def transposes_in(pe):
            pe.wait_ge(s_const, 16)
            for tt, (a, n) in enumerate(TILES):
                pe.wait_ge(x_in[tt % 2], 16 * (tt // 2 + 1))
                for g in range(4):
                    u = 4 * tt + g
                    if u >= 8:
                        pe.wait_ge(xt_act if u % 2 == 0 else xt_dve, (u - 8) // 2 + 1)
                    for k in range(4):
                        mm = pe.transpose(psum[:, u % 8, P * k:P * k + n], xs[0:n, tt % 2, P * (4 * g + k):P * (4 * g + k + 1)],
                                          ident[0:n, 0:n])
                    mm.then_inc(xt_tr, 1)
            pe.wait_ge(s_vec, 16 * 11)
            pe.wait_ge(xt_act, 7)
            pe.transpose(psum[:, 4, 0:42], vrow[0:42, :], ident[0:42, 0:42]).then_inc(s_vt, 1)

        def copies_in(eng, own, parity):
            for u in range(parity, 4 * NTT, 2):
                tt, g = divmod(u, 4)
                a, n = TILES[tt]
                if own is xt_act and g == 0:
                    x_square(eng, tt)
                eng.wait_ge(xt_tr, u + 1)
                dst = xT[:, 4 * g:4 * g + 4, a:a + n]
                src = psum[:, u % 8, :].rearrange("p (k t) -> p k t", k=4)[:, :, 0:n]
                ins = eng.activation(dst, src, ACT.Copy) if own is xt_act else eng.tensor_copy(dst, src)
                ins.then_inc(own, 1)

        def square(act, nrm, k, slot):
            act.wait_ge(acc_done, KT * nrm + k - 1) if nrm or k >= 2 else None
            x = xT[:, k] if isinstance(k, int) else xT[:, bass.ds(k, 1), :].rearrange("p o t -> p (o t)")
            act.activation(tmp2[:, slot], x, ACT.Square).then_inc(sq_done, 1)

        def add_square(dve, nrm, k, slot):
            dve.wait_ge(sq_done, KT * nrm + k + 1)
            if nrm or k:
                dve.wait_ge(acc_done, KT * nrm + k)
            dve.tensor_tensor(rstd, rstd, tmp2[:, slot], ALU.add).then_inc(acc_done, 1)

        def clear_sums(dve):
            clears[0] += 1
            dve.memset(rstd, 0.0).then_inc(acc_clear, 1)
            dve.wait_ge(acc_clear, clears[0])

        clears = [0]
        acc_clear = sem("square_sums_cleared")

        def x_square(act, tt):
            n = TILES[tt][1]
            act.wait_ge(x_in[tt % 2], 16 * (tt // 2 + 1))
            if tt:
                act.wait_ge(xsq_done, tt)
            act.activation(act_r[0:n, 1, 0:4, 0:512], xs[0:n, tt % 2, :].rearrange("p (a b) -> p a b", a=4), ACT.Square,
                           accum_out=rtok[0:n, tt:tt + 1]).then_inc(xsq_done, 1)

        def token_sums(pe, bank):
            for t2, (a2, n2) in enumerate(TILES):
                mm = pe.matmul(psum[0:n2, bank, t2:t2 + 1], rstd[:, a2:a2 + n2], ones[:, 0:1], start=True, stop=True)
            mm.then_inc(ss_done, 1)

        def token_rms(act, src):
            for c, n in ((slice(0, NTT - 1), P), (slice(NTT - 1, NTT), TS)):
                act.activation(rtok[0:n, c], src[0:n, c], ACT.Sqrt, bias=eps_c[0:n], scale=1.0 / D).then_inc(rms_done, 1)

        def token_scales(dve, nrm):
            dve.wait_ge(rms_done, 2 * nrm + 2)
            for c, n in ((slice(0, NTT - 1), P), (slice(NTT - 1, NTT), TS)):
                dve.reciprocal(rtok[0:n, c], rtok[0:n, c]).then_inc(rcp_done, 1)
            dve.wait_ge(rcp_done, 2 * nrm + 2)

        def norm_act(act, nrm):
            for k in range(KT):
                n = KT * nrm + k
                act.wait_ge(h_done, n + 1)
                act.activation(hi[:, k], tmp2[:, k % 2], ACT.Copy).then_inc(hhi_done, 1)

        def norm_dve(dve, nrm, gain):
            token_scales(dve, nrm)
            for tt, (a, n) in enumerate(TILES):
                dve.tensor_scalar(diag_t[0:n, tt, 0:n], ident[0:n, 0:n], rtok[0:n, tt:tt + 1], None, ALU.mult).then_inc(diag_done, 1)
            dve.wait_ge(spread_done, nrm + 1)
            dve.tensor_copy(rstd[:, 0:TP], psum[:, 0, :]).then_inc(rstd_done, 1)
            dve.tensor_copy(rstd[:, TP:T], psum[:, 1, 0:TS]).then_inc(rstd_done, 1)
            dve.wait_ge(rstd_done, 2 * nrm + 2)
            for k in range(KT):
                n = KT * nrm + k
                if k >= 2:
                    dve.wait_ge(hlo_done, n - 1)
                dve.scalar_tensor_tensor(out=tmp2[:, k % 2], in0=xT[:, k], scalar=gain[:, k:k + 1], in1=rstd,
                                         op0=ALU.mult, op1=ALU.mult).then_inc(h_done, 1)
                if nrm == 0 and k % 4 == 1:
                    split_low(dve, 0, k // 4)

        def norm_pool(pool, nrm):
            for k in range(KT):
                n = KT * nrm + k
                pool.wait_ge(hhi_done, n + 1)
                pool.tensor_tensor(lo[:, k], tmp2[:, k % 2], hi[:, k].bitcast(F32), ALU.subtract).then_inc(hlo_done, 1)

        def norm_pe(pe, nrm):
            pe.wait_ge(diag_done, NTT * (nrm + 1))
            for tt, (a, n) in enumerate(TILES):
                mm = pe.matmul(psum[:, tt // 4, P * (tt % 4):P * (tt % 4) + n], ones[0:n, :], diag_t[0:n, tt, 0:n], start=True, stop=True)
            mm.then_inc(spread_done, 1)

        G_ROW, G_LAST = 11, G_IN - 1
        PAIRS = (G_ROW - 1) // 2

        def in_store(pool, g):
            pool.wait_ge(in_ev, 2 + g + 1)
            pool.dma_start(proj_m[:, bass.ds(2 * g, 2), :], stage_in).then_inc(in_out, 16)

        def in_copy(eng, g, bank):
            eng.wait_ge(w_used, 4 * g + 4)
            if not (isinstance(g, int) and g == 0):
                eng.wait_ge(in_out, 16 * g)
            dst = stage_in.rearrange("p m (a t) -> p (m a) t", a=2)
            ins = eng.tensor_copy(dst, two(bank)) if eng is nc.vector else eng.activation(dst, two(bank), ACT.Copy)
            ins.then_inc(in_ev, 1)

        def in_pe(pe):
            pe.wait_ge(rstd_done, 2)
            for g in range(2):
                full_group(pe, g, 4 * g, norm=0)
            with pe.Fori(1, PAIRS) as i:
                for s in range(2):
                    pe.wait_ge(in_ev, 2 * i + s + 1)
                    full_group(pe, 2 * i + s, 4 * s)
            pe.wait_ge(in_ev, G_ROW)
            chunk(pe, G_ROW - 1, 0, 0)
            dec_pe(pe)
            for q in range(1, 4):
                chunk(pe, G_ROW - 1, 0, q)

        def ga_pe(pe, k):
            for w, r, n in ((ga_hi, hi, 0), (ga_hi, lo, 1), (ga_lo, hi, 2)):
                for half in range(2):
                    mm = pe.matmul(psum[0:RANK, half, 0:HALF], w[:, k, :], r[:, k, half * HALF:(half + 1) * HALF],
                                   start=k == 0 and n == 0, stop=k == KT - 1 and n == 2)
            if k == KT - 1:
                mm.then_inc(s_gm, 1)

        def in_act(act):
            for q in range(4):
                split_high(act, 0, q)
            act.wait_ge(s_ga, 16)
            act.activation(ga_hi, ga_raw, ACT.Copy).then_inc(s_gs, 1)

        def in_act_loop(act):
            with act.Fori(1, G_ROW) as g:
                for q in range(4):
                    split_high(act, g, q)
            dec_act_scale(act)
            split_high(act, G_ROW, 0)
            dec_act_copies(act)
            for q in range(1, 4):
                split_high(act, G_ROW, q)

        def ga_act(act):
            act.wait_ge(s_gm, 1)
            act.wait_ge(s_ready, 3)
            act.activation(gaT[0:RANK, :].rearrange("p (a t) -> p a t", a=2), psum[0:RANK, 0:2, 0:HALF], ACT.Copy).then_inc(s_gT, 1)

        def in_dve(dve):
            dve.wait_ge(s_gs, 1)
            dve.tensor_tensor(ga_lo, ga_raw, ga_hi.bitcast(F32), ALU.subtract).then_inc(s_gs, 1)

        def in_dve_loop(dve):
            def pair(i):
                for s in range(2):
                    g = 2 * i + s
                    for q in range(4):
                        split_low(dve, g + 1, q)
                    in_copy(dve, g, 4 * s)

            pair(0)
            with dve.Fori(1, PAIRS) as i:
                pair(i)
            for q in range(4):
                split_low(dve, G_ROW, q)
            in_copy(dve, G_ROW - 1, 0)

        def in_pool(pool):
            with pool.Fori(0, G_ROW) as g:
                in_store(pool, g)

        def o_pe(pe):
            pe.wait_ge(s_mix, 1)
            with pe.Fori(0, G_O // 2) as i:
                for s in range(2):
                    pe.wait_ge(o_added, 2 * i + s + 1)
                    full_group(pe, G_IN + 2 * i + s, 4 * s)

        def o_dve(dve):
            dve.wait_ge(xt_in, 16)
            clear_sums(dve)
            with dve.Fori(0, G_O // 2) as i:
                for s in range(2):
                    g = 2 * i + s
                    for q in range(4):
                        split_low(dve, G_IN + g + 1, q)
                    dve.wait_ge(w_used, 4 * (G_IN + g) + 4)
                    x2 = xT[:, bass.ds(2 * g, 2), :].rearrange("p m (a t) -> p (m a) t", a=2)
                    dve.tensor_tensor(x2, two(4 * s), x2, ALU.add).then_inc(o_added, 1)
                    for m in range(2):
                        add_square(dve, 1, 2 * g + m, m)

        def o_act(act):
            with act.Fori(0, G_O) as g:
                for q in range(4):
                    split_high(act, G_IN + g + 1, q)
                act.wait_ge(o_added, g + 3)
                for m in range(2):
                    square(act, 1, 2 * g + m, m)

        def g_gate(j):
            return G_IN + G_O + (3 * j - 1 if not (isinstance(j, int) and j == 0) else 0)

        def g_up(j):
            return g_gate(j) + 1

        def g_down(j):
            return G_IN + G_O + 3 * (j + 1) + (1 if not (isinstance(j, int) and j == NJ - 1) else -1)

        def sp_ffn(sp):
            load_group(sp, g_gate(0), cols(wg_v, 0))
            load_group(sp, g_up(0), cols(wu_v, 0))
            with sp.Fori(1, NJ) as j:
                load_group(sp, g_gate(j), cols(wg_v, j))
                load_group(sp, g_up(j), cols(wu_v, j))
                load_group(sp, g_down(j - 1), down_src(j - 1))
            load_group(sp, g_down(NJ - 1), down_src(NJ - 1))

        def down_group(pe, j, s, last=False):
            g = g_down(j)
            fh, fl = ffn_r[:, s, 0], ffn_r[:, s, 1]
            pe.wait_ge(flo_done, 2 * j + 2)
            for q in range(4):
                pe.wait_ge(wlo_done, 4 * g + q + 1)
                for pair in range(2):
                    n = 2 * q + pair
                    if n == 1 and not last:
                        pe.wait_ge(f_done, 2 * (j + 1) + 2)
                    if n >= 2 or last:
                        pe.wait_ge(dn_added, 8 * j + n - 1)
                    for k in range(2):
                        for m in range(2):
                            mm = product(pe, 4 * pair + 2 * m, q, 512 * k + 256 * pair + P * m, fh[:, k], fl[:, k], k == 0, k == 1)
                    mm.then_inc(dn_done if pair == 0 else w_used, 1)

        def gate_up(pe, j, norm=None):
            pe.wait_ge(dn_added, 8 * (j - 1) - 1) if not (isinstance(j, int) and j <= 1) else None
            full_group(pe, g_gate(j), 0, norm)
            pe.wait_ge(dn_added, 8 * (j - 1)) if not (isinstance(j, int) and j <= 1) else None
            full_group(pe, g_up(j), 4)

        def before_down(pe, j):
            pe.wait_ge(sil_done, 2 * j + 2)

        def ffn_pe(pe):
            gate_up(pe, 0, norm=1)
            gate_up(pe, 1)
            before_down(pe, 1)
            down_group(pe, 0, 0)
            with pe.Fori(0, NJ // 2 - 1) as i:
                for s in range(2):
                    gate_up(pe, 2 * i + 2 + s)
                    before_down(pe, 2 * i + 2 + s)
                    down_group(pe, 2 * i + 1 + s, 1 - s)
            down_group(pe, NJ - 1, 1, last=True)

        def act_silu(act, j):
            act.wait_ge(w_used, 4 * g_gate(j) + 4)
            for t in range(2):
                if not (isinstance(j, int) and j == 0):
                    act.wait_ge(f_done, 2 * (j - 1) + t + 1)
                act.activation(sil[:, t].rearrange("p (a t) -> p a t", a=2), psum[:, 2 * t:2 * t + 2, 0:HALF], ACT.Silu).then_inc(sil_done, 1)

        def act_fhigh(act, j, s):
            for t in range(2):
                act.wait_ge(f_done, 2 * j + t + 1)
                if not (isinstance(j, int) and j < 2):
                    act.wait_ge(w_used, 4 * g_down(j - 2) + 4)
                act.activation(ffn_r[:, s, 0, t], ftmp[:, t], ACT.Copy).then_inc(fhi_done, 1)

        def dve_gated(dve, j):
            dve.wait_ge(w_used, 4 * g_up(j) + 4)
            for t in range(2):
                dve.wait_ge(sil_done, 2 * j + t + 1)
                if not (isinstance(j, int) and j == 0):
                    dve.wait_ge(flo_done, 2 * (j - 1) + t + 1)
                dve.tensor_tensor(ftmp[:, t].rearrange("p (a t) -> p a t", a=2), psum[:, 4 + 2 * t:6 + 2 * t, 0:HALF],
                                  sil[:, t].rearrange("p (a t) -> p a t", a=2), ALU.mult).then_inc(f_done, 1)

        def dve_flow(dve, j, s):
            for t in range(2):
                dve.wait_ge(fhi_done, 2 * j + t + 1)
                dve.tensor_tensor(ffn_r[:, s, 1, t], ftmp[:, t], ffn_r[:, s, 0, t].bitcast(F32), ALU.subtract).then_inc(flo_done, 1)

        def dve_add_down(dve, j, n):
            if n % 2 == 0:
                dve.wait_ge(dn_done, 4 * j + n // 2 + 1)
            else:
                dve.wait_ge(w_used, 4 * g_down(j) + n // 2 + 1)
            if not (isinstance(j, int) and j == 0):
                dve.wait_ge(dn_added, 8 * (j - 1) + n + 1)
            x2 = xT[:, 2 * n:2 * n + 2, :].rearrange("p m (a t) -> p (m a) t", a=2)
            dve.tensor_tensor(x2, two(4 * (n % 2)), x2, ALU.add).then_inc(dn_added, 1)

        def ffn_act(act):
            def split(g, qs):
                for q in qs:
                    split_high(act, g, q)

            def step(j, s, nxt):
                split(g_up(j), range(3))
                act_silu(act, j)
                split(g_up(j), [3])
                split(g_down(j - 1), range(4))
                act_fhigh(act, j, s)
                split(nxt, range(4))

            split(g_up(0), range(3))
            act_silu(act, 0)
            split(g_up(0), [3])
            split(g_gate(1), range(4))
            act_fhigh(act, 0, 0)
            step(1, 1, g_gate(2))
            with act.Fori(0, NJ // 2 - 2) as i:
                for s in range(2):
                    step(2 * i + 2 + s, s, g_gate(2 * i + 3 + s))
            step(NJ - 2, 0, g_gate(NJ - 1))
            step(NJ - 1, 1, g_down(NJ - 1))

        def ffn_dve(dve):
            def split(g, qs):
                for q in qs:
                    split_low(dve, g, q)

            def step(j, s, nxt):
                split(g_up(j), range(4))
                split(g_down(j - 1), range(3))
                dve_gated(dve, j)
                split(g_down(j - 1), [3])
                dve_flow(dve, j, s)
                for q in range(4):
                    dve_add_down(dve, j - 1, 2 * q)
                    dve_add_down(dve, j - 1, 2 * q + 1)
                    split(nxt, [q])

            split(g_up(0), range(4))
            split(g_gate(1), range(3))
            dve_gated(dve, 0)
            split(g_gate(1), [3])
            dve_flow(dve, 0, 0)
            step(1, 1, g_gate(2))
            with dve.Fori(0, NJ // 2 - 2) as i:
                for s in range(2):
                    step(2 * i + 2 + s, s, g_gate(2 * i + 3 + s))
            step(NJ - 2, 0, g_gate(NJ - 1))
            step(NJ - 1, 1, g_down(NJ - 1))
            clear_sums(dve)
            for n in range(8):
                dve_add_down(dve, NJ - 1, n)
                for m in range(2):
                    add_square(dve, 2, 2 * n + m, m)

        ysb = [area(D, at=KT * T + 3 * T), area(D), w_raw.rearrange("p a b -> p (a b)")[:, D:2 * D]]
        gain_rows = w_raw.rearrange("p a b -> p (a b)")[:, 0:D]
        gain_in = sem("final_gains_in")
        YBANKS = 7

        def final_add_squares(act):
            for n in range(8):
                act.wait_ge(dn_added, 8 * (NJ - 1) + n + 1)
                for m in range(2):
                    square(act, 2, 2 * n + m, m)

        def final_act(act):
            act.wait_ge(ss_done, 2)
            token_rms(act, psum[:, 7, 0:NTT])

        def final_dve(dve):
            token_scales(dve, 2)
            dve.wait_ge(gain_in, 16)
            for u in range(4 * NTT):
                tt, g = divmod(u, 4)
                a, n = TILES[tt]
                dve.wait_ge(y_tr, u + 1)
                if tt >= 3:
                    dve.wait_ge(y_out[tt % 3], 16 * (tt // 3))
                dve.scalar_tensor_tensor(out=ysb[tt % 3][0:n, 512 * g:512 * g + 512], in0=psum[0:n, u % YBANKS, :], scalar=rtok[0:n, tt:tt + 1],
                                         in1=gain_rows[0:n, 512 * g:512 * g + 512], op0=ALU.mult, op1=ALU.mult).then_inc(y_ev, 1)

        def final_pe(pe):
            for u in range(4 * NTT):
                tt, g = divmod(u, 4)
                a, n = TILES[tt]
                if u == YBANKS:
                    pe.wait_ge(acc_done, 3 * KT)
                    token_sums(pe, 7)
                pe.wait_ge(dn_added, 8 * NJ - (1 if u < 3 else 0))
                if u >= YBANKS:
                    pe.wait_ge(y_ev, u - YBANKS + 1)
                for k in range(4):
                    mm = pe.transpose(psum[0:n, u % YBANKS, P * k:P * k + P], xT[:, 4 * g + k, a:a + n], ident)
                mm.then_inc(y_tr, 1)

        def final_sp(sp):
            sp.wait_ge(wlo_done, 4 * (g_down(NJ - 1) + 1))
            sp.dma_start(gain_rows, bass.AP(final_g.tensor, final_g.offset, [[0, P], [1, D]])).then_inc(gain_in, 16)
            for tt, (a, n) in enumerate(TILES):
                sp.wait_ge(y_ev, 4 * tt + 4)
                sp.dma_start(y_d[tt], ysb[tt % 3][0:n, :]).then_inc(y_out[tt % 3], 16)
            for i in range(3):
                sp.wait_ge(y_out[i], 16 * len(TILES[i::3]))

        kvf = area(2, 2 * HA * P, at=0)
        kvt = area(2, 2 * DA)
        kv_in = [sem(f"kv_in{i}") for i in range(2)]
        kv_tr = sem("kv_transposed")
        kv_act = sem("kv_copied_act")
        kv_dve = sem("kv_copied_dve")
        kv_st = [sem(f"kv_stored{i}") for i in range(2)]

        def kv_sp(sp):
            sp.wait_ge(o_ready, TB + 1)
            def store(tt):
                a, n = TILES[tt]
                sp.wait_ge(kv_act, 2 * tt + 2)
                sp.wait_ge(kv_dve, tt + 1)
                for i in range(2):
                    sp.dma_start(kv_out[tt][i], kvt[0:n, tt % 2, DA * i:DA * i + DA]).then_inc(kv_st[tt % 2], 16)
            for tt, (a, n) in enumerate(TILES):
                if tt >= 2:
                    sp.wait_ge(kv_tr, 3 * (tt - 1))
                sp.dma_start(kvf[:, tt % 2, :].rearrange("p (m t) -> p m t", t=P)[:, :, 0:n],
                             proj_m[:, OK // P:OU // P, a:a + n]).then_inc(kv_in[tt % 2], 16)
                if tt == 1:
                    pool_sp_in(sp)
                if tt:
                    store(tt - 1)
            store(NTT - 1)

        def kv_bank(tt, b):
            return 4 + (3 * tt + b) % 4

        def kv_pe(pe, tt):
            a, n = TILES[tt]
            pe.wait_ge(kv_in[tt % 2], 16 * (tt // 2 + 1))
            for b in range(3):
                u = 3 * tt + b - 4
                if u >= 0:
                    pe.wait_ge(*((kv_act, 2 * (u // 3) + u % 3 + 1) if u % 3 < 2 else (kv_dve, u // 3 + 1)))
                for k in range(4):
                    m = 4 * b + k
                    mm = pe.transpose(psum[0:n, kv_bank(tt, b), P * k:P * k + P], kvf[:, tt % 2, P * m:P * m + n], ident)
                mm.then_inc(kv_tr, 1)

        def kv_copies(eng, own, banks, tt):
            a, n = TILES[tt]
            for b in banks:
                eng.wait_ge(kv_tr, 3 * tt + b + 1)
                if tt >= 2:
                    eng.wait_ge(kv_st[tt % 2], 32 * (tt // 2))
                dst, src = kvt[0:n, tt % 2, 512 * b:512 * b + 512], psum[0:n, kv_bank(tt, b), :]
                ins = eng.activation(dst, src, ACT.Copy) if own is kv_act else eng.tensor_copy(dst, src)
                ins.then_inc(own, 1)

        def kv_stage_pe(pe):
            pe.wait_ge(in_ev, 2 + G_LAST)
            for q in range(4):
                chunk(pe, G_LAST, 0, q)
                if q == 0:
                    pe.wait_ge(ob_done, 3 * TB + 1)
                kv_pe(pe, q)
            kv_pe(pe, NTT - 1)

        def kv_stage_act(act):
            for q in range(4):
                split_high(act, G_IN, q)
                kv_copies(act, kv_act, (0, 1), q)
            kv_copies(act, kv_act, (0, 1), NTT - 1)

        def kv_stage_dve(dve):
            dve.wait_ge(wlo_done, 4 * G_IN)
            for q in range(4):
                split_low(dve, G_IN, q)
                kv_copies(dve, kv_dve, (2,), q)
            in_copy(dve, G_LAST, 0)
            kv_copies(dve, kv_dve, (2,), NTT - 1)

        NS = UNIQ + 2 * DIL
        k_sb = area(5, DA, at=0)
        v_sb = area(5, DA)
        q_rep = area(2, DA)
        u_sb = area(DA)
        kT9 = area(DA)
        q_tok = area(DA)
        v_new = area(DA)
        junk = u_sb
        o_sb = q_tok
        qf = area(HA, TS)
        kf = area(HA, TS)
        vf = kT9[:, 0:HA * TS].rearrange("p (h t) -> p h t", h=HA)
        qs = qf
        s_dve = area(HA, NS)
        s_all = area(HA * TT)
        s_new = area(HA * TT)
        p_exp = area(DIL, HA * TT)
        p_oth = area(DIL, HA * TT)
        s_max_w = area(P)
        s_max = s_max_w[:, 0:HA * TT]
        s_tmp = area(HA * TT)
        s_tot = area(HA * TT)
        r_own = area(HA)
        r_oth = area(HA)
        diag = area(HA * TT)
        m_col = area(1)
        den_all = area(TB)
        den_tok = area(HA)
        assert pool_at[0] <= GW - 2 * T

        dec_in = sem("decode_inputs_in")
        dec_z = sem("decode_padding_zero")
        dec_q = sem("decode_queries_ready")
        dec_qT = sem("decode_queries_transposed")
        dec_qt = sem("decode_queries_tokenmajor")
        dec_vT = sem("decode_values_transposed")
        dec_vt = sem("decode_values_tokenmajor")
        dec_qd = sem("decode_queries_in_dram")
        dec_qd2 = sem("decode_queries_swapped")
        q_in = sem("decode_query_rows_in")
        k_in = [sem(f"k_in{i}") for i in range(5)]
        v_in = [sem(f"v_in{i}") for i in range(5)]
        k_used = sem("k_block_used")
        k9_used = sem("k_last_block_used")
        v_used = sem("v_block_used")
        kT9_done = sem("k_last_block_copied")
        sl_done = sem("last_scores_done")
        dd = sem("decode_dve_steps")
        mT_done = sem("decode_max_transposed")
        mb_done = sem("decode_max_spread")
        e_done = sem("decode_exp_done")
        den_done = sem("decode_den_done")
        o_ready = sem("decode_out_done")
        ob_done = sem("decode_out_copied")
        ob_out = sem("decode_out_stored")
        DVE_B, AT = 65, {"max": 10, "diag": 12, "arg": 20, "tot": 26, "exp": 29, "u": 65}

        def hb(ap, rows=P):
            return ap.unsqueeze(1).to_broadcast([rows, HA, TT])

        def tb(ap, n=TT, rows=P):
            return ap.unsqueeze(2).to_broadcast([rows, HA, n])

        def v3(ap):
            return ap.rearrange("p (h t) -> p h t", h=HA)

        def dec_sp(sp):
            sp.wait_ge(in_out, 16 * (G_ROW - 2))
            for dst, m in ((qf, 0), (kf, HA), (vf, 2 * HA)):
                sp.dma_start(dst, proj_m[:, m:m + HA, TP:T]).then_inc(dec_in, 16)
            load_group(sp, G_ROW, cols(win_v, G_ROW))
            for j in (0, 1, 2, 3, 9):
                sp.dma_start(k_sb[:, k_slot(j)], cache_rows(ck, 0, j)).then_inc(k_in[k_slot(j)], 16)
            sp.dma_start(v_sb[:, 0], cache_rows(cv, 0, 0)).then_inc(v_in[0], 16)
            sp.wait_ge(dec_qt, 2)
            sp.dma_start(q_d[0], q_tok[0:TS, :]).then_inc(dec_qd, 16)
            sp.wait_ge(dec_qd, 16)
            for s in range(2):
                sp.dma_start(q_d[1].rearrange("(b s q) c -> s b q c", s=2, q=4)[1 - s],
                             q_d[0].rearrange("(b s q) c -> s b q c", s=2, q=4)[s]).then_inc(dec_qd2, 16)
            sp.wait_ge(dec_qd2, 32)
            query_rows(sp, 0)
            load_group(sp, G_ROW + 1, cols(win_v, G_ROW + 1), range(3))

        def query_rows(sp, b):
            for i in range(2):
                qv = q_d[i, bass.ds(b * TT, TT), :]
                src = bass.AP(qv.tensor, qv.offset, [[0, P // TT], [DA, TT], [1, DA]])
                sp.dma_start(q_rep[:, i], src).then_inc(q_in, 16)

        def k_slot(j):
            return 4 if j == 9 else j % 4

        def cache_rows(c, b, j):
            v = c[bass.ds(b, 1)].rearrange("o r c -> (o r) c")
            if j < UNIQ:
                return v[256 * j:256 * j + 256, :].rearrange("(n s) c -> n s c", s=16)[:, 0:TT, :]
            return v[1536 + P * (j - UNIQ):1536 + P * (j - UNIQ + 1), :]

        def dec_sp_b(sp, b, last=False):
            def weights(q, g, src):
                sp.wait_ge(wlo_done, 4 * (g - 1) + q + 1)
                sp.dma_start(w_raw[:, q].rearrange("p (k e) -> p k e", k=4), src(q)).then_inc(raw_in[q], 16)

            g = G_ROW + 2 + b
            src = cols(wo_v, 0) if last else cols(win_v, g)

            def keys(r, j):
                sp.dma_start(k_sb[:, k_slot(j)], cache_rows(ck, r, j)).then_inc(k_in[k_slot(j)], 16)

            def values(r, j):
                sp.dma_start(v_sb[:, j % 5], cache_rows(cv, r, j)).then_inc(v_in[j % 5], 16)

            for j in range(4, 8):
                sp.wait_ge(k_used, 9 * b + j - 3)
                keys(b, j)
            weights(3, g - 1, cols(win_v, g - 1))
            sp.wait_ge(k_used, 9 * b + 5)
            keys(b, 8)
            sp.wait_ge(o_ready, b + 1)
            for j in range(1, 5):
                values(b, j)
            weights(0, g, src)
            if not last:
                for j in range(1, 4):
                    sp.wait_ge(k_used, 9 * b + j + 5)
                    keys(b + 1, j)
                sp.wait_ge(k9_used, b + 1)
                keys(b + 1, 9)
                sp.wait_ge(k_used, 9 * b + 9)
                query_rows(sp, b + 1)
                keys(b + 1, 0)
            weights(1, g, src)
            for j in range(5, 9):
                sp.wait_ge(v_used, UNIQ * b + j - 4)
                values(b, j)
            sp.wait_ge(v_used, UNIQ * b + 5)
            values(b, 9)
            weights(2, g, src)
            if not last:
                sp.wait_ge(v_used, UNIQ * b + 6)
                values(b + 1, 0)
            if last:
                weights(3, g, src)

        def dec_pool_b(pool, b):
            g = G_ROW + b
            for q in range(4):
                split_low(pool, g + 1, q)
            in_store(pool, g)

        def dec_act_scale(act):
            act.wait_ge(dec_in, 48)
            act.activation(qs, qf, ACT.Copy, scale=SCALE_A).then_inc(dec_q, 1)

        def dec_act_copies(act):
            act.wait_ge(dec_qT, 2)
            act.activation(q_tok[0:TS, 0:512], psum[0:TS, 6, :], ACT.Copy).then_inc(dec_qt, 1)
            act.activation(q_tok[0:TS, 512:DA], psum[0:TS, 7, 0:256], ACT.Copy).then_inc(dec_qt, 1)
            act.wait_ge(dec_vT, 2)
            act.activation(v_new[0:TS, 0:512], psum[0:TS, 4, :], ACT.Copy).then_inc(dec_vt, 1)
            act.activation(v_new[0:TS, 512:DA], psum[0:TS, 5, 0:256], ACT.Copy).then_inc(dec_vt, 1)

        def dec_pe(pe):
            pe.wait_ge(in_ev, 2 + G_ROW - 1)
            pe.wait_ge(dec_q, 1)
            for bank, src, done in ((6, qs, dec_qT), (4, vf, dec_vT)):
                for h in range(HA):
                    mm = pe.transpose(psum[0:TS, bank + h // 4, P * (h % 4):P * (h % 4) + P], src[:, h, :], ident)
                    if h in (3, 5):
                        mm.then_inc(done, 1)

        def dec_pe_b(pe, b):
            g = G_ROW + b
            pe.wait_ge(in_ev, 2 + g)
            chunk(pe, g, 0, 0, half=0)
            pe.wait_ge(k_in[4], 16 * b + 16)
            pe.wait_ge(ob_done, 3 * b + 1)
            for h in range(HA):
                mm = pe.transpose(psum[:, 4 + h // 4, P * (h % 4):P * (h % 4) + P], k_sb[:, 4, P * h:P * h + P], ident)
            mm.then_inc(k9_used, 1)
            chunk(pe, g, 0, 0, half=1)
            pe.wait_ge(kT9_done, 2 * b + 2)
            for h in range(HA):
                q8 = qs[:, h, bass.ds(b * TT, TT)]
                pe.matmul(psum[:, 6, TT * h:TT * h + TT], kT9[:, P * h:P * h + P], q8, start=True, stop=True)
                mm = pe.matmul(psum[0:TS, 6, 64 + TT * h:64 + TT * h + TT], kf[:, h, :], q8, start=True, stop=True)
            mm.then_inc(sl_done, 1)
            chunk(pe, g, 0, 1)
            pe.wait_ge(dd, DVE_B * b + AT["max"])
            pe.transpose(psum[:, 7, 0:P], s_max_w, ident).then_inc(mT_done, 1)
            pe.wait_ge(dd, DVE_B * b + AT["diag"])
            pe.matmul(psum[:, 7, P:P + HA * TT], ones[0:HA * TT, :], diag[0:HA * TT, :], start=True, stop=True).then_inc(mb_done, 1)
            chunk(pe, g, 0, 2)
            chunk(pe, g, 0, 3)
            pe.wait_ge(dd, DVE_B * b + AT["exp"])
            pe.matmul(psum[0:HA * TT, 7, 192:193], s_tot, ones[:, 0:1], start=True, stop=False)
            pe.matmul(psum[0:HA * TT, 7, 192:193], s_new[0:TS, :], ones[0:TS, 0:1], start=False, stop=True).then_inc(den_done, 1)
            def weighted(w, v, first=False):
                for h in range(HA):
                    pe.matmul(psum[0:TT, 4 + h // 4, P * (h % 4):P * (h % 4) + P], w[:, TT * h:TT * h + TT], v[:, P * h:P * h + P],
                              start=first and h % 4 == 0, stop=False, skip_group_check=True)

            weighted(s_new[0:TS, :], v_new[0:TS, :], first=True)
            for j in range(DIL):
                pe.wait_ge(v_in[1 + j], 32 * b + 32)
                weighted(p_exp[:, j], v_sb[:, 1 + j])
            pe.wait_ge(v_in[4], 32 * b + 32)
            weighted(s_all, v_sb[:, 4])
            pe.wait_ge(dd, DVE_B * b + AT["u"])
            for bank, h0, h1 in ((4, 0, 4), (5, 4, 6)):
                mm = pe.matmul(psum[0:TT, bank, 0:P * (h1 - h0)], C("is_own"), u_sb[:, P * h0:P * h1], start=False, stop=True,
                               skip_group_check=True)
            mm.then_inc(o_ready, 1)

        def dec_act_b(act, b):
            g = G_ROW + b
            act.wait_ge(k9_used, b + 1)
            act.wait_ge(sl_done, b + 1)
            act.activation(kT9[:, 0:512], psum[:, 4, :], ACT.Copy).then_inc(kT9_done, 1)
            act.activation(kT9[:, 512:DA], psum[:, 5, 0:256], ACT.Copy).then_inc(kT9_done, 1)
            split_high(act, g + 1, 0)
            act.wait_ge(dd, DVE_B * b + AT["arg"])
            act.activation(s_dve, s_dve, ACT.Exp).then_inc(e_done, 1)
            act.activation(s_all, s_all, ACT.Exp).then_inc(e_done, 1)
            act.activation(s_new[0:TS, :], s_new[0:TS, :], ACT.Exp).then_inc(e_done, 1)
            for q in range(1, 4):
                split_high(act, g + 1, q)
            in_copy(act, g, 0)
            act.wait_ge(den_done, b + 1)
            act.activation(den_all[0:HA * TT, bass.ds(b, 1)], psum[0:HA * TT, 7, 192:193], ACT.Copy).then_inc(ob_done, 1)
            act.wait_ge(o_ready, b + 2)
            act.wait_ge(ob_out, 16 * b + 16)
            act.activation(o_sb[0:TT, 0:512], psum[0:TT, 4, :], ACT.Copy).then_inc(ob_done, 1)
            act.activation(o_sb[0:TT, 512:DA], psum[0:TT, 5, 0:256], ACT.Copy).then_inc(ob_done, 1)
            act.wait_ge(ob_done, 3 * b + 4)
            act.dma_start(oa_d[bass.ds(b * TT, TT), :], o_sb[0:TT, :]).then_inc(ob_out, 16)

        def dec_dve_b(dve, b, base):
            st = Steps(dve, dd, base)
            at = {}
            dve.wait_ge(q_in, 32 * b + 32)
            junked = 0
            for j in range(UNIQ + DIL):
                s = k_slot(j)
                dve.wait_ge(k_in[s], (48 if s == 0 else 32) * b + 16 * (j // 4) + 16)
                for i in range(1 if j < UNIQ else 2):
                    col = j + (DIL if i else 0)
                    for h in range(HA):
                        kk = k_sb[:, s, P * h:P * h + P]
                        last = j < UNIQ or i == 1
                        if not last and j == UNIQ:
                            dve.wait_ge(o_ready, b + 1)
                        if not last and j > UNIQ:
                            dve.wait_ge(k_used, 9 * b + j)
                        ins = dve.tensor_tensor_reduce(kk if last else junk[:, P * h:P * h + P], kk, q_rep[:, i, P * h:P * h + P],
                                                       1.0, 0.0, ALU.mult, ALU.add, s_dve[:, h, col:col + 1])
                ins.then_inc(k_used, 1)
            dve.wait_ge(sl_done, b + 2)
            dve.wait_ge(k_used, 9 * b + 9)
            dve.wait_ge(o_ready, b + 1)
            st.done(dve.tensor_tensor(s_dve, s_dve, C("log_dve").unsqueeze(1).to_broadcast([P, HA, NS]), ALU.add))
            st.done(dve.tensor_tensor(v3(s_all), v3(psum[:, 6, 0:48]), hb(C("log_last")), ALU.add))
            st.done(dve.tensor_tensor(v3(s_new[0:TS, :]), v3(psum[0:TS, 6, 64:112]),
                                      hb(C("log_new", TS)[:, bass.ds(b * TT, TT)], TS), ALU.add))
            st.wait(1)
            st.done(dve.tensor_reduce(r_own, s_dve[:, :, 0:9], AX.X, ALU.max))
            st.done(dve.tensor_reduce(r_oth, s_dve[:, :, 9:NS], AX.X, ALU.max))
            st.last()
            st.done(dve.tensor_tensor(v3(s_max), tb(r_own), hb(C("neg_own")), ALU.add))
            st.done(dve.tensor_tensor(v3(s_tmp), tb(r_oth), hb(C("neg_oth")), ALU.add))
            st.last()
            st.done(dve.tensor_tensor(s_max, s_max, s_tmp, ALU.max))
            st.last()
            st.done(dve.tensor_tensor(s_max, s_max, s_all, ALU.max))
            st.last()
            at["max"] = st.done(dve.tensor_tensor(s_max[0:TS, :], s_max[0:TS, :], s_new[0:TS, :], ALU.max))
            dve.wait_ge(mT_done, b + 1)
            st.done(dve.tensor_reduce(m_col[0:48, :], psum[0:48, 7, 0:P], AX.X, ALU.max))
            st.last()
            at["diag"] = st.done(dve.tensor_scalar(diag[0:48, :], ident[0:48, 0:48], m_col[0:48, 0:1], -1.0, ALU.mult, ALU.mult))
            dve.wait_ge(mb_done, b + 1)
            mb = psum[:, 7, P:P + 48]
            st.done(dve.tensor_tensor(s_all, s_all, mb, ALU.add))
            st.done(dve.tensor_tensor(s_new[0:TS, :], s_new[0:TS, :], mb[0:TS, :], ALU.add))
            st.done(dve.tensor_tensor(v3(s_tmp), v3(mb), hb(C("is_own")), ALU.mult))
            st.done(dve.tensor_tensor(v3(s_tot), v3(mb), hb(C("is_oth")), ALU.mult))
            st.last()
            st.done(dve.tensor_reduce(r_own, v3(s_tmp), AX.X, ALU.add))
            st.done(dve.tensor_reduce(r_oth, v3(s_tot), AX.X, ALU.add))
            st.last()
            st.done(dve.tensor_tensor(s_dve[:, :, 0:9], s_dve[:, :, 0:9], tb(r_own, 9), ALU.add))
            at["arg"] = st.done(dve.tensor_tensor(s_dve[:, :, 9:NS], s_dve[:, :, 9:NS], tb(r_oth, 3), ALU.add))
            dve.wait_ge(e_done, 3 * b + 3)
            st.last()
            st.done(dve.tensor_reduce(r_own, s_dve[:, :, 0:9], AX.X, ALU.add))
            st.done(dve.tensor_reduce(r_oth, s_dve[:, :, 9:NS], AX.X, ALU.add))
            st.last()
            st.done(dve.tensor_tensor(v3(s_tmp), tb(r_own), hb(C("is_own")), ALU.mult))
            st.done(dve.tensor_tensor(v3(s_tot), tb(r_oth), hb(C("is_oth")), ALU.mult))
            st.last()
            st.done(dve.tensor_tensor(s_tot, s_tot, s_tmp, ALU.add))
            st.last()
            at["tot"] = st.done(dve.tensor_tensor(s_tot, s_tot, s_all, ALU.add))
            pj = lambda a: a.rearrange("p j (h t) -> p j h t", h=HA)
            wj = lambda a: a.rearrange("p h j -> p j h").unsqueeze(3).to_broadcast([P, DIL, HA, TT])
            sel = lambda name: C(name).unsqueeze(1).unsqueeze(1).to_broadcast([P, DIL, HA, TT])
            st.done(dve.tensor_tensor(pj(p_exp), wj(s_dve[:, :, UNIQ:UNIQ + DIL]), sel("is_own"), ALU.mult))
            st.done(dve.tensor_tensor(pj(p_oth), wj(s_dve[:, :, UNIQ + DIL:NS]), sel("is_oth"), ALU.mult))
            st.last()
            at["exp"] = st.done(dve.tensor_tensor(p_exp, p_exp, p_oth, ALU.add))
            prev = {}
            for j in range(UNIQ):
                dve.wait_ge(v_in[j % 5], 32 * b + 16 * (j // 5) + 16)
                for h in range(HA):
                    w = s_dve[:, h, j:j + 1]
                    u, v = u_sb[:, P * h:P * h + P], v_sb[:, j % 5, P * h:P * h + P]
                    if j == 0:
                        ins = dve.tensor_scalar(u, v, w, None, ALU.mult)
                    else:
                        st.wait(prev[h])
                        ins = dve.scalar_tensor_tensor(out=u, in0=v, scalar=w, in1=u, op0=ALU.mult, op1=ALU.add)
                    prev[h] = st.done(ins)
                st.last()
                dve.sem_inc(v_used, 1)
            at["u"] = st.n
            assert st.n == DVE_B and at == AT, (st.n, at)

        dt_in = sem("decode_results_in")
        dt_div = sem("decode_divided")
        dt_tr = sem("decode_results_transposed")
        dt_hi = sem("decode_results_high")
        dt_lo = sem("decode_results_low")
        dt_out = sem("decode_den_stored")
        o_tok = v_new

        def dtail_sp(sp, part):
            if part == 0:
                sp.wait_ge(ob_done, 3 * TB + 1)
                with nc.allow_non_contiguous_dma(reason="384 denominators"):
                    for h in range(HA):
                        sp.dma_start(den_d[h].rearrange("(b t) -> t b", t=TT), den_all[TT * h:TT * h + TT, :]).then_inc(dt_out, 16)
                return
            sp.wait_ge(dt_out, 16 * HA)
            sp.wait_ge(ob_out, 16 * TB + 16)
            sp.dma_start(o_tok[0:TS, :], oa_d).then_inc(dt_in, 16)
            with nc.allow_non_contiguous_dma(reason="384 denominators"):
                sp.dma_start(den_tok[0:TS, :], den_d.rearrange("h c -> c h")).then_inc(dt_in, 16)

        def dtail_dve(dve):
            dve.wait_ge(dt_in, 32)
            dve.reciprocal(den_tok[0:TS, :], den_tok[0:TS, :]).then_inc(dt_div, 1)
            dve.wait_ge(dt_div, 1)
            o3 = o_tok[0:TS, :].rearrange("p (h d) -> p h d", h=HA)
            dve.tensor_tensor(o3, o3, den_tok[0:TS, :].unsqueeze(2).to_broadcast([TS, HA, HD]), ALU.mult).then_inc(dt_div, 1)
            dve.wait_ge(dt_hi, 1)
            dve.tensor_tensor(lo[:, 0:HA, TP:T], psum[:, 4, 0:HA * TS].rearrange("p (h t) -> p h t", h=HA),
                              hi[:, 0:HA, TP:T].bitcast(F32), ALU.subtract).then_inc(dt_lo, 1)

        def dtail_pe(pe):
            pe.wait_ge(dt_div, 2)
            pe.wait_ge(kv_act, 9)
            for h in range(HA):
                mm = pe.transpose(psum[:, 4, TS * h:TS * h + TS], o_tok[0:TS, P * h:P * h + P], ident[0:TS, 0:TS])
            mm.then_inc(dt_tr, 1)

        def dtail_act(act):
            act.wait_ge(dt_tr, 1)
            act.activation(hi[:, 0:HA, TP:T], psum[:, 4, 0:HA * TS].rearrange("p (h t) -> p h t", h=HA), ACT.Copy).then_inc(dt_hi, 1)

        NU = HA * 4
        qk = area(2, 2, TP, at=0)
        pr = area(2, TP)
        pT = area(2, TP)
        vp = area(4, DA)
        mx = area(2)
        dn = area(2)
        pa_v = sem("prompt_values_in")
        pa_in = [sem(f"prompt_qk_in{i}") for i in range(2)]
        pa_s = sem("prompt_scores_done")
        pa_m = sem("prompt_max_done")
        pa_e = sem("prompt_exp_done")
        pa_n = sem("prompt_probs_done")
        pa_t = sem("prompt_probs_transposed")
        pa_c = sem("prompt_probs_copied")
        pa_o = sem("prompt_out_done")
        pa_hi = sem("prompt_out_high")
        pa_lo = sem("prompt_out_low")

        def pa_sp(sp):
            sp.wait_ge(kv_tr, 3 * NTT)
            for h in range(HA):
                if h >= 2:
                    sp.wait_ge(pa_s, 4 * (h - 1))
                for i in range(2):
                    sp.dma_start(qk[:, h % 2, i, :], proj_m[:, HA * i + h, 0:TP]).then_inc(pa_in[h % 2], 16)
                if h == 1:
                    sp.wait_ge(kv_st[0], 32 * 3)
                    sp.wait_ge(kv_st[1], 32 * 2)
                    sp.dma_start(vp, pv.rearrange("(n p) c -> p n c", p=P)).then_inc(pa_v, 16)

        def pa_pe(pe):
            def scores(u):
                h, i = divmod(u, 4)
                pe.wait_ge(pa_in[h % 2], 32 * (h // 2 + 1))
                if u >= 2:
                    pe.wait_ge(pa_m, 2 * (u - 1))
                pe.matmul(psum[:, 2 + u % 2, 0:P * (i + 1)], qk[:, h % 2, 0, P * i:P * i + P], qk[:, h % 2, 1, 0:P * (i + 1)],
                          start=True, stop=True).then_inc(pa_s, 1)

            def turn(u):
                i = u % 4
                pe.wait_ge(pa_n, 2 * u + 2)
                if u >= 2:
                    pe.wait_ge(pa_c, u - 1)
                for j in range(i + 1):
                    mm = pe.transpose(psum[:, 4 + u % 2, P * j:P * j + P], pr[:, u % 2, P * j:P * j + P], ident)
                mm.then_inc(pa_t, 1)

            def out(u):
                h, i = divmod(u, 4)
                pe.wait_ge(pa_c, u + 1)
                if u == 0:
                    pe.wait_ge(pa_v, 16)
                if u >= 2:
                    pe.wait_ge(pa_lo, u - 1)
                for j in range(i + 1):
                    mm = pe.matmul(psum[:, 6 + u % 2, 0:P], vp[:, j, P * h:P * h + P], pT[:, u % 2, P * j:P * j + P],
                                   start=j == 0, stop=j == i)
                mm.then_inc(pa_o, 1)

            pe.wait_ge(in_ev, 2 + G_IN)
            pe.wait_ge(dt_lo, 1)
            pe.wait_ge(pl_hc, 1)
            pe.wait_ge(pl_rc, 2)
            for u in range(NU + 2):
                if u < NU:
                    scores(u)
                if u >= 2:
                    out(u - 2)
                if u < KT - HA:
                    ga_pe(pe, HA + u)
                if 1 <= u <= NU:
                    turn(u - 1)

        def pa_act(act):
            act.wait_ge(kv_st[0], 32 * 3)
            act.wait_ge(kv_st[1], 32 * 2)
            for u in range(NU + 2):
                if u < NU:
                    n = P * (u % 4 + 1)
                    act.wait_ge(pa_m, 2 * u + 2)
                    act.activation(pr[:, u % 2, 0:n], pr[:, u % 2, 0:n], ACT.Exp, bias=mx[:, u % 2:u % 2 + 1],
                                   accum_out=dn[:, u % 2:u % 2 + 1]).then_inc(pa_e, 1)
                if u >= 2:
                    w = u - 2
                    h, i = divmod(w, 4)
                    act.wait_ge(pa_o, w + 1)
                    act.activation(hi[:, h, P * i:P * i + P], psum[:, 6 + w % 2, 0:P], ACT.Copy).then_inc(pa_hi, 1)
                if 1 <= u <= NU:
                    w = u - 1
                    n = P * (w % 4 + 1)
                    act.wait_ge(pa_t, w + 1)
                    if w >= 2:
                        act.wait_ge(pa_o, w - 1)
                    act.activation(pT[:, w % 2, 0:n], psum[:, 4 + w % 2, 0:n], ACT.Copy).then_inc(pa_c, 1)

        def pa_dve(dve):
            for u in range(NU + 3):
                if u < NU:
                    n = P * (u % 4 + 1)
                    dve.wait_ge(pa_s, u + 1)
                    if u >= 2:
                        dve.wait_ge(pa_t, u - 1)
                    dve.tensor_tensor_reduce(pr[:, u % 2, 0:n], psum[:, 2 + u % 2, 0:n], C("mask_a")[:, TP - n:TP], SCALE_A, NEG,
                                             ALU.add, ALU.max, mx[:, u % 2:u % 2 + 1]).then_inc(pa_m, 1)
                    dve.wait_ge(pa_m, 2 * u + 1)
                    dve.tensor_scalar(mx[:, u % 2:u % 2 + 1], mx[:, u % 2:u % 2 + 1], -1.0, None, ALU.mult).then_inc(pa_m, 1)
                if 1 <= u <= NU:
                    w = u - 1
                    n = P * (w % 4 + 1)
                    dve.wait_ge(pa_e, w + 1)
                    dve.reciprocal(dn[:, w % 2:w % 2 + 1], dn[:, w % 2:w % 2 + 1]).then_inc(pa_n, 1)
                    dve.wait_ge(pa_n, 2 * w + 1)
                    dve.tensor_scalar(pr[:, w % 2, 0:n], pr[:, w % 2, 0:n], dn[:, w % 2:w % 2 + 1], None, ALU.mult).then_inc(pa_n, 1)
                if u >= 3:
                    w = u - 3
                    h, i = divmod(w, 4)
                    dve.wait_ge(pa_hi, w + 1)
                    dve.tensor_tensor(lo[:, h, P * i:P * i + P], psum[:, 6 + w % 2, 0:P],
                                      hi[:, h, P * i:P * i + P].bitcast(F32), ALU.subtract).then_inc(pa_lo, 1)

        UW = PBUF + TP
        us = TT + PBUF
        ub = area(NPOOL, UW, at=pool_at[0])
        ubs = area(NPOOL, TB, us)
        hist = area(DB)
        pool_at[0] -= DB
        acc = area(2, UW)
        accs = area(2, TB, us)
        ptmp = area(2, T)
        wp = area(NPOOL, P)
        ptmp_s = area(NPOOL, TS)
        rows_out = area(2, DB)
        cnt_tmp = area(16)
        pl_in = sem("pool_inputs_in")
        pl_hist = sem("pool_history_transposed")
        pl_hc = sem("pool_history_copied")
        pl_d = sem("pooling_steps")
        pl_mm = sem("pool_product_done")
        pl_sc = sem("pool_scaled")
        pl_hi = sem("pool_high")
        pl_lo = sem("pool_low")
        pl_ro = sem("pool_rows_transposed")
        pl_done = sem("pool_group_pooled")
        pl_rc = sem("pool_rows_copied")
        pl_out = sem("pool_rows_stored")

        def pool_sp_in(sp):
            for g in range(NPOOL):
                sp.dma_start(ub[:, g, PBUF:UW], proj_m[:, OU // P + g, 0:TP]).then_inc(pl_in, 16)
                sp.dma_start(ptmp_s[:, g, :], proj_m[:, OU // P + g, TP:T]).then_inc(pl_in, 16)
            sp.dma_start(wp, w_pool[0].rearrange("g c d -> c g d")).then_inc(pl_in, 16)
            sp.dma_start(hist[0:TB * PBUF, :], state_pool[0].rearrange("b r c -> (b r) c")).then_inc(pl_in, 16)
            sp.dma_start(o_sp[0, :, 0:PBUF - TT, :], state_pool[0, :, TT:PBUF, :]).then_inc(pl_out, 16)

        def pool_sp(sp):
            sp.wait_ge(pl_rc, 2)
            sp.dma_start(o_pp[0, 0], rows_out[0:PBUF, 0, :]).then_inc(pl_out, 16)
            sp.dma_start(o_sp[0, :, PBUF - TT:PBUF, :], rows_out[0:TS, 1, :]).then_inc(pl_out, 16)

        POOL_IN = 16 * (2 * NPOOL + 2)

        def pool_pe_turn(pe):
            pe.wait_ge(pl_in, POOL_IN)
            pe.wait_ge(kv_act, 10)
            pe.wait_ge(kv_dve, 5)
            for g in range(NPOOL):
                mm = pe.transpose(psum[:, 2, P * g:P * g + TB * PBUF], hist[0:TB * PBUF, P * g:P * g + P], ident[0:TB * PBUF, 0:TB * PBUF])
            mm.then_inc(pl_hist, 1)
            for g in range(NPOOL):
                mm = pe.transpose(psum[0:PBUF, 3, P * g:P * g + P], ub[:, g, TP:UW], ident)
            mm.then_inc(pl_ro, 1)
            for g in range(NPOOL):
                mm = pe.transpose(psum[0:TS, 5, P * g:P * g + P], ptmp_s[:, g, :], ident)
            mm.then_inc(pl_ro, 1)

        def pool_act_turned(act):
            act.wait_ge(pl_hist, 1)
            act.activation(ubs[:, :, :, 0:PBUF], psum[:, 2, :].rearrange("p (g c) -> p g c", g=NPOOL)[:, :, 0:TB * PBUF]
                           .rearrange("p g (b r) -> p g b r", r=PBUF), ACT.Copy).then_inc(pl_hc, 1)
            act.wait_ge(pl_ro, 1)
            act.wait_ge(in_out, 16 * G_IN)
            act.activation(rows_out[0:PBUF, 0, :], psum[0:PBUF, 3, :], ACT.Copy).then_inc(pl_rc, 1)
            act.wait_ge(pl_ro, 2)
            act.activation(rows_out[0:TS, 1, :], psum[0:TS, 5, :], ACT.Copy).then_inc(pl_rc, 1)

        def pool_pe(pe):
            pe.wait_ge(pa_lo, NU)
            pe.wait_ge(pa_c, NU)
            for g in range(NPOOL):
                b = 4 + 2 * (g % 2)
                pe.wait_ge(pl_done, g + 1)
                if g >= 2:
                    pe.wait_ge(pl_sc, 2 * (g - 1))
                pe.matmul(psum[:, b, :], wp[:, g, :], ub[:, g, PBUF:UW], start=True, stop=True)
                pe.matmul(psum[:, b + 1, 0:TS], wp[:, g, :], ptmp_s[:, g, :], start=True, stop=True).then_inc(pl_mm, 1)

        def pool_gp(pool):
            st = Steps(pool, pl_d)
            pool.wait_ge(in_out, 16 * G_IN)
            pool.wait_ge(pl_in, POOL_IN)
            st.done(pool.memset(ub[:, :, 0:PBUF], 0.0))
            for g in range(NPOOL):
                st.done(pool.tensor_copy(ubs[:, g, :, PBUF:us], ptmp_s[:, g, :].rearrange("p (b t) -> p b t", t=TT)))
            pool.wait_ge(pl_hc, 1)
            pool.wait_ge(pl_ro, 2)
            for g in range(NPOOL):
                w = 2 << g
                a, s = ub[:, g, :], ubs[:, g]
                for lev in range(g + 1):
                    sh = 1 << lev
                    first = 2 * sh - 1
                    st.last()
                    na, ns = acc[:, lev % 2, :], accs[:, lev % 2]
                    st.done(pool.tensor_tensor(na[:, first:UW], a[:, first:UW], a[:, first - sh:UW - sh], ALU.add))
                    st.done(pool.tensor_tensor(ns[:, :, first:us], s[:, :, first:us], s[:, :, first - sh:us - sh], ALU.add))
                    a, s = na, ns
                st.last()
                st.done(pool.tensor_tensor(cnt_tmp, a[:, PBUF:PBUF + 16], C("inv_count")[:, 16 * g:16 * g + 16], ALU.mult))
                st.done(pool.tensor_scalar(a[:, PBUF + 16:UW], a[:, PBUF + 16:UW], 1.0 / w, None, ALU.mult))
                st.done(pool.tensor_scalar(s[:, :, PBUF:us], s[:, :, PBUF:us], 1.0 / w, None, ALU.mult))
                st.last()
                x = ub[:, g, :]
                st.done(pool.tensor_tensor(x[:, PBUF:PBUF + 16], cnt_tmp, x[:, PBUF:PBUF + 16], ALU.subtract))
                st.done(pool.tensor_tensor(x[:, PBUF + 16:UW], a[:, PBUF + 16:UW], x[:, PBUF + 16:UW], ALU.subtract))
                st.done(pool.tensor_tensor(ptmp_s[:, g, :].rearrange("p (b t) -> p b t", t=TT), s[:, :, PBUF:us], ubs[:, g, :, PBUF:us], ALU.subtract))
                st.last()
                pool.sem_inc(pl_done, 1)
            for g in range(NPOOL):
                pool.wait_ge(pl_hi, g + 1)
                pool.tensor_tensor(lo[:, MIX_B + g, :], ptmp[:, g % 2], hi[:, MIX_B + g, :].bitcast(F32), ALU.subtract).then_inc(pl_lo, 1)

        def pool_act(act):
            for g in range(NPOOL):
                b = 4 + 2 * (g % 2)
                act.wait_ge(pl_mm, g + 1)
                if g >= 2:
                    act.wait_ge(pl_lo, g - 1)
                act.activation(ptmp[:, g % 2, 0:TP], psum[:, b, :], ACT.Copy, scale=GS[:, g:g + 1]).then_inc(pl_sc, 1)
                act.activation(ptmp[:, g % 2, TP:T], psum[:, b + 1, 0:TS], ACT.Copy, scale=GS[:, g:g + 1]).then_inc(pl_sc, 1)
                act.wait_ge(pl_sc, 2 * g + 2)
                act.activation(hi[:, MIX_B + g, :], ptmp[:, g % 2], ACT.Copy).then_inc(pl_hi, 1)

        rcf = [area(6, P, at=0)]
        qkv = area(12, P)
        gg = area(NTT, CK)
        shared = pool_at[0]
        az = area(NTT, CK)
        gjunk = area(CV, at=shared)
        out6 = area(6, P)
        rcf.append(area(6, P))
        assert pool_at[0] >= shared + NTT * CK
        eb = area(CK)
        enb = area(CK)
        ebd = area(CK)
        qe = area(CK)
        ke = area(CK)
        kd = area(CK)
        vt = area(CV)
        qeT = area(HC, P)
        keT = area(HC, P)
        am = area(HC, P)
        S = area(5, CV)
        qd = S[:, 2:5, :].rearrange("p a b -> p (a b)").rearrange("p (h t) -> p h t", h=HC)
        ebl = area(32)
        rs = area(HC)
        kdm = gg[:, 0:4, :].rearrange("p (a b) e -> p a (b e)", b=2)[:, :, 0:CK]
        w_free = w_raw.rearrange("p a b -> p (a b)")
        s0 = [w_free[:, 0:CV], w_free[:, CV:2 * CV]]
        s0 += [g_sb[:, 6 * P + CV * i:6 * P + CV * (i + 1)] for i in range(2)]
        sn = w_free[:, 2 * CV:4 * CV].rearrange("p (a b) -> p a b", a=2)
        wg2 = sn[:, 0, 0:CK]
        oc = w_free[:, 4 * CV:5 * CV]
        am_s = w_free[:, 5 * CV:5 * CV + HC * TS].rearrange("p (h t) -> p h t", h=HC)

        gl_w = sem("gla_gate_weights_in")
        qkv_in = sem("gla_qkv_in")
        rc_in = [sem(f"gla_output_gates_in{i}") for i in range(2)]
        gl_z0 = sem("gla_zeros_done")
        gp = sem("gla_pe_steps")
        ga_ = sem("gla_act_steps")
        gv = sem("gla_dve_steps")
        s0_in = [sem(f"gla_state_in{i}") for i in range(4)]
        sn_out = [sem(f"gla_state_stored{i}") for i in range(2)]
        pg_out = sem("gla_prompt_state_stored")
        s_mix = sem("mix_split")

        NT = NTT
        GP, GA, GV = {}, {}, {}

        def gla_names():
            def number(names, into):
                n = 0
                for name in names:
                    n += 1
                    into[name] = n
            tiles = range(NT)
            pe_n = [(tt, "z") for tt in tiles] + [(0, "qk"), (0, "sums")]
            act_n = [(tt, x) for x in ("e", "l") for tt in tiles] + [(0, x) for x in ("ebl", "eb", "enb", "ebd")]
            dve_n = [(tt, x) for tt in tiles for x in ("zs", "az")] + [(tt, "g") for tt in tiles] + [(0, x) for x in ("qe", "ke", "kd")]
            for tt in tiles:
                smp = tt == NT - 1
                pe_n += [(tt, "turn"), (tt, "v"), (tt, "scores")]
                act_n += [(tt, "qeT"), (tt, "keT"), (tt, "v0"), (tt, "v1")]
                dve_n += [(tt, "mask")]
                before = [(tt - 1, "rs"), (tt - 1, "on")] if tt else []
                gated = [(tt - 1, "out", m) for m in range(6)] if tt else []
                if tt:
                    act_n += [(tt - 1, "sq", h) for h in range(HC)] + [(tt - 1, "rms")]
                act_n += [(tt, "silu")]
                if not smp:
                    act_n += [(tt + 1, x) for x in ("ebl", "eb", "enb", "ebd")]
                if tt:
                    act_n += [(tt - 1, "hi")]
                if smp:
                    pe_n += [(tt, "intra")]
                    dve_n += [(tt, "qd")]
                    for b in range(TB):
                        pe_n += [(tt, "state", b), (tt, "inter", b)] + ([(tt - 1, "oT")] if b == 0 else [])
                        dve_n += [(tt, "kdm", 0)] if b == 0 else []
                        dve_n += [(tt, "kdm", b + 1)] if b + 1 < TB else []
                        dve_n += before if b == 0 else gated if b == 1 else [(tt - 1, "lo")] if b == 2 else []
                        dve_n += [(tt, "S", b, h) for h in range(HC)]
                else:
                    for c in range(4):
                        dve_n += [(tt, "S", c, h) for h in range(HC)] + (before if c == 1 else [])
                    pe_n += [(tt, "state", c) for c in range(4)] + [(tt + 1, "qk"), (tt + 1, "sums")]
                    pe_n += ([(tt - 1, "oT")] if tt else []) + [(tt, "out")]
                    dve_n += gated + [(tt + 1, x) for x in ("qe", "ke", "kd")]
                dve_n += [(tt, "oc", 0), (tt, "oc", 1)]
                if tt and not smp:
                    dve_n += [(tt - 1, "lo")]
            last = NT - 1
            pe_n += [(last, "oT")]
            act_n += [(last, "sq", h) for h in range(HC)] + [(last, "rms"), (last, "hi")]
            dve_n += [(last, "rs"), (last, "on")] + [(last, "out", m) for m in range(6)] + [(last, "lo")]
            number(pe_n, GP)
            number(act_n, GA)
            number(dve_n, GV)

        gla_names()

        class Named:

            def __init__(self, eng, sem_, table_):
                self.eng, self.sem, self.table, self.n = eng, sem_, table_, 0

            def done(self, ins, *name):
                self.n += 1
                assert self.table[name] == self.n, (name, self.n, self.table[name])
                ins.then_inc(self.sem, 1)

            def after_pe(self, *name):
                self.eng.wait_ge(gp, GP[name])

            def after_act(self, *name):
                self.eng.wait_ge(ga_, GA[name])

            def after_dve(self, *name):
                self.eng.wait_ge(gv, GV[name])

        def sfx(tt):
            return "_s" if tt == NT - 1 else "_p"

        def gla_sp_early(sp):
            sp.wait_ge(wlo_done, 4 * G_IN + 4)
            sp.dma_start(wg2[0:RANK, :], w_gate2[0]).then_inc(gl_w, 16)
            sp.dma_start(wg2[RANK:RANK + 1, :], b_gate).then_inc(gl_w, 16)
            for b in range(2):
                gla_state(sp, b)

        def gla_sp(sp):
            sp.wait_ge(pa_lo, NU)
            sp.wait_ge(in_out, 16 * G_IN)
            for tt, (a, n) in enumerate(TILES):
                if tt:
                    sp.wait_ge(gp, GP[tt - 1, "v"])
                sp.dma_start(qkv[:, :, 0:n], proj_m[:, OQC // P:ORC // P, a:a + n]).then_inc(qkv_in, 16)
                if tt == 1:
                    sp.wait_ge(gv, GV[NT - 1, "g"])
                if tt >= 2:
                    sp.wait_ge(gv, GV[tt - 2, "out", 5])
                sp.dma_start(rcf[tt % 2][:, :, 0:n], proj_m[:, ORC // P:OGA // P, a:a + n]).then_inc(rc_in[tt % 2], 16)
            sp.wait_ge(gp, GP[NT - 1, "v"])
            for b in range(2, 4):
                gla_state(sp, b)
            for b in range(TB):
                gla_store(sp, b)
                if b + 4 < TB:
                    sp.wait_ge(gp, GP[NT - 1, "inter", b])
                    gla_state(sp, b + 4)
                if b == 0:
                    last = S[0:DK, 16 % 5, :].rearrange("p (h v) -> p h v", h=HC)
                    sp.dma_start(o_pg[0, 0].rearrange("h k v -> k h v"), last).then_inc(pg_out, 16)

        def gla_state(sp, b):
            sp.dma_start(s0[b % 4][0:DK, :].rearrange("p (h v) -> p h v", h=HC), state_gla[0, b].rearrange("h k v -> k h v")).then_inc(s0_in[b % 4], 16)

        def gla_store(sp, b):
            sp.wait_ge(gv, GV[4, "S", b, HC - 1])
            sp.dma_start(o_sg[0, b].rearrange("h k v -> k h v"), sn[0:DK, b % 2, :].rearrange("p (h v) -> p h v", h=HC)).then_inc(sn_out[b % 2], 16)

        ubanks = ((7, 0), (5, 6))

        def gla_pe_sums(pe, nd, tt):
            a, n = TILES[tt]
            nch = TB if tt == NT - 1 else 4
            pe.wait_ge(qkv_in, 16 * tt + 16)
            if tt:
                nd.after_dve(tt - 1, "S", 2, HC - 1)
            for m in range(6):
                dst = psum[0:n, 0, P * m:P * m + P] if m < 3 else psum[0:n, 7, P * (m - 2):P * (m - 1)]
                mm = pe.transpose(dst, qkv[:, m, 0:n], ident)
            nd.done(mm, tt, "qk")
            nd.after_dve(tt, "g")
            if tt:
                nd.after_dve(tt - 1, "S", 3, HC - 1)
            pe.matmul(psum[0:n, 5, 0:CK], C("upto" + sfx(tt), n), gg[0:n, tt, :], start=True, stop=True)
            pe.matmul(psum[0:n, 6, 0:CK], C("after" + sfx(tt), n), gg[0:n, tt, :], start=True, stop=True)
            for h in range(HC):
                mm = pe.matmul(psum[0:DK, 7, nch * h:nch * h + nch], gg[0:n, tt, DK * h:DK * h + DK], C("chunk" + sfx(tt), n), start=True, stop=True)
            nd.done(mm, tt, "sums")

        def gla_pe_turn_out(pe, nd, tt):
            n = TILES[tt][1]
            nd.after_dve(tt, "on")
            for m in range(6):
                mm = pe.transpose(psum[:, 1 + m // 4, P * (m % 4):P * (m % 4) + n], oc[0:n, P * m:P * m + P], ident[0:n, 0:n])
            nd.done(mm, tt, "oT")

        def gla_pe_gates(pe, nd):
            pe.wait_ge(gl_w, 32)
            pe.wait_ge(s_gT, 1)
            pe.wait_ge(pa_m, 2 * NU)
            for tt, (a, n) in enumerate(TILES):
                if tt >= 4:
                    nd.after_dve(tt - 4, "zs")
                nd.done(pe.matmul(psum[0:n, tt % 4, 0:CK], gaT[0:RANK + 1, a:a + n], wg2[0:RANK + 1, :], start=True, stop=True), tt, "z")

        def gla_pe(pe, nd):
            nd.after_dve(NT - 1, "zs")
            pe.wait_ge(pl_sc, 2 * NPOOL)
            gla_pe_sums(pe, nd, 0)
            for tt, (a, n) in enumerate(TILES):
                smp = tt == NT - 1
                nd.after_dve(tt, "kd")
                nd.after_act(tt, "ebd")
                for b, src in ((0, qe), (5, ke)):
                    for h in range(HC):
                        mm = pe.transpose(psum[0:DK, b, P * h:P * h + n], src[0:n, DK * h:DK * h + DK], ident[0:n, 0:n])
                nd.done(mm, tt, "turn")
                if tt:
                    nd.after_dve(tt - 1, "oc", 1)
                for m in range(6):
                    mm = pe.transpose(psum[0:n, 3 + m // 4, P * (m % 4):P * (m % 4) + P], qkv[:, 6 + m, 0:n], ident)
                nd.done(mm, tt, "v")
                nd.after_act(tt, "keT")
                for h in range(HC):
                    mm = pe.matmul(psum[0:n, 6, P * h:P * h + n], keT[0:DK, h, 0:n], qeT[0:DK, h, 0:n], start=True, stop=True)
                nd.done(mm, tt, "scores")
                nd.after_act(tt, "v1")

                def intra():
                    nd.after_dve(tt, "mask")
                    for h in range(HC):
                        mm = pe.matmul(psum[0:n, 3 + h // 2, DV * (h % 2):DV * (h % 2) + DV], (am_s if smp else am)[0:n, h, 0:n],
                                       vt[0:n, DV * h:DV * h + DV], start=h % 2 == 0, stop=False, skip_group_check=True)
                    return mm

                if smp:
                    nd.done(intra(), tt, "intra")
                    for b in range(TB):
                        r = slice(32 * (b // 4), 32 * (b // 4) + 32)
                        nd.after_dve(tt, "kdm", b)
                        if b >= 2:
                            nd.after_dve(tt, "S", b - 2, HC - 1)
                        for h in range(HC):
                            mm = pe.matmul(psum[0:DK, ubanks[b % 2][h // 2], DV * (h % 2):DV * (h % 2) + DV],
                                           kdm[r, b % 2, DK * h:DK * h + DK], vt[r, DV * h:DV * h + DV], start=True, stop=True)
                        nd.done(mm, tt, "state", b)
                        nd.after_dve(tt, "qd")
                        pe.wait_ge(s0_in[b % 4], 16 * (b // 4) + 16)
                        for h in range(HC):
                            mm = pe.matmul(psum[r, 3 + h // 2, DV * (h % 2):DV * (h % 2) + DV], qd[0:DK, h, TS * b + r.start:TS * b + r.stop],
                                           s0[b % 4][0:DK, DV * h:DV * h + DV], start=False, stop=b % 4 == 3, skip_group_check=True)
                        nd.done(mm, tt, "inter", b)
                        if b == 0:
                            gla_pe_turn_out(pe, nd, tt - 1)
                else:
                    for c in range(4):
                        if c == 1:
                            intra()
                        if c >= 2:
                            nd.after_dve(tt, "S", c - 2, HC - 1)
                        r = slice(CHUNK_P * c, CHUNK_P * c + CHUNK_P)
                        for h in range(HC):
                            mm = pe.matmul(psum[0:DK, ubanks[c % 2][h // 2], DV * (h % 2):DV * (h % 2) + DV],
                                           kd[r, DK * h:DK * h + DK], vt[r, DV * h:DV * h + DV], start=True, stop=True)
                        nd.done(mm, tt, "state", c)
                    gla_pe_sums(pe, nd, tt + 1)
                    if tt:
                        gla_pe_turn_out(pe, nd, tt - 1)
                    for c in range(4):
                        if c:
                            nd.after_dve(tt, "S", c - 1, HC - 1)
                        r = slice(CHUNK_P * c, CHUNK_P * c + CHUNK_P)
                        for h in range(HC):
                            mm = pe.matmul(psum[r, 3 + h // 2, DV * (h % 2):DV * (h % 2) + DV], qeT[0:DK, h, r],
                                           S[0:DK, (4 * tt + c) % 5, DV * h:DV * h + DV], start=False, stop=True, skip_group_check=True)
                    nd.done(mm, tt, "out")
            gla_pe_turn_out(pe, nd, NT - 1)

        def gla_act(act, nd):
            for tt, (a, n) in enumerate(TILES):
                nd.after_dve(tt, "az")
                nd.done(act.activation(az[0:n, tt, :], az[0:n, tt, :], ACT.Exp, scale=-1.0), tt, "e")
            for tt, (a, n) in enumerate(TILES):
                act.wait_ge(ga_, GA[tt, "e"])
                nd.done(act.activation(az[0:n, tt, :], az[0:n, tt, :], ACT.Ln, bias=ones[0:n, 0:1]), tt, "l")

            def decays(tt):
                n = TILES[tt][1]
                nch = TB if tt == NT - 1 else 4
                nd.after_pe(tt, "sums")
                nd.done(act.activation(ebl[0:DK, 0:HC * nch], psum[0:DK, 7, 0:HC * nch], ACT.Exp), tt, "ebl")
                nd.done(act.activation(eb[0:n, :], psum[0:n, 5, 0:CK], ACT.Exp), tt, "eb")
                nd.done(act.activation(enb[0:n, :], psum[0:n, 5, 0:CK], ACT.Exp, scale=-1.0), tt, "enb")
                nd.done(act.activation(ebd[0:n, :], psum[0:n, 6, 0:CK], ACT.Exp), tt, "ebd")

            def rms(tt):
                n = TILES[tt][1]
                nd.after_dve(tt, "oc", 1)
                for h in range(HC):
                    nd.done(act.activation(gjunk[0:n, DV * h:DV * h + DV], oc[0:n, DV * h:DV * h + DV], ACT.Square,
                                           accum_out=rs[0:n, h:h + 1]), tt, "sq", h)
                act.wait_ge(ga_, GA[tt, "sq", HC - 1])
                nd.done(act.activation(rs[0:n, :], rs[0:n, :], ACT.Sqrt, bias=eps_c[0:n], scale=1.0 / DV), tt, "rms")

            def high(tt):
                a, n = TILES[tt]
                nd.after_dve(tt, "out", 5)
                nd.done(act.activation(hi[:, MIX_C:KT, a:a + n], out6[:, :, 0:n], ACT.Copy), tt, "hi")

            decays(0)
            for tt, (a, n) in enumerate(TILES):
                nd.after_pe(tt, "turn")
                v = lambda ap: ap.rearrange("p (h t) -> p h t", h=HC)[:, :, 0:n]
                nd.done(act.activation(qeT[0:DK, :, 0:n], v(psum[0:DK, 0, :]), ACT.Copy), tt, "qeT")
                nd.done(act.activation(keT[0:DK, :, 0:n], v(psum[0:DK, 5, :]), ACT.Copy), tt, "keT")
                nd.after_pe(tt, "v")
                nd.done(act.activation(vt[0:n, 0:512], psum[0:n, 3, :], ACT.Copy), tt, "v0")
                nd.done(act.activation(vt[0:n, 512:CV], psum[0:n, 4, 0:256], ACT.Copy), tt, "v1")
                if tt:
                    rms(tt - 1)
                act.wait_ge(rc_in[tt % 2], 16 * (tt // 2) + 16)
                nd.done(act.activation(rcf[tt % 2][:, :, 0:n], rcf[tt % 2][:, :, 0:n], ACT.Silu), tt, "silu")
                if tt + 1 < NT:
                    decays(tt + 1)
                if tt:
                    high(tt - 1)
            rms(NT - 1)
            high(NT - 1)

        def gla_dve(dve, nd):
            dve.wait_ge(pa_o, NU)
            dve.wait_ge(pa_lo, NU)
            for tt, (a, n) in enumerate(TILES):
                nd.after_pe(tt, "z")
                nd.done(dve.tensor_copy(gg[0:n, tt, :], psum[0:n, tt % 4, 0:CK]), tt, "zs")
                nd.after_dve(tt, "zs")
                nd.done(dve.scalar_tensor_tensor(out=az[0:n, tt, :], in0=gg[0:n, tt, :], scalar=-1.0, in1=gg[0:n, tt, :], op0=ALU.mult, op1=ALU.max), tt, "az")
            for tt, (a, n) in enumerate(TILES):
                nd.after_act(tt, "l")
                nd.done(dve.scalar_tensor_tensor(out=gg[0:n, tt, :], in0=gg[0:n, tt, :], scalar=0.0, in1=az[0:n, tt, :], op0=ALU.min, op1=ALU.subtract), tt, "g")
            dve.wait_ge(pl_mm, NPOOL)
            dve.wait_ge(pl_lo, NPOOL)
            dve.wait_ge(pl_out, 48)
            dve.wait_ge(wlo_done, 4 * G_IN + 4)
            dve.memset(am, 0.0).then_inc(gl_z0, 1)
            dve.memset(am_s, 0.0).then_inc(gl_z0, 1)
            dve.memset(S[:, 0, :], 0.0).then_inc(gl_z0, 1)
            dve.wait_ge(gl_z0, 3)

            def decayed(tt):
                n = TILES[tt][1]
                nd.after_act(tt, "ebd")
                nd.after_pe(tt, "qk")
                nd.done(dve.scalar_tensor_tensor(out=qe[0:n, :], in0=psum[0:n, 0, 0:CK], scalar=SCALE_C, in1=eb[0:n, :], op0=ALU.mult, op1=ALU.mult), tt, "qe")
                nd.done(dve.tensor_tensor(ke[0:n, :], psum[0:n, 7, P:P + CK], enb[0:n, :], ALU.mult), tt, "ke")
                nd.done(dve.tensor_tensor(kd[0:n, :], psum[0:n, 7, P:P + CK], ebd[0:n, :], ALU.mult), tt, "kd")

            def normed(tt):
                n = TILES[tt][1]
                nd.after_act(tt, "rms")
                nd.done(dve.reciprocal(rs[0:n, :], rs[0:n, :]), tt, "rs")
                nd.after_dve(tt, "rs")
                o4 = oc[0:n, :].rearrange("p (h v) -> p h v", h=HC)
                nd.done(dve.tensor_tensor(o4, o4, rs[0:n, :].unsqueeze(2).to_broadcast([n, HC, DV]), ALU.mult), tt, "on")

            def gated(tt):
                n = TILES[tt][1]
                nd.after_pe(tt, "oT")
                nd.after_act(tt, "silu")
                for m in range(6):
                    nd.done(dve.scalar_tensor_tensor(out=out6[:, m, 0:n], in0=psum[:, 1 + m // 4, P * (m % 4):P * (m % 4) + n], scalar=GN[:, m:m + 1],
                                                     in1=rcf[tt % 2][:, m, 0:n], op0=ALU.mult, op1=ALU.mult), tt, "out", m)

            def low_part(tt):
                a, n = TILES[tt]
                nd.after_act(tt, "hi")
                nd.done(dve.tensor_tensor(lo[:, MIX_C:KT, a:a + n], out6[:, :, 0:n], hi[:, MIX_C:KT, a:a + n].bitcast(F32), ALU.subtract), tt, "lo")

            decayed(0)
            for tt, (a, n) in enumerate(TILES):
                smp = tt == NT - 1
                if smp:
                    dve.memset(qd[0:DK], 0.0).then_inc(gl_z0, 1)
                nd.after_pe(tt, "scores")
                m = C("upto" + sfx(tt), n).bitcast(I32)
                nd.done(dve.copy_predicated((am_s if smp else am)[0:n, :, 0:n], m.unsqueeze(1).to_broadcast([n, HC, n]),
                                            psum[0:n, 6, :].rearrange("p (h t) -> p h t", h=HC)[:, :, 0:n]), tt, "mask")
                if smp:
                    dve.wait_ge(gl_z0, 4)
                    nd.done(dve.tensor_copy(qd[0:DK].rearrange("p h (b s) -> p h b s", b=TB)[:, :, :, 0:TT],
                                            qeT[0:DK, :, 0:n].rearrange("p h (b t) -> p h b t", b=TB)), tt, "qd")
                for c in range(TB if smp else 4):
                    if smp:
                        for b in ([0, 1] if c == 0 else [c + 1] if c + 1 < TB else []):
                            nd.done(dve.tensor_scalar(kdm[0:n, b % 2, :], kd[0:n, :], C("chunk_s", n)[:, b:b + 1], GATE_NORM, ALU.mult, ALU.mult), tt, "kdm", b)
                        if c < 3:
                            (normed, gated, low_part)[c](tt - 1)
                        src, dst = s0[c % 4], sn[:, c % 2, :]
                        dve.wait_ge(s0_in[c % 4], 16 * (c // 4) + 16)
                        if c >= 2:
                            dve.wait_ge(sn_out[c % 2], 16 * (c // 2))
                        nch = TB
                    else:
                        src, dst = S[:, (4 * tt + c) % 5, :], S[:, (4 * tt + c + 1) % 5, :]
                        if c:
                            nd.after_dve(tt, "S", c - 1, HC - 1)
                        nch = 4
                    nd.after_pe(tt, "state", c)
                    for h in range(HC):
                        x = slice(DV * h, DV * h + DV)
                        nd.done(dve.scalar_tensor_tensor(out=dst[0:DK, x], in0=src[0:DK, x], scalar=ebl[0:DK, nch * h + c:nch * h + c + 1],
                                                         in1=psum[0:DK, ubanks[c % 2][h // 2], DV * (h % 2):DV * (h % 2) + DV],
                                                         op0=ALU.mult, op1=ALU.add), tt, "S", c, h)
                    if tt and not smp and c == 1:
                        normed(tt - 1)
                if not smp:
                    if tt:
                        gated(tt - 1)
                    decayed(tt + 1)
                nd.after_pe(tt, *(("inter", TB - 1) if smp else ("out",)))
                for i in range(2):
                    nd.done(dve.tensor_copy(oc[0:n, 2 * DV * i:2 * DV * (i + 1)], psum[0:n, 3 + i, 0:2 * DV]), tt, "oc", i)
                if tt and not smp:
                    low_part(tt - 1)
            normed(NT - 1)
            gated(NT - 1)
            low_part(NT - 1)
            dve.wait_ge(gv, GV[NT - 1, "lo"])
            dve.sem_inc(s_mix, 1)

        @block.sync
        def _(sp):
            sp_start(sp)
            with sp.Fori(1, G_ROW) as g:
                load_group(sp, g, cols(win_v, g))
            dec_sp(sp)
            with sp.Fori(0, TB - 1) as b:
                dec_sp_b(sp, b)
            dec_sp_b(sp, TB - 1, last=True)
            dtail_sp(sp, 0)
            kv_sp(sp)
            dtail_sp(sp, 1)
            pa_sp(sp)
            gla_sp_early(sp)
            pool_sp(sp)
            gla_sp(sp)
            sp.wait_ge(s_mix, 1)
            for i in range(2):
                sp.wait_ge(sn_out[i], 64)
            sp.wait_ge(pg_out, 16)
            sp.wait_ge(xt_out, 16)
            sp.dma_start(xT.rearrange("p k t -> p (k t)"), xT_d).then_inc(xt_in, 16)
            with sp.Fori(1, G_O) as g:
                load_group(sp, G_IN + g, cols(wo_v, g))
            sp_ffn(sp)
            final_sp(sp)
            sp.wait_ge(kv_st[0], 32 * 3)
            sp.wait_ge(kv_st[1], 32 * 2)

        @block.gpsimd
        def _(pool):
            norm_pool(pool, 0)
            in_pool(pool)
            pool.wait_ge(wlo_done, 4 * (G_ROW + 1))
            with pool.Fori(0, TB) as b:
                dec_pool_b(pool, b)
            in_store(pool, G_LAST)
            pool_gp(pool)
            norm_pool(pool, 1)

        @block.scalar
        def _(act):
            act.wait_ge(s_ready, 3)
            copies_in(act, xt_act, 0)
            act.wait_ge(xsq_done, NTT)
            token_rms(act, rtok)
            in_act(act)
            norm_act(act, 0)
            in_act_loop(act)
            with act.Fori(0, TB) as b:
                dec_act_b(act, b)
            kv_stage_act(act)
            dtail_act(act)
            pool_act_turned(act)
            pa_act(act)
            ga_act(act)
            pool_act(act)
            gla_act(act, Named(act, ga_, GA))
            o_act(act)
            act.wait_ge(ss_done, 1)
            token_rms(act, psum[:, 0, 0:NTT])
            norm_act(act, 1)
            ffn_act(act)
            final_add_squares(act)
            final_act(act)

        @block.vector
        def _(dve):
            dve.memset(ones[:, :], 1.0).then_inc(s_ready, 1)
            dve.memset(misc[:, :], EPS).then_inc(s_ready, 1)
            dve.memset(gaT[:, :], 1.0).then_inc(s_ready, 1)
            for s_ in (o_ready, sl_done, ob_done):
                dve.sem_inc(s_, 1)
            for s_ in (sq_done, acc_done):
                dve.sem_inc(s_, KT)
            dve.sem_inc(ob_out, 16)
            for s_ in (in_ev, o_added):
                dve.sem_inc(s_, 2)
            copies_in(dve, xt_dve, 1)
            dve.wait_ge(s_vt, 1)
            dve.tensor_copy(vecs[:, 0:42], psum[:, 4, 0:42]).then_inc(s_vc, 1)
            dve.wait_ge(s_vc, 1)
            dve.wait_ge(s_ready, 3)
            dve.wait_ge(xt_act, 10)
            dve.wait_ge(xt_dve, 10)
            norm_dve(dve, 0, G1)
            in_dve(dve)
            dve.wait_ge(xt_out, 16)
            in_dve_loop(dve)
            dve.memset(s_max_w, 0.0).then_inc(dec_z, 1)
            dve.wait_ge(dec_z, 1)
            with dve.Fori(0, TB) as b:
                dec_dve_b(dve, b, DVE_B * b)
            kv_stage_dve(dve)
            dtail_dve(dve)
            pa_dve(dve)
            gla_dve(dve, Named(dve, gv, GV))
            o_dve(dve)
            norm_dve(dve, 1, G2)
            ffn_dve(dve)
            final_dve(dve)

        @block.tensor
        def _(pe):
            transposes_in(pe)
            pe.wait_ge(s_ready, 3)
            pe.wait_ge(xt_act, 10)
            pe.wait_ge(xt_dve, 10)
            norm_pe(pe, 0)
            pe.wait_ge(s_vc, 1)
            in_pe(pe)
            with pe.Fori(0, TB) as b:
                dec_pe_b(pe, b)
            kv_stage_pe(pe)
            pe.wait_ge(s_gs, 2)
            pe.wait_ge(in_ev, 2 + G_IN)
            for k in range(HA):
                ga_pe(pe, k)
            dtail_pe(pe)
            pool_pe_turn(pe)
            pa_pe(pe)
            gla_steps = Named(pe, gp, GP)
            gla_pe_gates(pe, gla_steps)
            pool_pe(pe)
            gla_pe(pe, gla_steps)
            o_pe(pe)
            pe.wait_ge(acc_done, 2 * KT)
            token_sums(pe, 0)
            norm_pe(pe, 1)
            ffn_pe(pe)
            final_pe(pe)


_INS = ['x_prompt', 'x_sample', 'cache_win_k', 'cache_win_v', 'state_pool', 'state_gla', 'norm1_g', 'w_in', 'w_gate2', 'b_gate',
        'w_pool', 'pool_scale', 'gla_norm_g', 'w_o', 'norm2_g', 'w_ffn_gate', 'w_ffn_up', 'w_ffn_down', 'final_norm_g']
_OUTS = [(1, TP, D), (TB, TT, D), (1, 1, TP, HA, HD), (1, 1, TP, HA, HD), (1, 1, PBUF, DB), (1, 1, HC, DK, DV),
         (1, TB, TT, HA, HD), (1, TB, TT, HA, HD), (1, TB, PBUF, DB), (1, TB, HC, DK, DV)]


def kernel(**inputs):
    import numpy as _np
    import concourse.bacc as _bacc
    from concourse.bass_utils import run_bass_kernel_spmd as _run

    nc = _bacc.Bacc("TRN2", target_bir_lowering=False, num_devices=1)
    arrays, args = {}, []
    data = {name: _np.ascontiguousarray(inputs[name]) for name in _INS}
    data["table"] = table_columns()
    for name, a in data.items():
        arrays[f"in_{name}"] = a
        args.append(nc.dram_tensor(f"in_{name}", a.shape, mybir.dt.from_np(a.dtype), kind="ExternalInput").ap())
    for i, shape in enumerate(_OUTS):
        args.append(nc.dram_tensor(f"out_{i}", shape, F32, kind="ExternalOutput").ap())
    build(nc, *args)
    r = _run(nc, [arrays], core_ids=[0])
    return tuple(r.results[0][f"out_{i}"] for i in range(len(_OUTS)))
```
